# Optimizing a Trainium2 kernel written in Bass

```python
import jax, jax.numpy as jnp
from jax import lax
import numpy as np
import math

D_MODEL = 1024
BATCH = 1
SEQ = 256
DEPTH = 1

CHUNK = 64
Q_BLOCK = 128
SB_HEADS = 8
SB_HEAD_DIM = D_MODEL // SB_HEADS
SB_WIDTH = SB_HEADS * SB_HEAD_DIM
RET_HEADS = 4
RET_KEY_DIM = D_MODEL // RET_HEADS
RET_VAL_DIM = D_MODEL // RET_HEADS
RET_QK_WIDTH = RET_HEADS * RET_KEY_DIM
RET_WIDTH = RET_HEADS * RET_VAL_DIM
ROPE_BASE = 10000.0
EPS = 1e-6
SPLIT_SIZES = (SB_WIDTH, SB_WIDTH, SB_WIDTH, SB_WIDTH,
               RET_QK_WIDTH, RET_QK_WIDTH, RET_WIDTH, RET_WIDTH,
               D_MODEL, D_MODEL)
IN_COLS = sum(SPLIT_SIZES)
SPLIT_POINTS = tuple(int(v) for v in np.cumsum(SPLIT_SIZES)[:-1])


def rms_norm(x, gain):
    xf = x.astype(jnp.float32)
    y = xf * lax.rsqrt(jnp.mean(xf * xf, axis=-1, keepdims=True) + EPS)
    return (y * gain.astype(jnp.float32)).astype(x.dtype)

def split_heads(t, n_heads):
    b, s, w = t.shape
    return t.reshape(b, s, n_heads, w // n_heads).transpose(0, 2, 1, 3)

def merge_heads(t):
    b, h, s, d = t.shape
    return t.transpose(0, 2, 1, 3).reshape(b, s, h * d)

def rotary(t):
    s, d = t.shape[2], t.shape[3]
    inv_freq = ROPE_BASE ** (-jnp.arange(0, d, 2, dtype=jnp.float32) / d)
    ang = jnp.arange(s, dtype=jnp.float32)[:, None] * inv_freq[None, :]
    cos, sin = jnp.cos(ang), jnp.sin(ang)
    tf = t.astype(jnp.float32)
    t1, t2 = tf[..., : d // 2], tf[..., d // 2:]
    out = jnp.concatenate([t1 * cos - t2 * sin, t1 * sin + t2 * cos], axis=-1)
    return out.astype(t.dtype)

def stick_breaking_attention(q, k, v):
    b, h, s, d = q.shape
    nb = s // Q_BLOCK
    qb = q.reshape(b, h, nb, Q_BLOCK, d).transpose(2, 0, 1, 3, 4)
    kpos = jnp.arange(s)
    scale = d ** -0.5

    def block(args):
        qi, i = args
        z = jnp.einsum('bhqd,bhkd->bhqk', qi, k).astype(jnp.float32) * scale
        qpos = i * Q_BLOCK + jnp.arange(Q_BLOCK)
        mask = kpos[None, :] < qpos[:, None]
        log_keep = jnp.where(mask, jax.nn.log_sigmoid(-z), 0.0)
        suffix = lax.cumsum(log_keep, axis=3, reverse=True) - log_keep
        w = jnp.where(mask, jnp.exp(jax.nn.log_sigmoid(z) + suffix), 0.0)
        return jnp.einsum('bhqk,bhkd->bhqd', w.astype(v.dtype), v)

    out = lax.map(block, (qb, jnp.arange(nb)))
    return out.transpose(1, 2, 0, 3, 4).reshape(b, h, s, d)

def chunkwise_retention(q, k, v):
    dtype = v.dtype
    q, k, v = (a.astype(jnp.float32) for a in (q, k, v))
    b, h, s, dk = q.shape
    dv = v.shape[-1]
    n = s // CHUNK
    log_gamma = jnp.log1p(-jnp.exp2(-5.0 - jnp.arange(h, dtype=jnp.float32)))
    qc = q.reshape(b, h, n, CHUNK, dk)
    kc = k.reshape(b, h, n, CHUNK, dk)
    vc = v.reshape(b, h, n, CHUNK, dv)
    idx = jnp.arange(CHUNK, dtype=jnp.float32)
    intra_decay = jnp.exp(log_gamma[:, None, None] * jnp.abs(idx[:, None] - idx[None, :]))
    scores = jnp.einsum('bhnqd,bhnkd->bhnqk', qc, kc) * intra_decay[None, :, None]
    intra = jnp.einsum('bhnqk,bhnke->bhnqe', scores, vc)
    q_decay = jnp.exp(log_gamma[:, None] * (idx + 1.0))[None, :, :, None]
    k_decay = jnp.exp(log_gamma[:, None] * (CHUNK - 1.0 - idx))[None, :, :, None]
    chunk_decay = jnp.exp(log_gamma * CHUNK)[None, :, None, None]

    def step(state, inp):
        qi, ki, vi = inp
        out = jnp.einsum('bhqd,bhde->bhqe', qi * q_decay, state)
        state = state * chunk_decay + jnp.einsum('bhkd,bhke->bhde', ki * k_decay, vi)
        return state, out

    init = jnp.zeros((b, h, dk, dv), jnp.float32)
    xs = (qc.transpose(2, 0, 1, 3, 4), kc.transpose(2, 0, 1, 3, 4), vc.transpose(2, 0, 1, 3, 4))
    _, inter = lax.scan(step, init, xs)
    out = intra + inter.transpose(1, 2, 0, 3, 4)
    return out.reshape(b, h, s, dv).astype(dtype)

def first_inputs(seed: int = 0) -> dict:
    key = jax.random.key(seed)
    ks = jax.random.split(key, 10)
    f32 = jnp.float32
    x = jax.random.normal(ks[0], (BATCH, SEQ, D_MODEL), f32)
    norm_gain = 1.0 + 0.05 * jax.random.normal(ks[1], (DEPTH, D_MODEL), f32)
    w_in = jax.random.normal(ks[2], (DEPTH, D_MODEL, IN_COLS), f32) * D_MODEL ** -0.5
    b_merge = 0.01 * jax.random.normal(ks[3], (DEPTH, 2, D_MODEL), f32)
    sb_q_gain = 1.0 + 0.05 * jax.random.normal(ks[4], (DEPTH, SB_HEAD_DIM), f32)
    sb_k_gain = 1.0 + 0.05 * jax.random.normal(ks[5], (DEPTH, SB_HEAD_DIM), f32)
    ret_out_gain = 1.0 + 0.05 * jax.random.normal(ks[6], (DEPTH, RET_HEADS, RET_VAL_DIM), f32)
    w_branch_sb = jax.random.normal(ks[7], (DEPTH, SB_WIDTH, D_MODEL), f32) * SB_WIDTH ** -0.5
    w_branch_ret = jax.random.normal(ks[8], (DEPTH, RET_WIDTH, D_MODEL), f32) * RET_WIDTH ** -0.5
    w_out = jax.random.normal(ks[9], (DEPTH, D_MODEL, D_MODEL), f32) * D_MODEL ** -0.5
    return {"x": x, "norm_gain": norm_gain, "w_in": w_in, "b_merge": b_merge,
            "sb_q_gain": sb_q_gain, "sb_k_gain": sb_k_gain, "ret_out_gain": ret_out_gain,
            "w_branch_sb": w_branch_sb, "w_branch_ret": w_branch_ret, "w_out": w_out}

def first_block(x, norm_gain, w_in, b_merge, sb_q_gain, sb_k_gain, ret_out_gain,
              w_branch_sb, w_branch_ret, w_out):
    for layer in range(DEPTH):
        h = rms_norm(x, norm_gain[layer])
        proj = jnp.einsum('bsd,dc->bsc', h, w_in[layer])
        (sb_q, sb_k, sb_v, sb_g, r_q, r_k, r_v, r_g, m_sb, m_ret) = jnp.split(proj, SPLIT_POINTS, axis=-1)

        qa = rms_norm(split_heads(sb_q, SB_HEADS), sb_q_gain[layer])
        ka = rms_norm(split_heads(sb_k, SB_HEADS), sb_k_gain[layer])
        va = split_heads(sb_v, SB_HEADS)
        out_a = merge_heads(stick_breaking_attention(qa, ka, va)) * jax.nn.silu(sb_g)

        qb = rotary(split_heads(r_q, RET_HEADS))
        kb = rotary(split_heads(r_k, RET_HEADS)) * (RET_KEY_DIM ** -0.5)
        vb = split_heads(r_v, RET_HEADS)
        ret = chunkwise_retention(qb, kb, vb)
        ret = rms_norm(ret, ret_out_gain[layer][None, :, None, :])
        out_b = merge_heads(ret) * jax.nn.silu(r_g)

        p_a = jnp.einsum('bsw,wd->bsd', out_a, w_branch_sb[layer])
        p_b = jnp.einsum('bsw,wd->bsd', out_b, w_branch_ret[layer])
        merged = (jax.nn.sigmoid(m_sb + b_merge[layer, 0]) * p_a
                  + jax.nn.sigmoid(m_ret + b_merge[layer, 1]) * p_b)
        x = x + jnp.einsum('bsd,de->bse', merged, w_out[layer])
    return x


MLA_HEADS = 8
QK_NOPE = 64
QK_ROPE = 32
QK_HEAD = QK_NOPE + QK_ROPE
V_HEAD = 64
Q_LORA = 256
KV_LORA = 128
ROPE_THETA = 10000.0
RWKV_HEADS = 8
RWKV_HEAD = 64
RWKV_DIM = RWKV_HEADS * RWKV_HEAD
DECAY_LORA = 64
AAA_LORA = 64
GATE_LORA = 128
GN_EPS = 64e-5
PEER_HEADS = 8
N_KEYS = 128
N_EXPERTS = N_KEYS * N_KEYS
D_KEY = 256
HALF_KEY = D_KEY // 2
TOPK_HALF = 16
TOPK = 16
PEER_BLOCK = 64
N_BRANCH = 2
MLA_IN = Q_LORA + KV_LORA + QK_ROPE
RWKV_IN = 3 * RWKV_DIM + DECAY_LORA + AAA_LORA + GATE_LORA
GATE_IN = N_BRANCH * D_MODEL
IN_DIM = MLA_IN + RWKV_IN + GATE_IN
N_MOD = 6


def rms_norm_2(x, g, eps=EPS):
    xf = x.astype(jnp.float32)
    y = xf * lax.rsqrt(jnp.mean(xf * xf, axis=-1, keepdims=True) + eps)
    return (y * g.astype(jnp.float32)).astype(x.dtype)

def modulate(h, shift, scale):
    return h * (1.0 + scale[:, None, :]) + shift[:, None, :]

def rope(x, positions):
    half = x.shape[-1] // 2
    inv_freq = ROPE_THETA ** (-jnp.arange(half, dtype=jnp.float32) / half)
    ang = positions.astype(jnp.float32)[..., None] * inv_freq
    cos = jnp.cos(ang)[:, :, None, :]
    sin = jnp.sin(ang)[:, :, None, :]
    xf = x.astype(jnp.float32)
    x1, x2 = xf[..., :half], xf[..., half:]
    return jnp.concatenate([x1 * cos - x2 * sin, x1 * sin + x2 * cos], axis=-1).astype(x.dtype)

def causal_block_attention(q, k, v):
    B, S, H, Dq = q.shape
    nb = S // Q_BLOCK
    scale = Dq ** -0.5
    qb = q.reshape(B, nb, Q_BLOCK, H, Dq).transpose(1, 0, 2, 3, 4)
    kpos = jnp.arange(S)

    def one_block(args):
        i, q_blk = args
        s = jnp.einsum('bqhd,bkhd->bhqk', q_blk, k).astype(jnp.float32) * scale
        qpos = i * Q_BLOCK + jnp.arange(Q_BLOCK)
        mask = kpos[None, :] <= qpos[:, None]
        s = jnp.where(mask[None, None], s, -jnp.inf)
        p = jax.nn.softmax(s, axis=-1).astype(v.dtype)
        return jnp.einsum('bhqk,bkhd->bqhd', p, v)

    out = lax.map(one_block, (jnp.arange(nb), qb))
    return out.transpose(1, 0, 2, 3, 4).reshape(B, S, H, v.shape[-1])

def mla_branch(q_a, kv_a, k_rope_raw, positions, q_a_norm, w_uq, kv_a_norm, w_ukv, q_norm, k_norm, w_o_mla):
    B, S, _ = q_a.shape
    cq = rms_norm_2(q_a, q_a_norm)
    q = (cq @ w_uq).reshape(B, S, MLA_HEADS, QK_HEAD)
    ckv = rms_norm_2(kv_a, kv_a_norm)
    kv = (ckv @ w_ukv).reshape(B, S, MLA_HEADS, QK_NOPE + V_HEAD)
    k_nope, v = kv[..., :QK_NOPE], kv[..., QK_NOPE:]
    q_nope = rms_norm_2(q[..., :QK_NOPE], q_norm[:QK_NOPE])
    q_pe = rope(rms_norm_2(q[..., QK_NOPE:], q_norm[QK_NOPE:]), positions)
    k_nope = rms_norm_2(k_nope, k_norm[:QK_NOPE])
    k_pe = rope(rms_norm_2(k_rope_raw[:, :, None, :], k_norm[QK_NOPE:]), positions)
    k_pe = jnp.broadcast_to(k_pe, (B, S, MLA_HEADS, QK_ROPE))
    qh = jnp.concatenate([q_nope, q_pe], axis=-1)
    kh = jnp.concatenate([k_nope, k_pe], axis=-1)
    o = causal_block_attention(qh, kh, v)
    return o.reshape(B, S, MLA_HEADS * V_HEAD) @ w_o_mla

def token_shift(p, mu):
    prev = jnp.pad(p, ((0, 0), (1, 0), (0, 0)))[:, :-1]
    return p + (prev - p) * mu

def rwkv7_scan(r, decay, k, v, kk, a):
    B, S, H, N = r.shape
    b = kk * a

    def step(state, inp):
        r_t, w_t, k_t, v_t, kk_t, b_t = inp
        sa = jnp.einsum('bhvk,bhk->bhv', state, -kk_t)
        state = (state * w_t[:, :, None, :] + sa[..., None] * b_t[:, :, None, :]
                 + v_t[..., None] * k_t[:, :, None, :])
        y = jnp.einsum('bhvk,bhk->bhv', state, r_t)
        return state, y

    xs = tuple(t.transpose(1, 0, 2, 3) for t in (r, decay, k, v, kk, b))
    s0 = jnp.zeros((B, H, N, N), jnp.float32)
    _, y = lax.scan(step, s0, xs)
    return y.transpose(1, 0, 2, 3)

def rwkv7_branch(p, mu_shift, w_decay_up, decay_base, w_aaa_up, aaa_base, w_gate_up,
                 k_k, k_a, r_k, ln_x_w, ln_x_b, w_o_rwkv):
    B, S, _ = p.shape
    p = token_shift(p, mu_shift)
    splits = [RWKV_DIM, 2 * RWKV_DIM, 3 * RWKV_DIM, 3 * RWKV_DIM + DECAY_LORA,
              3 * RWKV_DIM + DECAY_LORA + AAA_LORA]
    r, k, v, wd, ad, gd = jnp.split(p, splits, axis=-1)
    w = -jax.nn.softplus(-(decay_base + jnp.tanh(wd) @ w_decay_up)) - 0.5
    decay = jnp.exp(-jnp.exp(w.astype(jnp.float32)))
    a = jax.nn.sigmoid(aaa_base + ad @ w_aaa_up)
    g = jax.nn.sigmoid(gd) @ w_gate_up

    def heads(t):
        return t.reshape(B, S, RWKV_HEADS, RWKV_HEAD).astype(jnp.float32)

    kk = heads(k * k_k)
    kk = kk / jnp.maximum(jnp.linalg.norm(kk, axis=-1, keepdims=True), 1e-12)
    a_h = heads(a)
    k_h = heads(k) * (1.0 + (a_h - 1.0) * k_a.reshape(RWKV_HEADS, RWKV_HEAD).astype(jnp.float32))
    r_h, v_h = heads(r), heads(v)
    y = rwkv7_scan(r_h, heads(decay), k_h, v_h, kk, a_h)
    mu = jnp.mean(y, axis=-1, keepdims=True)
    var = jnp.mean(jnp.square(y - mu), axis=-1, keepdims=True)
    y = (y - mu) * lax.rsqrt(var + GN_EPS)
    y = y * ln_x_w.reshape(RWKV_HEADS, RWKV_HEAD) + ln_x_b.reshape(RWKV_HEADS, RWKV_HEAD)
    y = y + jnp.sum(r_h * k_h * r_k, axis=-1, keepdims=True) * v_h
    y = y.reshape(B, S, RWKV_DIM).astype(p.dtype) * g
    return y @ w_o_rwkv

def token_mixer(h, positions, w_in, mu_shift, q_a_norm, w_uq, kv_a_norm, w_ukv, q_norm, k_norm, w_o_mla,
                w_decay_up, decay_base, w_aaa_up, aaa_base, w_gate_up, k_k, k_a, r_k, ln_x_w, ln_x_b,
                w_o_rwkv, w_out):
    proj = h @ w_in
    q_a, kv_a, k_rope_raw, rwkv_in, gate_logits = jnp.split(
        proj, [Q_LORA, Q_LORA + KV_LORA, MLA_IN, MLA_IN + RWKV_IN], axis=-1)
    o_mla = mla_branch(q_a, kv_a, k_rope_raw, positions, q_a_norm, w_uq, kv_a_norm, w_ukv,
                       q_norm, k_norm, w_o_mla)
    o_rwkv = rwkv7_branch(rwkv_in, mu_shift, w_decay_up, decay_base, w_aaa_up, aaa_base, w_gate_up,
                          k_k, k_a, r_k, ln_x_w, ln_x_b, w_o_rwkv)
    g_mla, g_rwkv = jnp.split(jax.nn.sigmoid(gate_logits), 2, axis=-1)
    return (g_mla * o_mla + g_rwkv * o_rwkv) @ w_out

def peer_ffn(h, w_query, sub_keys1, sub_keys2, expert_down, expert_up):
    B, S, D = h.shape
    q = (h @ w_query).reshape(B, S, PEER_HEADS, 2, HALF_KEY)
    s1 = jnp.einsum('bshd,nd->bshn', q[..., 0, :], sub_keys1).astype(jnp.float32)
    s2 = jnp.einsum('bshd,nd->bshn', q[..., 1, :], sub_keys2).astype(jnp.float32)
    v1, i1 = lax.top_k(s1, TOPK_HALF)
    v2, i2 = lax.top_k(s2, TOPK_HALF)
    cand = (v1[..., :, None] + v2[..., None, :]).reshape(B, S, PEER_HEADS, TOPK_HALF * TOPK_HALF)
    cand_idx = (i1[..., :, None] * N_KEYS + i2[..., None, :]).reshape(B, S, PEER_HEADS, TOPK_HALF * TOPK_HALF)
    top_v, pos = lax.top_k(cand, TOPK)
    expert_idx = jnp.take_along_axis(cand_idx, pos, axis=-1)
    gates = jax.nn.softmax(top_v, axis=-1).astype(h.dtype)
    nb = S // PEER_BLOCK
    hb = h.reshape(B, nb, PEER_BLOCK, D).transpose(1, 0, 2, 3)
    idxb = expert_idx.reshape(B, nb, PEER_BLOCK, PEER_HEADS, TOPK).transpose(1, 0, 2, 3, 4)
    gb = gates.reshape(B, nb, PEER_BLOCK, PEER_HEADS, TOPK).transpose(1, 0, 2, 3, 4)

    def one_block(args):
        h_blk, idx_blk, g_blk = args
        u = jnp.take(expert_down, idx_blk, axis=0)
        act = jax.nn.gelu(jnp.einsum('bpd,bphkd->bphk', h_blk, u))
        vv = jnp.take(expert_up, idx_blk, axis=0)
        return jnp.einsum('bphk,bphkd->bpd', g_blk * act, vv)

    out = lax.map(one_block, (hb, idxb, gb))
    return out.transpose(1, 0, 2, 3).reshape(B, S, D)

def second_inputs(seed: int = 0) -> dict:
    key = jax.random.key(seed)
    ks = jax.random.split(key, 40)
    f32 = jnp.float32

    def nrm(k, shape, scale):
        return jax.random.normal(k, (DEPTH,) + shape, f32) * scale

    def gain(k, shape):
        return 1.0 + 0.1 * jax.random.normal(k, (DEPTH,) + shape, f32)

    x = jax.random.normal(ks[0], (BATCH, SEQ, D_MODEL), f32)
    c = jax.random.normal(ks[1], (BATCH, D_MODEL), f32)
    offsets = jax.random.randint(ks[2], (BATCH, 1), 0, 1024, dtype=jnp.int32)
    positions = offsets + jnp.arange(SEQ, dtype=jnp.int32)[None, :]
    return {
        "x": x, "c": c, "positions": positions,
        "w_ada": nrm(ks[3], (D_MODEL, N_MOD * D_MODEL), 0.3 * D_MODEL ** -0.5),
        "b_ada": nrm(ks[4], (N_MOD * D_MODEL,), 0.05),
        "norm_mix": gain(ks[5], (D_MODEL,)),
        "w_in": nrm(ks[6], (D_MODEL, IN_DIM), D_MODEL ** -0.5),
        "mu_shift": jax.random.uniform(ks[7], (DEPTH, RWKV_IN), f32),
        "q_a_norm": gain(ks[8], (Q_LORA,)),
        "w_uq": nrm(ks[9], (Q_LORA, MLA_HEADS * QK_HEAD), Q_LORA ** -0.5),
        "kv_a_norm": gain(ks[10], (KV_LORA,)),
        "w_ukv": nrm(ks[11], (KV_LORA, MLA_HEADS * (QK_NOPE + V_HEAD)), KV_LORA ** -0.5),
        "q_norm": gain(ks[12], (QK_HEAD,)),
        "k_norm": gain(ks[13], (QK_HEAD,)),
        "w_o_mla": nrm(ks[14], (MLA_HEADS * V_HEAD, D_MODEL), (MLA_HEADS * V_HEAD) ** -0.5),
        "w_decay_up": nrm(ks[15], (DECAY_LORA, RWKV_DIM), 0.1),
        "decay_base": jax.random.uniform(ks[16], (DEPTH, RWKV_DIM), f32, -6.0, 2.0),
        "w_aaa_up": nrm(ks[17], (AAA_LORA, RWKV_DIM), 0.1),
        "aaa_base": nrm(ks[18], (RWKV_DIM,), 0.5),
        "w_gate_up": nrm(ks[19], (GATE_LORA, RWKV_DIM), GATE_LORA ** -0.5),
        "k_k": 0.85 + nrm(ks[20], (RWKV_DIM,), 0.1),
        "k_a": gain(ks[21], (RWKV_DIM,)),
        "r_k": nrm(ks[22], (RWKV_HEADS, RWKV_HEAD), 0.1),
        "ln_x_w": gain(ks[23], (RWKV_DIM,)),
        "ln_x_b": nrm(ks[24], (RWKV_DIM,), 0.02),
        "w_o_rwkv": nrm(ks[25], (RWKV_DIM, D_MODEL), RWKV_DIM ** -0.5),
        "w_out": nrm(ks[26], (D_MODEL, D_MODEL), D_MODEL ** -0.5),
        "norm_ffn": gain(ks[27], (D_MODEL,)),
        "w_query": nrm(ks[28], (D_MODEL, PEER_HEADS * D_KEY), D_MODEL ** -0.5),
        "sub_keys1": nrm(ks[29], (N_KEYS, HALF_KEY), HALF_KEY ** -0.5),
        "sub_keys2": nrm(ks[30], (N_KEYS, HALF_KEY), HALF_KEY ** -0.5),
        "expert_down": nrm(ks[31], (N_EXPERTS, D_MODEL), D_MODEL ** -0.5),
        "expert_up": nrm(ks[32], (N_EXPERTS, D_MODEL), PEER_HEADS ** -0.5),
    }

def second_block(x, c, positions, w_ada, b_ada, norm_mix, w_in, mu_shift, q_a_norm, w_uq, kv_a_norm, w_ukv,
              q_norm, k_norm, w_o_mla, w_decay_up, decay_base, w_aaa_up, aaa_base, w_gate_up, k_k, k_a, r_k,
              ln_x_w, ln_x_b, w_o_rwkv, w_out, norm_ffn, w_query, sub_keys1, sub_keys2, expert_down, expert_up):
    for l in range(DEPTH):
        mod = jax.nn.silu(c) @ w_ada[l] + b_ada[l]
        sh1, sc1, gt1, sh2, sc2, gt2 = jnp.split(mod, N_MOD, axis=-1)
        h = modulate(rms_norm_2(x, norm_mix[l]), sh1, sc1)
        mix = token_mixer(h, positions, w_in[l], mu_shift[l], q_a_norm[l], w_uq[l], kv_a_norm[l], w_ukv[l],
                          q_norm[l], k_norm[l], w_o_mla[l], w_decay_up[l], decay_base[l], w_aaa_up[l],
                          aaa_base[l], w_gate_up[l], k_k[l], k_a[l], r_k[l], ln_x_w[l], ln_x_b[l],
                          w_o_rwkv[l], w_out[l])
        x = x + gt1[:, None, :] * mix
        h = modulate(rms_norm_2(x, norm_ffn[l]), sh2, sc2)
        x = x + gt2[:, None, :] * peer_ffn(h, w_query[l], sub_keys1[l], sub_keys2[l], expert_down[l], expert_up[l])
    return x


def setup_inputs(seed=0):
    out = dict(first_inputs(seed))
    for name, value in second_inputs(seed + 1).items():
        if name != "x":
            out[name + "_2"] = value
    return out


def reference(
    x, norm_gain, w_in, b_merge, sb_q_gain, sb_k_gain, ret_out_gain, w_branch_sb, w_branch_ret,
    w_out, c_2, positions_2, w_ada_2, b_ada_2, norm_mix_2, w_in_2, mu_shift_2, q_a_norm_2,
    w_uq_2, kv_a_norm_2, w_ukv_2, q_norm_2, k_norm_2, w_o_mla_2, w_decay_up_2, decay_base_2,
    w_aaa_up_2, aaa_base_2, w_gate_up_2, k_k_2, k_a_2, r_k_2, ln_x_w_2, ln_x_b_2, w_o_rwkv_2,
    w_out_2, norm_ffn_2, w_query_2, sub_keys1_2, sub_keys2_2, expert_down_2, expert_up_2,
):
    x = first_block(
        x, norm_gain, w_in, b_merge, sb_q_gain, sb_k_gain, ret_out_gain, w_branch_sb,
        w_branch_ret, w_out,
    )
    return second_block(
        x, c_2, positions_2, w_ada_2, b_ada_2, norm_mix_2, w_in_2, mu_shift_2, q_a_norm_2,
        w_uq_2, kv_a_norm_2, w_ukv_2, q_norm_2, k_norm_2, w_o_mla_2, w_decay_up_2, decay_base_2,
        w_aaa_up_2, aaa_base_2, w_gate_up_2, k_k_2, k_a_2, r_k_2, ln_x_w_2, ln_x_b_2,
        w_o_rwkv_2, w_out_2, norm_ffn_2, w_query_2, sub_keys1_2, sub_keys2_2, expert_down_2,
        expert_up_2,
    )


_drawn_inputs = setup_inputs


def setup_inputs(seed=0):
    import zlib

    import numpy as np

    out = dict(_drawn_inputs(seed))
    spreads = {}
    factors = {'b_merge': 8.0,
     'sb_q_gain': 8.0,
     'sb_k_gain': 8.0,
     'ret_out_gain': 3.529,
     'norm_mix_2': 5.083,
     'q_a_norm_2': 64.0,
     'w_uq_2': 17.644,
     'kv_a_norm_2': 64.0,
     'q_norm_2': 64.0,
     'k_norm_2': 64.0,
     'w_decay_up_2': 64.0,
     'w_aaa_up_2': 3.545,
     'aaa_base_2': 5.002,
     'k_k_2': 64.0,
     'k_a_2': 7.525,
     'r_k_2': 4.091,
     'ln_x_w_2': 64.0,
     'ln_x_b_2': 200.0,
     'norm_ffn_2': 39.168,
     'w_ukv_2': 5.022,
     'w_o_mla_2': 4.987,
     'decay_base_2': 8.0,
     'w_query_2': 8.0,
     'sub_keys1_2': 8.0,
     'sub_keys2_2': 8.0,
     'expert_down_2': 8.0,
     'expert_up_2': 8.0}
    for name, (base, spread) in spreads.items():
        noise = np.random.default_rng([zlib.crc32(name.encode()), seed]).standard_normal(out[name].shape)
        drawn = base * np.exp(spread * noise) if base else spread * noise
        out[name] = __import__('jax').numpy.asarray(drawn.astype(out[name].dtype))
    for name, factor in factors.items():
        out[name] = (out[name] * factor).astype(out[name].dtype)
    return out
```

```python
from contextlib import ExitStack, contextmanager

import numpy as np

import concourse.bass as bass
from concourse import mybir
from concourse.alu_op_type import AluOpType as ALU

F32 = mybir.dt.float32
I32 = mybir.dt.int32
U32 = mybir.dt.uint32
F32R = mybir.dt.float32r
ACT = mybir.ActivationFunctionType
AX = mybir.AxisListType.X

P = 128
S = 256
TT = S // P
D = 1024
KT = D // P
CW = 512
EPS = 1e-6
SB_H, SB_D = 8, 128
RET_H, RET_D, CHUNK = 4, 256, 64
MLA_H, NOPE, ROPE, VH, QH = 8, 64, 32, 64, 96
Q_LORA, KV_LORA = 256, 128
RH, RN = 8, 64
RD = RH * RN
GN_EPS = 64e-5
N_KEYS, PEER_H, TOPK = 128, 8, 16
N_EXP = N_KEYS * N_KEYS
NEG = -1e30


class Mark:

    def __init__(self, sem, base, i=None, per=0):
        self.sem, self.base, self.i, self.per = sem, base, i, per

    def value(self):
        return self.base if self.i is None else self.i * self.per + self.base

    def last(self, n):
        return Mark(self.sem, self.base + (n - 1) * self.per)

    def before(self, k):
        assert self.base >= k * self.per
        return Mark(self.sem, self.base - k * self.per, self.i, self.per)


class Queue:

    name = "queue"

    def __init__(self, eng, sem):
        self.eng, self.sem, self.count = eng, sem, 0
        self.i, self.per, self.seen = None, 0, {}

    def after(self, *marks):
        for m in marks:
            if m.i is None:
                if self.seen.get(id(m.sem), 0) >= m.base:
                    continue
                if self.i is None:
                    self.seen[id(m.sem)] = m.base
            assert m.base > 0
            self.eng.wait_ge(m.sem, m.value())
        return self.eng

    def mark(self, instruction):
        instruction.then_inc(self.sem, 1)
        self.count += 1
        return self.now()

    def now(self):
        return Mark(self.sem, self.count, self.i, self.per)


class Count:

    name = "count"

    def __init__(self, sem, step=16):
        self.sem, self.step, self.count, self.i, self.per = sem, step, 0, None, 0

    def mark(self, instruction):
        instruction.then_inc(self.sem, self.step)
        self.count += self.step
        return self.now()

    def now(self, back=0):
        assert self.count >= back * self.step
        return Mark(self.sem, self.count - back * self.step, self.i, self.per)


@contextmanager
def engine_loop(nc, n, queues, per):
    with nc.Fori(0, n, 1, engines=tuple(q.eng.engine for q in queues)) as i:
        start = {}
        for c, k in per.items():
            start[c] = c.count
            c.i, c.per = i, k
        for q in queues:
            q.i = i
        yield i, {c: Mark(c.sem, start[c], i, per[c]) for c in per}
    for c, k in per.items():
        assert c.count - start[c] == k, (c.name, c.count - start[c], k)
        c.count = start[c] + n * k
    for c in list(per) + list(queues):
        c.i, c.per = None, 0


def constants():
    r = np.arange(P)
    s, t = r[:, None], r[None, :]
    lt = (s < t).astype(np.float32)
    c = {"ident": np.eye(P), "negtri": -(s >= t).astype(np.float32), "negones": -np.ones((P, P)),
         "lt": lt, "ltbias": np.concatenate([(1 - lt) * NEG, np.zeros((P, P)), (1 - lt) * NEG], 1)}
    tok = np.arange(S, dtype=np.float32)[:, None]
    inv = np.float32(10000.0) ** (-np.arange(0, RET_D, 2, dtype=np.float32) / np.float32(RET_D))
    ang = (tok * inv[None, :]).astype(np.float32).astype(np.float64).reshape(TT, P, RET_D // 2)
    c["cos"] = np.cos(ang).transpose(1, 0, 2).reshape(P, -1)
    c["sin"] = np.sin(ang).transpose(1, 0, 2).reshape(P, -1)
    full = np.arange(S)
    dec = []
    for h in range(RET_H):
        lg = np.log1p(-2.0 ** (-5.0 - h))
        m = np.exp(lg * np.abs(full[:, None] - full[None, :])) * RET_D ** -0.5
        m = m * ((full[:, None] // CHUNK) <= (full[None, :] // CHUNK))
        dec += [m[:P, :], m[P:, P:]]
    c["decay"] = np.concatenate(dec, 1)
    first = {k: np.asarray(v, np.float32) for k, v in c.items()}
    w = np.arange(RN)[None, :]
    sl = s % RN
    rate = -np.exp(-0.5)
    same = s // RN == t // RN
    c = {"upto": rate * ((s <= t) & same), "below": rate * ((s < t) & same),
         "ends": rate * np.stack([r // RN == 0, r // RN == 1], 1),
         "shift": (s == t - 1) * 1.0 - (s == t), "carry": (s == P - 1) & (t == 0),
         "strict": sl < w, "incl": sl <= w, "id64": sl == w, "a0": -1.0 * ((sl % 2 == 1) & (w == sl - 1)),
         "levels": np.concatenate([-1.0 * (((w // n) % 2 == 1) & (sl // n == w // n - 1))
                                   for n in (1, 2, 4, 8, 16, 32)], 1)}
    causal = np.where(t <= s, 0.0, NEG)
    c["causal"] = np.concatenate([causal, np.zeros((P, P)), causal], 1)
    c["iota"] = np.broadcast_to(t * 1.0, (P, P))
    inv = np.float32(10000.0) ** (-np.arange(ROPE // 2, dtype=np.float32) / np.float32(ROPE // 2))
    c["invf"] = np.broadcast_to(inv[None, :], (P, ROPE // 2))
    second = {k: np.asarray(v, np.float32) for k, v in c.items()}
    return first, second


def pack(tables):
    at, where = 0, {}
    for k, v in tables.items():
        where[k] = (at, v.shape[1])
        at += v.shape[1]
    return np.ascontiguousarray(np.concatenate(list(tables.values()), 1)), where


def build(nc, I, out):
    with ExitStack() as ctx:
        program(nc, ctx, I, out)


def program(nc, ctx, I, out):
    def sem(name):
        return ctx.enter_context(nc.semaphore(name))

    pe, dve = Queue(nc.tensor, sem("pe_done")), Queue(nc.vector, sem("dve_done"))
    act, pool = Queue(nc.scalar, sem("act_done")), Queue(nc.gpsimd, sem("pool_done"))
    sp = Queue(nc.sync, sem("sp_unused"))
    pe.name, dve.name, act.name, pool.name = "pe", "dve", "act", "pool"
    compute = (pe, dve, act)
    everyone = (pe, dve, act, pool)

    def arrivals(name, step=16):
        c = Count(sem(name), step)
        c.name = name
        return c

    slot_in = [arrivals("slot0_in"), arrivals("slot1_in")]
    block_done = arrivals("block_done", 1)
    taken = [arrivals("taken_dve", 1), arrivals("taken_act", 1)]
    start_in, first_in, merge_in = arrivals("start_in"), arrivals("first_in"), arrivals("merge_in")
    second_in, third_in = arrivals("second_in"), arrivals("third_in")
    ada_in = [arrivals("ada0_in"), arrivals("ada1_in")]
    mod_out = [arrivals("mod_out0"), arrivals("mod_out1")]
    mod_in = arrivals("mod_in")
    out_done = arrivals("out_done")
    peer_in, x_out, x_in = arrivals("peer_in"), arrivals("x_out"), arrivals("x_in")
    exp_in = [arrivals(f"expert{j}_in") for j in range(4)]
    turned_done, down_high, down_low, up_high, up_split, down_done, gelu_done, weighed_done, tile_done = (
        arrivals(n, 1) for n in ("turned_done", "down_high", "down_low", "up_high", "up_split", "down_done",
                                 "gelu_done", "weighed_done", "tile_done"))

    cursor = [(nc.sbuf_base + 63) // 64 * 64]

    def carve(name, *shape, dt=F32):
        n = int(np.prod(shape)) * 4
        t = nc.alloc_sbuf_tensor_at(name, [P, *shape], dt, offset=cursor[0])
        cursor[0] += (n + 31) // 32 * 32
        assert cursor[0] <= nc.sbuf_usable_end, (name, cursor[0])
        return t.ap()

    bank = [ctx.enter_context(nc.psum_tensor(f"bank{b}", [P, CW], F32)).ap() for b in range(8)]

    def fence():
        marks = [q.now() for q in everyone]
        for q in everyone:
            q.after(*marks)
        return marks

    ident = carve("ident", P)
    hT_at = cursor[0]
    hT = carve("hT", KT, S)
    slot_at = cursor[0]
    slot = [carve(f"slot{j}", KT * CW) for j in range(2)]
    stat = carve("stat", 192)
    col = carve("col", 3)
    cT, cs = carve("cT", KT), carve("cs", KT)
    gain1 = carve("gain1", KT)
    modT = carve("modT", 8, KT)
    lasting_top = cursor[0]
    X = carve("X", TT, D)
    gt = carve("gt", D)
    persistent_top = cursor[0]

    def load(dst, src, count, q=sp):
        return count.mark(q.eng.dma_start(dst, src, allow_slow_non_contiguous=True))

    def table(name):
        src, where = (I["first"], I["first_at"]) if name in I["first_at"] else (I["second"], I["second_at"])
        a, n = where[name]
        return src[:, a:a + n]

    load(X, I["x"][0].rearrange("(t p) d -> p t d", p=P), start_in)
    load(ident, table("ident"), start_in)
    load(gain1, I["norm_gain"][0].rearrange("(k p) -> p k", p=P), start_in)
    start_loaded = load(cT, I["c_2"][0].rearrange("(k p) -> p k", p=P), start_in)

    blocks_behind = [0, 0]

    def slot_view(j, k, n):
        return slot[j][:, 0:k * n].rearrange("p (k n) -> p k n", k=k)

    def load_chunk(src, c, i=None):
        j = c % 2
        if c >= 2:
            sp.after(Mark(block_done.sem, blocks_behind[c], i, 4))
        slot_in[j].mark(sp.eng.dma_start(slot_view(j, src.shape[1], src.shape[2]), src))

    def used(blocks):
        blocks_behind.append(blocks + (blocks_behind[-1] if len(blocks_behind) > 2 else 0))

    def stream(W, starts_widths, blocks=2):
        for a, n in starts_widths:
            c = len(blocks_behind) - 2
            load_chunk(W[:, a:a + n].rearrange("(k p) n -> p k n", p=P), c)
            used(blocks)

    def stream_loop(W, c0, pairs):
        c = len(blocks_behind) - 2
        with engine_loop(nc, pairs, (sp,), {slot_in[0]: 16, slot_in[1]: 16}) as (i, _):
            for j in range(2):
                load_chunk(W[:, bass.ds(i * 2 * CW + c0 + j * CW, CW)].rearrange("(k p) n -> p k n", p=P), c + j, i)
        for _ in range(2 * pairs):
            used(2)

    w_in, w_in2 = I["w_in"][0], I["w_in_2"][0]
    MLA_IN = Q_LORA + KV_LORA + ROPE
    GATES = MLA_IN + 3 * RD + 64 + 64 + 128
    stream(w_in, [(0, CW), (CW, CW)])
    stream_loop(w_in, 2 * CW, 9)
    for name in ("w_branch_sb", "w_branch_ret", "w_out"):
        stream(I[name][0], [(0, CW), (CW, CW)])
    stream(w_in2, [(0, MLA_IN)] + [(MLA_IN + CW * j, CW) for j in range(3)] + [(MLA_IN + 3 * CW, 256)])
    for j in range(4):
        stream(w_in2, [(GATES + CW * j, CW)], 10 if j == 0 else 2)
    stream(I["w_o_mla_2"][0], [(0, D)], 4)
    stream(I["w_o_rwkv_2"][0], [(0, D)], 4)
    stream(I["w_out_2"][0], [(0, CW), (CW, CW)])
    stream(I["w_query_2"][0], [(CW * j, CW) for j in range(4)])
    for c in slot_in:
        c.count = 0

    for k, v in enumerate((1.0, EPS, GN_EPS)):
        col_ready = dve.mark(dve.eng.memset(col[:, k:k + 1], v))
    for _ in range(2):
        taken[0].mark(dve.after(dve.now()).memset(stat[:, 190:191], 0.0))
        dve.after(taken[0].now())
        taken[1].mark(act.after(col_ready).copy(stat[:, 191:192], col[:, 0:1]))
        act.after(taken[1].now())

    next_slot, next_bank = [0], [0]

    def next_chunk():
        j = next_slot[0]
        next_slot[0] = 1 - j
        slot_in[j].count += 16
        return j, slot_in[j].now()

    def open_block(t, arrived):
        b = next_bank[0]
        next_bank[0] = (b + 1) % 4
        pe.after(arrived, taken[t].now(1))
        return bank[b]

    def token_block(lhs, w, t, arrived):
        sums = open_block(t, arrived)[:, 0:w.shape[2]]
        for k in range(w.shape[1]):
            mm = pe.eng.matmul(sums, lhsT=lhs[:, k, t * P:(t + 1) * P], rhs=w[:, k, :],
                               start=(k == 0), stop=(k == w.shape[1] - 1))
        return sums, block_done.mark(mm)

    def project(lhs, kn, n, take, parts=1, before=None):
        j, arrived = next_chunk()
        w = slot_view(j, kn, n * parts)
        for part in range(parts):
            for t in range(TT):
                if before:
                    before(part * TT + t)
                take(part, t, *token_block(lhs, w[:, :, part * n:(part + 1) * n], t, arrived))

    def take_copy(dst, t, sums, done):
        if t == 0:
            return taken[0].mark(dve.after(done).tensor_copy(dst, sums))
        return taken[1].mark(act.after(done).copy(dst, sums))

    def rstd(dst, sums, n, eps_col, *after):
        m = act.mark(act.after(*after).activation(dst, sums, ACT.Sqrt, bias=col[:, eps_col:eps_col + 1],
                                                  scale=1.0 / n))
        return dve.mark(dve.after(m).reciprocal(dst, dst))

    bank_read = {b: [] for b in range(4, 8)}

    def transposes(dst, tiles, ready, scale=None, bias=None, size=4):
        marks = []
        for g in range(0, len(tiles), size):
            b = 4 + (g // size) % 4
            pe.after(*ready, *bank_read[b])
            n = size
            for k in range(n):
                tr = pe.eng.transpose(bank[b][:, k * P:(k + 1) * P], tiles[g + k], ident)
            tr = pe.mark(tr)
            to, frm = dst(g, n), bank[b][:, 0:n * P].rearrange("p (k n) -> p k n", k=n)
            if scale is None:
                q = (dve, act)[(g // size) % 2]
                m = q.mark(q.after(tr).tensor_copy(to, frm) if q is dve else q.after(tr).copy(to, frm))
            else:
                m = dve.mark(dve.after(tr).tensor_tensor(to, frm, scale(g, n), ALU.mult))
            bank_read[b] = [m]
            if bias is not None:
                m = dve.mark(dve.after(m).tensor_tensor(to, to, bias(g, n), ALU.add))
            marks.append(m)
        return marks

    def features(tmp, gain, bias, *ready):
        for t in range(TT):
            m = act.mark(act.after(*ready).activation(tmp[:, t, :], X[:, t, :], ACT.Square,
                                                      accum_out=stat[:, t:t + 1]))
        r = rstd(stat[:, 2:4], stat[:, 0:2], D, 1, m)
        m = dve.mark(dve.after(r).tensor_tensor(tmp, X, stat[:, 2:4].unsqueeze(2).broadcast_to([P, TT, D]),
                                                ALU.mult))
        tiles = [tmp[:, t, k * P:(k + 1) * P] for t in range(TT) for k in range(KT)]

        def of(v):
            return lambda g, n: v[:, g % KT:g % KT + n].unsqueeze(2).broadcast_to([P, n, P])
        return transposes(lambda g, n: hT[:, g % KT:g % KT + n, (g // KT) * P:(g // KT + 1) * P], tiles, [m],
                          of(gain), of(bias) if bias is not None else None)

    P1 = carve("P1", TT, 10, D)
    Q_, K_, V_, G_, RQ, RK, RV, RG, M1, M2 = range(10)
    negtri, negones, lt = carve("negtri", P), carve("negones", P), carve("lt", P)
    ltbias = carve("ltbias", 3 * P)
    cos1, sin1 = carve("cos1", TT, P), carve("sin1", TT, P)
    decay = carve("decay", RET_H, 3 * P)
    sbgain = carve("sbgain", 2)
    for name, ap in (("negtri", negtri), ("negones", negones), ("lt", lt), ("ltbias", ltbias)):
        load(ap, table(name), first_in, act)
    for name, ap in (("cos", cos1), ("sin", sin1)):
        load(ap, table(name).rearrange("p (t n) -> p t n", t=TT), first_in, act)
    load(decay, table("decay").rearrange("p (h n) -> p h n", h=RET_H), first_in, act)
    load(sbgain[:, 0:1], I["sb_q_gain"].rearrange("a p -> p a"), first_in, act)
    first_loaded = load(sbgain[:, 1:2], I["sb_k_gain"].rearrange("a p -> p a"), first_in, act)
    work_top = cursor[0]

    h_ready = features(P1[:, :, M2, :], gain1, None, start_loaded)
    c_ready = act.mark(act.after(start_loaded).activation(cs, cT, ACT.Silu))

    AW, PIECES = 256, ((0, 1), (2,), (3, 4), (5,))
    NP = 6
    ada_w = [carve(f"ada_w{j}", KT, AW) for j in range(2)]
    ada_acc = [carve(f"ada_acc{j}", AW) for j in range(2)]
    ada_b = [carve(f"ada_b{j}", AW) for j in range(2)]
    mod_row = [carve(f"mod_row{j}", AW) for j in range(2)]
    w_ada, mod_dram = I["w_ada_2"][0], I["mod_dram"]
    for j in range(2):
        load(mod_row[j][0:1, :], I["b_ada_2"][:, 0:AW], mod_out[j], act)
    P1c = P1.rearrange("p t g d -> p t (g d)")
    pe.after(*h_ready)
    dve.after(c_ready, *h_ready)
    act.after(*h_ready)
    with engine_loop(nc, 4, (pe, dve, act),
                     {pe: 6, dve: 54, ada_in[0]: 96, ada_in[1]: 96, mod_out[0]: 48, mod_out[1]: 48, block_done: 4,
                      taken[0]: 2, taken[1]: 2, slot_in[0]: 16, slot_in[1]: 16}) as (i, start):
        row_done = {}

        def sum_pieces(b):
            for a in PIECES[b]:
                acc, w = ada_acc[a % 2], ada_w[a % 2]
                arrived = start[ada_in[a % 2]]
                dve.after(Mark(arrived.sem, arrived.base + 32 * (a // 2 + 1), i, 96))
                m = dve.mark(dve.after(start[pe]).tensor_scalar(acc, w[:, 0, :], cs[:, 0:1], None, ALU.mult))
                for k in range(1, KT):
                    m = dve.mark(dve.after(m).scalar_tensor_tensor(acc, w[:, k, :], cs[:, k:k + 1], acc,
                                                                   ALU.mult, ALU.add))
                piece_done[a] = m

        def sum_rows(b):
            for a in PIECES[b]:
                row = bank[4 + a % 2][0:1, 0:AW]
                m = pe.mark(pe.after(piece_done[a]).matmul(row, lhsT=col[:, 0:1], rhs=ada_acc[a % 2],
                                                           start=True, stop=True))
                left = start[mod_out[a % 2]]
                dve.after(m, Mark(left.sem, left.base + 16 * (a // 2), i, 48))
                row_done[a] = dve.mark(dve.eng.tensor_tensor(mod_row[a % 2][0:1, :], row,
                                                             ada_b[a % 2][0:1, :], ALU.add))

        def load_piece(a):
            at = i * (NP * AW) + a * AW
            ada_in[a % 2].mark(act.eng.dma_start(
                ada_w[a % 2], w_ada[:, bass.ds(at, AW)].rearrange("(k p) n -> p k n", p=P)))
            ada_in[a % 2].mark(act.eng.dma_start(ada_b[a % 2][0:1, :], I["b_ada_2"][:, bass.ds(at, AW)]))

        def store_rows(b):
            for a in PIECES[b]:
                act.after(row_done[a])
                mod_out[a % 2].mark(act.eng.dma_start(mod_dram[:, bass.ds(i * (NP * AW) + a * AW, AW)],
                                               mod_row[a % 2][0:1, :]))
                if a + 2 < NP:
                    load_piece(a + 2)

        piece_done = {}
        act.after(start[dve])
        load_piece(0)
        load_piece(1)
        for j in range(2):
            def take(part, t, sums, done):
                take_copy(P1c[:, t, bass.ds(i * (2 * CW) + j * CW, CW)], t, sums, done)
                sum_rows(2 * j + t)
                store_rows(2 * j + t)
            project(hT, KT, CW, take, before=lambda b: sum_pieces(2 * j + b))
    mod_stored = [c.now() for c in mod_out]

    fenced = fence()
    act.after(taken[0].now(), taken[1].now())
    dve.after(taken[0].now(), taken[1].now())
    sq = P1[:, :, M1:M2 + 1, :]
    sums = stat[:, 0:32].rearrange("p (t g h) -> p t g h", t=TT, g=2)
    for t in range(TT):
        m = act.mark(act.eng.activation(sq[:, t], P1[:, t, Q_:K_ + 1, :], ACT.Square))
        m = dve.mark(dve.after(m).tensor_reduce(sums[:, t], sq[:, t].rearrange("p g (h d) -> p g h d", h=SB_H), AX, ALU.add))
    qk_rstd = rstd(stat[:, 0:32], stat[:, 0:32], SB_D, 1, m)
    gate_ready = act.mark(act.eng.activation(P1[:, :, G_, :], P1[:, :, G_, :], ACT.Silu))
    gains_ready = dve.mark(dve.after(first_loaded).tensor_scalar(sbgain[:, 0:1], sbgain[:, 0:1], SB_D ** -0.5, None, ALU.mult))

    cursor[0] = work_top
    sb_n = [carve(f"sb_n{j}", TT, 2, P) for j in range(2)]
    sb_T = [carve(f"sb_T{j}", 2, TT * P) for j in range(2)]
    sb_e = [carve(f"sb_e{j}", 3 * P) for j in range(2)]
    sb_p = [carve(f"sb_p{j}", 3 * P) for j in range(2)]
    sb_w = [carve(f"sb_w{j}", 3 * P) for j in range(2)]
    heads1 = P1.rearrange("p t g (h d) -> p t g h d", h=SB_H)
    rq = stat[:, 0:32].rearrange("p (t g h) -> p t g h", t=TT, g=2)
    T01, T1 = slice(0, 2 * P), slice(2 * P, 3 * P)
    ret_gain, bmerge = carve("ret_gain", D), carve("bmerge", 2 * D)
    load(ret_gain, I["ret_out_gain"][0].rearrange("h d -> (h d)").partition_broadcast(P), merge_in, act)
    merge_loaded = load(bmerge, I["b_merge"][0].rearrange("a d -> (a d)").partition_broadcast(P), merge_in, act)
    dve.after(qk_rstd, gate_ready, gains_ready)
    pe.after(first_loaded)
    with engine_loop(nc, 4, (pe, dve, act),
                     {pe: 8, dve: 14, act: 8, block_done: 4, taken[0]: 2, taken[1]: 2,
                      slot_in[0]: 16, slot_in[1]: 16}) as (i, start):
        n, zm, pm, wm, tr, z2 = {}, {}, {}, {}, {}, {}
        dve.after(start[pe], start[act])
        act.after(start[pe], start[dve])

        def head(j):
            return bass.ds(i * 2 + j, 1)

        def cols(j):
            return bass.ds(i * (2 * SB_D) + j * SB_D, SB_D)

        def normed(j):
            n[j] = dve.mark(dve.eng.tensor_tensor(sb_n[j], P1[:, :, Q_:K_ + 1, cols(j)],
                                                  rq[:, :, :, head(j)].broadcast_to([P, TT, 2, SB_D]), ALU.mult))

        def turned(j):
            b = bank[4 + j]
            pe.after(n[j])
            for g in range(2):
                for t in range(TT):
                    m = pe.eng.transpose(b[:, (2 * g + t) * P:(2 * g + t + 1) * P], sb_n[j][:, t, g, :], ident)
            m = pe.mark(m)
            for g in range(2):
                tr[j] = dve.mark(dve.after(m).tensor_scalar(sb_T[j][:, g, :], b[:, g * 2 * P:(g + 1) * 2 * P],
                                                            sbgain[:, g:g + 1], None, ALU.mult))

        def scores(j):
            z, (q, k) = bank[6 + j], (sb_T[j][:, 0, :], sb_T[j][:, 1, :])
            pe.after(tr[j])
            pe.eng.matmul(z[:, T01], lhsT=k[:, 0:P], rhs=q, start=True, stop=False, skip_group_check=True)
            m = pe.mark(pe.eng.matmul(z[:, T1], lhsT=k[:, P:], rhs=q[:, P:], start=False, stop=False,
                                      skip_group_check=True))
            m = act.mark(act.after(m).activation(sb_e[j], z[:, 0:3 * P], ACT.Abs))
            m = act.mark(act.after(m).activation(sb_e[j], sb_e[j], ACT.Exp, scale=-1.0))
            m = act.mark(act.after(m).activation(sb_e[j], sb_e[j], ACT.Ln, bias=col[:, 0:1]))
            m = dve.mark(dve.after(m).scalar_tensor_tensor(sb_p[j], z[:, 0:3 * P], 0.0, sb_e[j], ALU.max, ALU.add))
            diag = sb_p[j].rearrange("p (b n) -> p b n", b=3)[:, 0:3:2, :]
            pm[j] = dve.mark(dve.after(m).tensor_tensor(diag, diag, lt.unsqueeze(1).broadcast_to([P, 2, P]), ALU.mult))

        def kept(j):
            z = bank[6 + j]
            pe.after(pm[j])
            pe.eng.matmul(z[:, T01], lhsT=negtri, rhs=sb_p[j][:, T01], start=False, stop=False, skip_group_check=True)
            pe.eng.matmul(z[:, P:2 * P], lhsT=negones, rhs=sb_p[j][:, T1], start=False, stop=False, skip_group_check=True)
            m = pe.mark(pe.eng.matmul(z[:, T1], lhsT=negtri, rhs=sb_p[j][:, T1], start=False, stop=True,
                                      skip_group_check=True))
            m = dve.mark(dve.after(m).scalar_tensor_tensor(sb_w[j], z[:, 0:3 * P], 0.0, ltbias, ALU.min, ALU.add))
            wm[j] = act.mark(act.after(m).activation(sb_w[j], sb_w[j], ACT.Exp))

        def weighed(j):
            o, w = bank[4 + j], sb_w[j]
            v = [P1[:, t, V_, cols(j)] for t in range(TT)]
            pe.after(wm[j])
            pe.eng.matmul(o[:, 0:P], lhsT=w[:, 0:P], rhs=v[0], start=True, stop=True)
            pe.eng.matmul(o[:, P:2 * P], lhsT=w[:, P:2 * P], rhs=v[0], start=True, stop=False)
            m = pe.mark(pe.eng.matmul(o[:, P:2 * P], lhsT=w[:, T1], rhs=v[1], start=False, stop=True))
            g = P1[:, :, G_, cols(j)]
            dve.mark(dve.after(m).tensor_tensor(g, o[:, 0:2 * P].rearrange("p (t d) -> p t d", t=TT), g, ALU.mult))

        def before(b):
            for j in range(2):
                [normed, turned, scores, kept][b](j)

        for c in range(2):
            project(hT, KT, CW, lambda part, t, sums, done: take_copy(
                P1c[:, t, bass.ds(i * (2 * CW) + RQ * D + c * CW, CW)], t, sums, done),
                before=lambda b: before(2 * c + b))
        for j in range(2):
            weighed(j)

    fence()
    act.after(*[c.now() for c in taken])
    dve.after(*[c.now() for c in taken])
    m = act.mark(act.eng.activation(P1[:, :, RG, :], P1[:, :, RG, :], ACT.Silu))
    gate_ready = dve.mark(dve.after(m, merge_loaded).tensor_tensor(
        P1[:, :, RG, :], P1[:, :, RG, :], ret_gain.unsqueeze(1).broadcast_to([P, TT, D]), ALU.mult))

    ret_t = [carve(f"ret_t{j}", TT, 2, P) for j in range(2)]
    ret_n = [carve(f"ret_n{j}", TT, 2, 2, P) for j in range(2)]
    ret_T = [carve(f"ret_T{j}", 2, 2, TT * P) for j in range(2)]
    ret_w = [carve(f"ret_w{j}", 3 * P) for j in range(2)]
    with engine_loop(nc, 2, (pe, dve, act),
                     {pe: 8, dve: 16, act: 4, block_done: 4, taken[0]: 2, taken[1]: 2,
                      slot_in[0]: 16, slot_in[1]: 16}) as (i, start):
        n, tr, wm = {}, {}, {}
        dve.after(start[pe], start[act])
        act.after(start[pe], start[dve])

        def rotated(j):
            def half(h):
                return P1[:, :, RQ:RK + 1, bass.ds(i * (2 * RET_D) + (j * RET_D + h * P), P)]
            c, s = (v.unsqueeze(2).broadcast_to([P, TT, 2, P]) for v in (cos1, sin1))
            for h, (x, y, op) in enumerate(((c, s, ALU.subtract), (s, c, ALU.add))):
                dve.mark(dve.eng.tensor_tensor(ret_t[0], half(0), x, ALU.mult))
                m = dve.mark(dve.eng.tensor_tensor(ret_t[1], half(1), y, ALU.mult))
                n[j] = dve.mark(dve.after(m).tensor_tensor(ret_n[j][:, :, :, h, :], ret_t[0], ret_t[1], op))
                dve.after(n[j])

        def turned(j):
            for g in range(2):
                b = bank[4 + 2 * j + g]
                pe.after(n[j])
                for h in range(2):
                    for t in range(TT):
                        m = pe.eng.transpose(b[:, (2 * h + t) * P:(2 * h + t + 1) * P], ret_n[j][:, t, g, h, :], ident)
                m = pe.mark(m)
                dst, src = ret_T[j][:, g, :, :], b.rearrange("p (h n) -> p h n", h=2)
                tr[j, g] = dve.mark(dve.after(m).tensor_copy(dst, src)) if g == 0 else act.mark(act.after(m).copy(dst, src))

        def scores(j):
            z, q, k = bank[4 + 2 * j], ret_T[j][:, 0], ret_T[j][:, 1]
            pe.after(tr[j, 0], tr[j, 1])
            for h in range(2):
                pe.eng.matmul(z[:, T01], lhsT=k[:, h, 0:P], rhs=q[:, h, :], start=(h == 0), stop=False,
                              skip_group_check=True)
                m = pe.eng.matmul(z[:, T1], lhsT=k[:, h, P:], rhs=q[:, h, P:], start=False, stop=(h == 1),
                                  skip_group_check=True)
            m = pe.mark(m)
            wm[j] = dve.mark(dve.after(m, first_loaded).tensor_tensor(
                ret_w[j], z[:, 0:3 * P], decay[:, bass.ds(i * 2 + j, 1), :].rearrange("p a n -> p (a n)"), ALU.mult))

        def weighed(j):
            o, w = bank[5 + 2 * j], ret_w[j]
            v = [P1[:, t, RV, bass.ds(i * (2 * RET_D) + j * RET_D, RET_D)] for t in range(TT)]
            pe.after(wm[j])
            pe.eng.matmul(o[:, 0:RET_D], lhsT=w[:, 0:P], rhs=v[0], start=True, stop=True)
            pe.eng.matmul(o[:, RET_D:], lhsT=w[:, P:2 * P], rhs=v[0], start=True, stop=False)
            m = pe.mark(pe.eng.matmul(o[:, RET_D:], lhsT=w[:, T1], rhs=v[1], start=False, stop=True))
            act.mark(act.after(m).copy(P1[:, :, RQ, bass.ds(i * (2 * RET_D) + j * RET_D, RET_D)],
                                       o.rearrange("p (t d) -> p t d", t=TT)))

        def before(b):
            for j in range(2):
                [rotated, turned, scores, weighed][b](j)

        for c in range(2):
            project(hT, KT, CW, lambda part, t, sums, done: take_copy(
                P1c[:, t, bass.ds(i * (2 * CW) + M1 * D + c * CW, CW)], t, sums, done),
                before=lambda b: before(2 * c + b))

    fence()
    act.after(*[c.now() for c in taken])
    dve.after(*[c.now() for c in taken])
    cursor[0] = work_top
    oaT, obT = carve("oaT", KT, S), carve("obT", KT, S)

    def tiles_of(x):
        return [x[:, t, k * P:(k + 1) * P] for t in range(TT) for k in range(x.shape[2] // P)]

    def to_features(dst, x, *ready):
        n = x.shape[2] // P
        return transposes(lambda g, c: dst[:, g % n:g % n + c, (g // n) * P:(g // n + 1) * P], tiles_of(x), ready,
                          size=min(n, 4))

    oa_ready = to_features(oaT, P1[:, :, G_, :])
    merge = P1[:, :, M1:M2 + 1, :]
    bm = bmerge.rearrange("p (g d) -> p g d", g=2)
    for t in range(TT):
        m = dve.mark(dve.after(merge_loaded).tensor_tensor(merge[:, t], merge[:, t], bm, ALU.add))
        merge_ready = act.mark(act.after(m).activation(merge[:, t], merge[:, t], ACT.Sigmoid))
    ret_o, ret_sq = P1[:, :, RQ, :], P1[:, :, RK, :]
    m = act.mark(act.eng.activation(ret_sq, ret_o, ACT.Square))
    rs = stat[:, 32:40].rearrange("p (t h) -> p t h", t=TT)
    for t in range(TT):
        m = dve.mark(dve.after(m).tensor_reduce(rs[:, t], ret_sq[:, t].rearrange("p (h d) -> p h d", h=RET_H), AX, ALU.add))
    m = rstd(stat[:, 32:40], stat[:, 32:40], RET_D, 1, m)
    for t in range(TT):
        o = ret_o[:, t].rearrange("p (h d) -> p h d", h=RET_H)
        m = dve.mark(dve.after(m).tensor_tensor(o, o, rs[:, t].unsqueeze(2).broadcast_to([P, RET_H, RET_D]), ALU.mult))
    m = dve.mark(dve.after(m, gate_ready).tensor_tensor(ret_o, ret_o, P1[:, :, RG, :], ALU.mult))
    ret_ready = m

    last = {}

    def take_gated(gate, merged, aside, add, ready):
        def take(c, t, sums, done):
            at = slice(c * CW, (c + 1) * CW)
            to = aside if add else merged
            if t == 0:
                m = taken[0].mark(dve.after(done, ready).tensor_tensor(to[:, t, at], sums, gate(t, at), ALU.mult))
            else:
                m = taken[1].mark(act.after(done).copy(aside[:, t, at], sums))
                m = dve.mark(dve.after(m, ready).tensor_tensor(to[:, t, at], aside[:, t, at], gate(t, at), ALU.mult))
            if add:
                m = dve.mark(dve.after(m).tensor_tensor(merged[:, t, at], merged[:, t, at], aside[:, t, at], ALU.add))
            last["merged"] = m
        return take

    def take_residual(aside, gate=None):
        def take(c, t, sums, done):
            at = slice(c * CW, (c + 1) * CW)
            x, s = X[:, t, at], aside[:, t, at]
            if t == 1:
                done = taken[1].mark(act.after(done).copy(s, sums))
                sums = s
            if gate is None:
                m = dve.after(done).tensor_tensor(x, x, sums, ALU.add)
            else:
                m = dve.after(done).tensor_tensor(s, sums, gate[:, at], ALU.mult)
            m = taken[0].mark(m) if t == 0 else dve.mark(m)
            if gate is not None:
                m = dve.mark(dve.after(m).tensor_tensor(x, x, s, ALU.add))
        return take

    merged, aside = P1[:, :, Q_, :], P1[:, :, K_, :]
    pe.after(*oa_ready)
    for c in range(2):
        take = take_gated(lambda t, at: P1[:, t, M1, at], merged, aside, False, merge_ready)
        project(oaT, KT, CW, lambda part, t, sums, done: take(c, t, sums, done))
    act.after(last["merged"])
    ob_ready = to_features(obT, ret_o, ret_ready)
    pe.after(*ob_ready)
    for c in range(2):
        take = take_gated(lambda t, at: P1[:, t, M2, at], merged, aside, True, merge_ready)
        project(obT, KT, CW, lambda part, t, sums, done: take(c, t, sums, done))
    m_ready = to_features(hT, merged, last["merged"])
    pe.after(*m_ready)
    for c in range(2):
        take = take_residual(aside)
        project(hT, KT, CW, lambda part, t, sums, done: take(c, t, sums, done))

    fence()
    for q in everyone + (sp,):
        q.after(*[c.now() for c in taken])
    act.after(*mod_stored)
    cursor[0] = persistent_top
    P2 = carve("P2", TT, w_in2.shape[1])
    upto, below, shift, carry = (carve(n, P) for n in ("upto", "below", "shift", "carry"))
    ends = carve("ends", 2)
    strict, incl, id64, a0 = (carve(n, RN) for n in ("strict", "incl", "id64", "a0"))
    levels = carve("levels", 6 * RN)
    causal, iota, invf = carve("causal", 3 * P), carve("iota", P), carve("invf", ROPE // 2)
    mod_rows = carve("mod_rows", P)
    pos = carve("pos", TT, dt=I32)
    qa_gain, kva_gain, q_gain, k_gain = carve("qa_gain", Q_LORA), carve("kva_gain", KV_LORA), carve("q_gain", QH), carve("k_gain", QH)
    mla_weights = cursor[0]
    w_uq, w_ukv = carve("w_uq", 2, MLA_H * QH), carve("w_ukv", 1, MLA_H * (NOPE + VH))
    lora = carve("lora", RD)
    w_gate = carve("w_gate", RD)
    base_rows = carve("base_rows", 2, RD)
    ones_row = carve("ones_row", P)
    vec = {n: carve(n, RD) for n in ("k_k_2", "k_a_2", "r_k_2", "ln_x_w_2", "ln_x_b_2")}
    mu_at = cursor[0]
    mu = carve("mu", 3 * RD + 256)
    block2_top = cursor[0]

    mods = mod_rows[0:48, :]
    load(mods, mod_dram.rearrange("a (r p) -> (a r) p", p=P), mod_in, act)
    load(mod_rows[48:56, :], I["norm_mix_2"][0].rearrange("(r p) -> r p", p=P), mod_in, act)
    mod_loaded = load(mod_rows[56:64, :], I["norm_ffn_2"][0].rearrange("(r p) -> r p", p=P), mod_in, act)
    for name, ap in (("upto", upto), ("below", below), ("shift", shift), ("carry", carry), ("ends", ends),
                     ("strict", strict), ("incl", incl), ("id64", id64), ("a0", a0), ("levels", levels),
                     ("causal", causal), ("iota", iota), ("invf", invf)):
        load(ap, table(name), second_in, act)

    def spread(name):
        v = I[name][0]
        return (v if len(v.shape) == 1 else v.rearrange("h d -> (h d)")).partition_broadcast(P)

    load(pos, I["positions_2"].rearrange("a (t p) -> p (a t)", p=P), second_in, act)
    for name, ap in (("q_a_norm_2", qa_gain), ("kv_a_norm_2", kva_gain), ("q_norm_2", q_gain), ("k_norm_2", k_gain)):
        load(ap, spread(name), second_in, act)
    load(w_uq, I["w_uq_2"][0].rearrange("(k p) n -> p k n", p=P), second_in, act)
    load(w_ukv, I["w_ukv_2"][0].rearrange("(k p) n -> p k n", p=P), second_in, act)
    load(lora[0:64, :], I["w_decay_up_2"][0], second_in, act)
    load(lora[64:128, :], I["w_aaa_up_2"][0], second_in, act)
    load(w_gate, I["w_gate_up_2"][0], second_in, act)
    load(base_rows[0:1, 0, :], I["decay_base_2"], second_in, act)
    load(base_rows[0:1, 1, :], I["aaa_base_2"], second_in, act)
    second_loaded = load(gt, mod_dram[0, 2 * D:3 * D].partition_broadcast(P), second_in, act)
    for name, ap in list(vec.items()) + [("mu_shift_2", mu)]:
        third_loaded = load(ap, spread(name), third_in, act)
    ones_row_ready = pool.mark(pool.eng.memset(ones_row[0:1, :], 1.0))

    side = [0]

    def side_bank(*ready):
        b = 4 + side[0] % 4
        side[0] += 1
        pe.after(*bank_read[b], *ready)
        return b

    b = side_bank(mod_loaded)
    m = pe.mark(pe.eng.transpose(bank[b][:, 0:64], mod_rows[0:64, :], ident[0:64, 0:64]))
    m = dve.mark(dve.after(m).tensor_copy(modT.rearrange("p a k -> p (a k)"), bank[b][:, 0:64]))
    bank_read[b] = [m]
    for k, g in ((1, 6), (4, 7)):
        gains = dve.mark(dve.after(m).scalar_tensor_tensor(modT[:, g, :], modT[:, k, :], 1.0, modT[:, g, :], ALU.add, ALU.mult))
    h_ready = features(P2[:, :, 0:D], modT[:, 6, :], modT[:, 0, :], gains)
    pe.after(*h_ready)
    for q in (dve, act):
        q.after(*h_ready)
    at = [0]
    for n in (MLA_IN, CW, CW, CW, 256):
        project(hT, KT, n, lambda part, t, sums, done: take_copy(P2[:, t, at[0]:at[0] + n], t, sums, done))
        at[0] += n

    all_in = [c.now() for c in taken]
    dve.after(*all_in, second_loaded)
    act.after(*all_in, second_loaded)
    lat = carve("lat", TT, Q_LORA + KV_LORA)
    latT = carve("latT", 3, S)
    kpe = carve("kpe", TT, 1, ROPE)
    tmp = carve("tmp", TT, MLA_H * P)
    Qm, KVm = carve("Qm", TT, MLA_H * QH), carve("KVm", TT, MLA_H * P)
    qh, kh = carve("qh", TT, MLA_H, QH), carve("kh", TT, MLA_H, QH)
    cs2 = carve("cs2", 4, TT * ROPE // 2)
    ropet = [carve(f"ropet{j}", TT, MLA_H, ROPE // 2) for j in range(2)]
    for t in range(TT):
        for j, (c0, n) in enumerate(((0, Q_LORA), (Q_LORA, KV_LORA), (Q_LORA + KV_LORA, ROPE))):
            m = act.mark(act.eng.activation(tmp[:, t, 0:n], P2[:, t, c0:c0 + n], ACT.Square,
                                            accum_out=stat[:, 48 + 2 * j + t:49 + 2 * j + t]))
            act.after(m)
    for j, n in enumerate((Q_LORA, KV_LORA, ROPE)):
        r = rstd(stat[:, 48 + 2 * j:50 + 2 * j], stat[:, 48 + 2 * j:50 + 2 * j], n, 1, m)
    for t in range(TT):
        for j, (c0, n, g) in enumerate(((0, Q_LORA, qa_gain), (Q_LORA, KV_LORA, kva_gain))):
            m = dve.mark(dve.after(r).scalar_tensor_tensor(lat[:, t, c0:c0 + n], P2[:, t, c0:c0 + n],
                                                           stat[:, 48 + 2 * j + t:49 + 2 * j + t], g, ALU.mult, ALU.mult))
        kpe_ready = dve.mark(dve.eng.scalar_tensor_tensor(
            kpe[:, t, 0, :], P2[:, t, Q_LORA + KV_LORA:MLA_IN], stat[:, 52 + t:53 + t], k_gain[:, NOPE:], ALU.mult, ALU.mult))
    lat_ready = to_features(latT, lat, m)

    two_pi, pi = 2 * np.pi, float(np.nextafter(np.float32(np.pi), np.float32(0)))
    c1 = 6.28125
    c2 = float(np.round((two_pi - c1) * 2.0 ** 21) / 2.0 ** 21)
    c3 = two_pi - c1 - c2
    magic = 1.5 * 2.0 ** 23
    angle, turns, cosv, sinv = (cs2[:, k, :] for k in range(4))
    posf = stat[:, 60:62]
    m = dve.mark(dve.eng.tensor_copy(posf, pos))
    m = dve.mark(dve.after(m).tensor_tensor(angle.rearrange("p (t n) -> p t n", t=TT), posf.unsqueeze(2).broadcast_to([P, TT, ROPE // 2]),
                                            invf.unsqueeze(1).broadcast_to([P, TT, ROPE // 2]), ALU.mult))
    m = dve.mark(dve.after(m).tensor_scalar(turns, angle, 1 / two_pi, magic, ALU.mult, ALU.add))
    m = dve.mark(dve.after(m).tensor_scalar(turns, turns, -magic, None, ALU.add))
    for c in (c1, c2, c3):
        m = dve.mark(dve.after(m).scalar_tensor_tensor(angle, turns, -c, angle, ALU.mult, ALU.add))
    m = dve.mark(dve.after(m).tensor_scalar(angle, angle, pi, -pi, ALU.min, ALU.max))
    m = dve.mark(dve.after(m).tensor_scalar(cosv, angle, np.pi / 2, None, ALU.add))
    m = dve.mark(dve.after(m).tensor_scalar(turns, cosv, np.pi, -two_pi, ALU.is_gt, ALU.mult))
    m = dve.mark(dve.after(m).tensor_tensor(cosv, cosv, turns, ALU.add))
    m = dve.mark(dve.after(m).tensor_scalar(cosv, cosv, pi, -pi, ALU.min, ALU.max))
    m = act.mark(act.after(m).activation(cs2[:, 2, :], cosv, ACT.Sin))
    angles_ready = act.mark(act.eng.activation(sinv, angle, ACT.Sin))
    m = dve.mark(dve.eng.tensor_scalar(q_gain, q_gain, QH ** -0.5, None, ALU.mult))
    cos2, sin2 = (cs2[:, k, :].rearrange("p (t a n) -> p t a n", t=TT, a=1) for k in (2, 3))

    pe.after(*lat_ready)
    for half in range(2):
        n = MLA_H * QH // 2
        for t in range(TT):
            sums, done = token_block(latT, w_uq[:, :, half * n:(half + 1) * n], t, second_loaded)
            take_copy(Qm[:, t, half * n:(half + 1) * n], t, sums, done)
    for half in range(2):
        for t in range(TT):
            sums, done = token_block(latT[:, 2:3, :], w_ukv[:, :, half * CW:(half + 1) * CW], t, second_loaded)
            take_copy(KVm[:, t, half * CW:(half + 1) * CW], t, sums, done)
    for q in (dve, act):
        q.after(*[c.now() for c in taken])
    Qv = Qm.rearrange("p t (h d) -> p t h d", h=MLA_H)
    KVv = KVm.rearrange("p t (h d) -> p t h d", h=MLA_H)
    sqQ = tmp[:, :, 0:MLA_H * QH].rearrange("p t (h d) -> p t h d", h=MLA_H)
    m = act.mark(act.after(m).activation(sqQ, Qv, ACT.Square))
    st = [stat[:, 64 + 16 * k:80 + 16 * k] for k in range(3)]
    sv = [x.rearrange("p (t h) -> p t h", t=TT) for x in st]
    dve.after(m)
    dve.mark(dve.eng.tensor_reduce(sv[0], sqQ[:, :, :, 0:NOPE], AX, ALU.add))
    m = dve.mark(dve.eng.tensor_reduce(sv[1], sqQ[:, :, :, NOPE:], AX, ALU.add))
    sqK = tmp.rearrange("p t (h d) -> p t h d", h=MLA_H)
    m = act.mark(act.after(m).activation(sqK, KVv, ACT.Square))
    m = dve.mark(dve.after(m).tensor_reduce(sv[2], sqK[:, :, :, 0:NOPE], AX, ALU.add))
    for k, n in enumerate((NOPE, ROPE, NOPE)):
        r = rstd(st[k], st[k], n, 1, m)

    def over(v, n):
        return v.unsqueeze(3).broadcast_to([P, TT, MLA_H, n])

    def gain(v, n):
        return v.unsqueeze(1).broadcast_to([P, MLA_H, n])

    dve.after(r)
    for dst, src, f, g, n, at_ in ((qh, Qv, 0, q_gain[:, 0:NOPE], NOPE, 0), (qh, Qv, 1, q_gain[:, NOPE:], ROPE, NOPE),
                              (kh, KVv, 2, k_gain[:, 0:NOPE], NOPE, 0)):
        d = dst[:, :, :, at_:at_ + n]
        m = dve.mark(dve.eng.tensor_tensor(d, src[:, :, :, at_:at_ + n], over(sv[f], n), ALU.mult))
        for t in range(TT):
            m = dve.mark(dve.after(m).tensor_tensor(d[:, t], d[:, t], gain(g, n), ALU.mult))
    dve.after(m, angles_ready)

    def rope(dst, x, heads):
        R = ROPE // 2
        c, s = (v.broadcast_to([P, TT, heads, R]) if heads == 1 else v for v in (cos2, sin2))
        a, b = (v[:, :, 0:heads, :] for v in ropet)
        lo, hi = x[:, :, :, 0:R], x[:, :, :, R:]
        def mul(d, u, v):
            for t in range(TT):
                m = dve.mark(dve.eng.tensor_tensor(d[:, t], u[:, t], v[:, t].broadcast_to([P, heads, R]), ALU.mult))
            return m
        mul(a, lo, cos2)
        m = mul(b, hi, sin2)
        m1 = dve.mark(dve.after(m).tensor_tensor(a, a, b, ALU.subtract))
        dve.after(m1)
        m = mul(b, hi, cos2)
        x2 = rope_c[:, :, 0:heads, :]
        m = mul(x2, lo, sin2)
        m = dve.mark(dve.after(m).tensor_tensor(b, b, x2, ALU.add))
        dve.after(m)
        dve.mark(dve.eng.tensor_copy(dst[:, :, :, 0:R], a))
        m = dve.mark(dve.eng.tensor_copy(dst[:, :, :, R:], b))
        dve.after(m)
        return m

    rope_c = carve("rope_c", TT, MLA_H, ROPE // 2)
    rope(qh[:, :, :, NOPE:], qh[:, :, :, NOPE:], MLA_H)
    rope(kpe, kpe, 1)
    for t in range(TT):
        heads_ready = dve.mark(dve.eng.tensor_copy(kh[:, t, :, NOPE:], kpe[:, t].broadcast_to([P, MLA_H, ROPE])))

    mla_i = [carve(f"mla_i{j}", TT, 2, QH) for j in range(4)]
    mla_T = [carve(f"mla_T{j}", 4, P) for j in range(4)]
    mla_s = [carve(f"mla_s{j}", 3 * P) for j in range(4)]
    mla_w = [carve(f"mla_w{j}", 3 * P) for j in range(4)]
    om = tmp[:, :, 0:MLA_H * VH]
    st4 = stat[:, 112:144].rearrange("p (j n) -> p j n", j=4)
    P2c = P2
    pe.after(heads_ready)
    dve.after(heads_ready)
    with engine_loop(nc, 2, (pe, dve, act),
                     {pe: 16, dve: 40, act: 12, block_done: 4, taken[0]: 2, taken[1]: 2,
                      slot_in[0]: 16, slot_in[1]: 16}) as (i, start):
        ready, tr, sm, wm = {}, {}, {}, {}
        dve.after(start[pe], start[act])
        act.after(start[pe], start[dve])

        def staged(j):
            for t in range(TT):
                for g, x in enumerate((qh, kh)):
                    ready[j] = dve.mark(dve.eng.tensor_copy(mla_i[j][:, t, g, :],
                                                            x[:, t, bass.ds(i * 4 + j, 1), :].rearrange("p a d -> p (a d)")))

        def turned(j):
            b = bank[4 + j]
            pe.after(ready[j])
            for g in range(2):
                for t in range(TT):
                    m = pe.eng.transpose(b[0:QH, (2 * g + t) * P:(2 * g + t + 1) * P], mla_i[j][:, t, g, :], ident)
            m = pe.mark(m)
            dst, src = mla_T[j][0:QH].rearrange("p a n -> p (a n)"), b[0:QH, :]
            tr[j] = dve.mark(dve.after(m).tensor_copy(dst, src)) if j % 2 else act.mark(act.after(m).copy(dst, src))

        def scores(j):
            z, T = bank[4 + j], mla_T[j][0:QH].rearrange("p a n -> p (a n)")
            pe.after(tr[j])
            pe.eng.matmul(z[:, 0:P], lhsT=T[:, 0:P], rhs=T[:, 2 * P:3 * P], start=True, stop=True)
            m = pe.mark(pe.eng.matmul(z[:, P:3 * P], lhsT=T[:, P:2 * P], rhs=T[:, 2 * P:], start=True, stop=True))
            m = dve.mark(dve.after(m).tensor_tensor(mla_s[j], z[:, 0:3 * P], causal, ALU.add))
            for t, at_ in enumerate((slice(0, P), slice(P, 3 * P))):
                m = dve.mark(dve.after(m).tensor_reduce(st4[:, j, t:t + 1], mla_s[j][:, at_], AX, ALU.max, negate=True))
            for t, at_ in enumerate((slice(0, P), slice(P, 3 * P))):
                m = act.mark(act.after(m).activation(mla_w[j][:, at_], mla_s[j][:, at_], ACT.Exp, bias=st4[:, j, t:t + 1],
                                                     accum_out=st4[:, j, 2 + t:3 + t]))
            sm[j] = m
            dve.mark(dve.after(m).reciprocal(st4[:, j, 4:6], st4[:, j, 2:4]))

        def by_keys(j):
            b = bank[4 + j]
            pe.after(sm[j])
            for k in range(3):
                m = pe.eng.transpose(b[:, k * P:(k + 1) * P], mla_w[j][:, k * P:(k + 1) * P], ident)
            m = pe.mark(m)
            dst, src = mla_s[j], b[:, 0:3 * P]
            wm[j] = act.mark(act.after(m).copy(dst, src)) if j % 2 else dve.mark(dve.after(m).tensor_copy(dst, src))

        def weighed(j):
            o, w = bank[4 + j], mla_s[j]
            v = [KVm[:, t, bass.ds(i * (4 * P) + (j * P + NOPE), VH)] for t in range(TT)]
            pe.after(wm[j])
            pe.eng.matmul(o[:, 0:VH], lhsT=w[:, 0:P], rhs=v[0], start=True, stop=True)
            pe.eng.matmul(o[:, VH:2 * VH], lhsT=w[:, P:2 * P], rhs=v[0], start=True, stop=False)
            m = pe.mark(pe.eng.matmul(o[:, VH:2 * VH], lhsT=w[:, 2 * P:], rhs=v[1], start=False, stop=True))
            dve.after(m)
            dve.mark(dve.eng.tensor_tensor(
                om[:, :, bass.ds(i * (4 * VH) + j * VH, VH)], o[:, 0:2 * VH].rearrange("p (t d) -> p t d", t=TT),
                st4[:, j, 4:6].unsqueeze(2).broadcast_to([P, TT, VH]), ALU.mult))

        def before(b):
            for j in range(4):
                [staged, turned, scores, by_keys][b](j)

        for c in range(2):
            project(hT, KT, CW, lambda part, t, sums, done: take_copy(
                P2[:, t, bass.ds(i * (2 * CW) + (GATES + c * CW), CW)], t, sums, done),
                before=lambda b: before(2 * c + b))
        for j in range(4):
            weighed(j)
    fence()
    for q in everyone:
        q.after(*[c.now() for c in taken])

    omT = hT.rearrange("p k n -> p (k n)")[:, 0:4 * S].rearrange("p (k n) -> p k n", k=4)
    om_ready = to_features(omT, om)
    for t in range(TT):
        g = P2[:, t, GATES:]
        gates2_ready = act.mark(act.eng.activation(g, g, ACT.Sigmoid))
    fence()
    cursor[0] = block2_top
    RW = carve("RW", TT, 3 * RD + 256)
    beta, kappa = carve("beta", TT, RD), carve("kappa", TT, RD)
    arT = carve("arT", 4, 2, S)
    betaT, kappaT = carve("betaT", 4, S), carve("kappaT", 4, S)
    ldT = carve("ldT", 2, S)
    WT = carve("WT", 4, S)
    Gend = carve("Gend", 4, 4)
    temps = cursor[0]
    sg, a_, kk, kx = (carve(n, TT, RD) for n in ("sg", "a", "kk", "kx"))
    cursor[0] = mla_weights
    alpha, u0 = carve("alpha", TT, RD), carve("u0", TT, RD)
    cursor[0] = mu_at
    states = carve("states", 4, 4, RN)
    U = hT.rearrange("p k n -> p (k n)")[:, TT * RD:].rearrange("p (t n) -> p t n", t=TT)
    r_, k_, v_ = (RW[:, :, j * RD:(j + 1) * RD] for j in range(3))
    y = P2[:, :, MLA_IN:MLA_IN + RD]
    g_ = P2[:, :, MLA_IN + RD:MLA_IN + 2 * RD]
    NM = P2[:, :, MLA_IN + 2 * RD:MLA_IN + 3 * RD]
    rho = NM
    pe.after(second_loaded, ones_row_ready)
    dve.after(third_loaded)
    pool.after(third_loaded)
    for j, n in enumerate((CW, CW, CW, 256)):
        for t in range(TT):
            b = side_bank()
            at_ = slice(MLA_IN + j * CW, MLA_IN + j * CW + n)
            m = pe.eng.matmul(bank[b][:, 0:n], lhsT=shift, rhs=P2[:, t, at_], start=True, stop=(t == 0))
            if t == 1:
                m = pe.eng.matmul(bank[b][:, 0:n], lhsT=carry, rhs=P2[:, 0, at_], start=False, stop=True)
            m = pe.mark(m)
            d = RW[:, t, j * CW:j * CW + n]
            m = dve.mark(dve.after(m).tensor_tensor(d, bank[b][:, 0:n], mu[:, j * CW:j * CW + n], ALU.mult))
            bank_read[b] = [m]
            m = pool.mark(pool.after(m).tensor_tensor(d, d, P2[:, t, at_], ALU.add))
    shifted = m
    m = act.mark(act.after(shifted).activation(RW[:, :, 3 * RD:3 * RD + 64], RW[:, :, 3 * RD:3 * RD + 64], ACT.Tanh))
    m = act.mark(act.eng.activation(RW[:, :, 3 * RD + 128:], RW[:, :, 3 * RD + 128:], ACT.Sigmoid))
    m = to_features(ldT, RW[:, :, 3 * RD:], m, shifted)
    pe.after(*m)
    for t in range(TT):
        tok = slice(t * P, (t + 1) * P)
        for which, dst in ((0, sg), (1, a_)):
            rows = slice(64 * which, 64 * which + 64)
            b = side_bank()
            pe.eng.matmul(bank[b], lhsT=ldT[rows, 0, tok], rhs=lora[rows, :], start=True, stop=False)
            m = pe.mark(pe.eng.matmul(bank[b], lhsT=ones_row[0:1, :], rhs=base_rows[0:1, which, :], start=False, stop=True))
            low_ready = act.mark(act.after(m).activation(dst[:, t, :], bank[b], ACT.Sigmoid))
            bank_read[b] = [low_ready]
        b = side_bank()
        m = pe.mark(pe.eng.matmul(bank[b], lhsT=ldT[:, 1, tok], rhs=w_gate, start=True, stop=True))
        bank_read[b] = [act.mark(act.after(m).copy(g_[:, t, :], bank[b]))]

    def both(v):
        return v.unsqueeze(1).broadcast_to([P, TT, RD])

    def by_head(x):
        return x.rearrange("p t (h d) -> p t h d", h=RH)

    def tt(q, out_, x, z, op, *after):
        return q.mark(q.after(*after).tensor_tensor(out_, x, z, op))

    m = tt(dve, kk, k_, both(vec["k_k_2"]), ALU.mult, shifted)
    m = act.mark(act.after(m).activation(alpha, kk, ACT.Square))
    ks = stat[:, 64:80]
    m = dve.mark(dve.after(m).tensor_reduce(ks.rearrange("p (t h) -> p t h", t=TT), by_head(alpha), AX, ALU.add))
    m = act.mark(act.after(m).activation(ks, ks, ACT.Sqrt))
    m = dve.mark(dve.after(m).tensor_scalar(ks, ks, 1e-12, None, ALU.max))
    m = dve.mark(dve.after(m).reciprocal(ks, ks))
    ksv = ks.rearrange("p (t h) -> p t h", t=TT)
    kk_ready = tt(dve, by_head(kk), by_head(kk), ksv.unsqueeze(3).broadcast_to([P, TT, RH, RN]), ALU.mult, m)
    m = dve.mark(dve.after(low_ready).scalar_tensor_tensor(kx, a_, -1.0, both(vec["k_a_2"]), ALU.add, ALU.mult))
    kx_ready = dve.mark(dve.after(m).scalar_tensor_tensor(kx, kx, 1.0, k_, ALU.add, ALU.mult))
    m = tt(pool, y, r_, kx, ALU.mult, kx_ready)
    m = tt(pool, y, y, both(vec["r_k_2"]), ALU.mult, m)
    bonus = stat[:, 80:96]
    bonus_ready = dve.mark(dve.after(m).tensor_reduce(bonus.rearrange("p (t h) -> p t h", t=TT), by_head(y), AX, ALU.add))
    for t in range(TT):
        b = side_bank(low_ready)
        m = pe.mark(pe.eng.matmul(bank[b], lhsT=upto, rhs=sg[:, t, :], start=True, stop=True))
        act.mark(act.after(m).activation(rho[:, t, :], bank[b], ACT.Exp))
        e1 = act.mark(act.eng.activation(beta[:, t, :], bank[b], ACT.Exp, scale=-1.0))
        bank_read[b] = [e1]
        b = side_bank()
        m = pe.mark(pe.eng.matmul(bank[b], lhsT=below, rhs=sg[:, t, :], start=True, stop=True))
        e2 = act.mark(act.after(m, kk_ready).activation(alpha[:, t, :], bank[b], ACT.Exp))
        bank_read[b] = [e2]
    b = side_bank()
    for p in range(4):
        for t in range(TT):
            m = pe.eng.matmul(bank[b][:, 4 * p + 2 * t:4 * p + 2 * t + 2], lhsT=sg[:, t, p * P:(p + 1) * P], rhs=ends,
                              start=True, stop=True)
    m = pe.mark(m)
    gend_ready = act.mark(act.after(m).activation(Gend.rearrange("p a c -> p (a c)"), bank[b][:, 0:16], ACT.Exp))
    bank_read[b] = [gend_ready]
    a_ready = tt(dve, alpha, alpha, kk, ALU.mult, e2, kk_ready)
    r_ready = tt(dve, rho, rho, r_, ALU.mult)
    k_ready = tt(pool, kappa, kx, beta, ALU.mult, e1, kx_ready)
    m = tt(dve, a_, a_, kk, ALU.mult)
    b_ready = tt(dve, beta, beta, a_, ALU.mult, m, k_ready)
    f1 = to_features(arT[:, :, 0, :], alpha, a_ready)
    f2 = to_features(arT[:, :, 1, :], rho, r_ready)
    f3 = to_features(kappaT, kappa, k_ready)
    f4 = to_features(betaT, beta, b_ready)
    fence()
    cursor[0] = temps
    AT, BT, D1, D2, XI, YI, T1_ = (carve(n, TT, RH, RN) for n in ("AT", "BT", "D1", "D2", "XI", "YI", "T1_"))
    HALF = [slice(0, 64), slice(64, 128)]
    odds = [range(q, RH, 2) for q in range(2)]

    def mask(v, n=RH):
        return v.unsqueeze(1).broadcast_to([P, n, RN])

    def chunk(t, cp):
        return slice((2 * t + cp) * RN, (2 * t + cp + 1) * RN)

    for t in range(TT):
        for src, lt_, le_ in ((betaT, AT, D1), (kappaT, BT, D2)):
            for q in range(2):
                b = side_bank()
                for h in odds[q]:
                    for cp in range(2):
                        o = bank[b][HALF[cp], h // 2 * P:h // 2 * P + P].rearrange("p (a n) -> p a n", a=2)
                        m = pe.eng.matmul(o, lhsT=src[HALF[q], h // 2, chunk(t, cp)],
                                          rhs=arT[HALF[q], h // 2, :, chunk(t, cp)], start=True, stop=True)
                m = pe.mark(m)
                o = bank[b].rearrange("p (h a n) -> p h a n", h=4, a=2)
                dve.mark(dve.after(m).tensor_tensor(lt_[:, t, q:RH:2, :], o[:, :, 0, :], mask(strict, 4), ALU.mult))
                m = dve.mark(dve.eng.tensor_tensor(le_[:, t, q:RH:2, :], o[:, :, 1, :], mask(incl, 4), ALU.mult))
                bank_read[b] = [m]
        for q in range(2):
            b = side_bank()
            for h in odds[q]:
                for cp in range(2):
                    m = pe.eng.matmul(bank[b][HALF[cp], h // 2 * RN:(h // 2 + 1) * RN],
                                      lhsT=arT[HALF[q], h // 2, 0, chunk(t, cp)],
                                      rhs=betaT[HALF[q], h // 2, chunk(t, cp)], start=True, stop=True)
            m = pe.mark(m)
            m = dve.mark(dve.after(m).tensor_tensor(XI[:, t, q:RH:2, :], bank[b][:, 0:4 * RN].rearrange("p (h n) -> p h n", h=4),
                                                    mask(a0, 4), ALU.mult))
            bank_read[b] = [m]
        dve.mark(dve.after(m).tensor_tensor(XI[:, t], XI[:, t], mask(id64), ALU.add))
        m = dve.mark(dve.eng.tensor_tensor(YI[:, t], AT[:, t], mask(levels[:, 0:RN]), ALU.mult))
        m = dve.mark(dve.after(m).tensor_tensor(YI[:, t], YI[:, t], mask(id64), ALU.add))
    NMv = NM.rearrange("p t (h n) -> p t h n", h=RH)
    with engine_loop(nc, 5, (pe, dve, act), {pe: 4, dve: 6, act: 2}) as (i, start):
        dve.after(start[pe], start[dve])
        lev = levels[:, bass.ds(i * RN + RN, RN)]
        nm = [dve.mark(dve.eng.tensor_tensor(NMv[:, t], AT[:, t], mask(lev), ALU.mult)) for t in range(TT)]
        pe.after(start[dve], start[act])
        act.after(start[pe])

        def carry_wait(t):
            pe.eng.matmul(bank[6 + t][:, 0:P], lhsT=ident, rhs=ident, start=True, stop=True)

        t1 = []
        for t in range(TT):
            pe.after(nm[t])
            carry_wait(t)
            for h in range(RH):
                for rows in HALF:
                    m = pe.eng.matmul(bank[4 + t][rows, h * RN:(h + 1) * RN], lhsT=NMv[rows, t, h, :],
                                      rhs=XI[rows, t, h, :], start=True, stop=True)
            m = pe.mark(m)
            t1.append(act.mark(act.after(m).copy(T1_[:, t].rearrange("p h n -> p (h n)"), bank[4 + t])))
        for t in range(TT):
            pe.after(t1[t])
            carry_wait(t)
            for h in range(RH):
                for rows in HALF:
                    at_ = slice(h * RN, (h + 1) * RN)
                    pe.eng.matmul(bank[t][rows, at_], lhsT=YI[rows, t, h, :], rhs=T1_[rows, t, h, :], start=True, stop=True)
                    m = pe.eng.matmul(bank[2 + t][rows, at_], lhsT=T1_[rows, t, h, :], rhs=YI[rows, t, h, :], start=True, stop=True)
            m = pe.mark(m)
            for dst, b in ((XI, t), (YI, 2 + t)):
                d = dst[:, t].rearrange("p h n -> p (h n)")
                dve.mark(dve.after(m).tensor_tensor(d, d, bank[b], ALU.add))
    fence()

    side[0] = 0
    vh = v_.rearrange("p t (h n) -> p t h n", h=RH)
    for t in range(TT):
        b = side_bank()
        for h in range(RH):
            for rows in HALF:
                m = pe.eng.matmul(bank[b][rows, h * RN:(h + 1) * RN], lhsT=BT[rows, t, h, :], rhs=vh[rows, t, h, :],
                                  start=True, stop=True)
        m = pe.mark(m)
        bv_ready = act.mark(act.after(m).copy(T1_[:, t].rearrange("p h n -> p (h n)"), bank[b]))
        bank_read[b] = [bv_ready]
        for cp in range(2):
            b = side_bank()
            for h in range(RH):
                m = pe.eng.matmul(bank[b][HALF[h % 2], h // 2 * RN:(h // 2 + 1) * RN],
                                  lhsT=alpha[HALF[cp], t, h * RN:(h + 1) * RN], rhs=YI[HALF[cp], t, h, :],
                                  start=True, stop=True)
            m = pe.mark(m)
            w_ready = dve.mark(dve.after(m).tensor_copy(WT[:, :, chunk(t, cp)],
                                                        bank[b][:, 0:4 * RN].rearrange("p (a n) -> p a n", a=4)))
            bank_read[b] = [w_ready]
        b = side_bank(bv_ready)
        for h in range(RH):
            for rows in HALF:
                m = pe.eng.matmul(bank[b][rows, h * RN:(h + 1) * RN], lhsT=YI[rows, t, h, :], rhs=T1_[rows, t, h, :],
                                  start=True, stop=True)
        m = pe.mark(m)
        u_ready = act.mark(act.after(m).mul(u0[:, t, :], bank[b], -1.0))
        bank_read[b] = [u_ready]
    dve.after(u_ready)
    pe.after(w_ready)
    st_ready = dve.mark(dve.eng.memset(states[:, 0], 0.0))
    for c in range(4):
        t, rows = c // 2, HALF[c % 2]
        for q in range(2):
            b = side_bank(st_ready)
            for h in odds[q]:
                m = pe.eng.matmul(bank[b][rows, h // 2 * RN:(h // 2 + 1) * RN], lhsT=WT[HALF[q], h // 2, chunk(t, c % 2)],
                                  rhs=states[HALF[q], c, h // 2, :], start=True, stop=True)
            m = pe.mark(m)
            uq, u0q = (x[rows, t, :].rearrange("p (h n) -> p h n", h=RH)[:, q:RH:2, :] for x in (U, u0))
            m = dve.mark(dve.after(m).tensor_tensor(uq, u0q, bank[b][rows, 0:4 * RN].rearrange("p (h n) -> p h n", h=4),
                                                    ALU.subtract))
            bank_read[b] = [m]
        us_ready = m
        if c == 3:
            break
        b = side_bank(us_ready)
        for h in range(RH):
            o = bank[b][HALF[h % 2], h // 2 * RN:(h // 2 + 1) * RN]
            at_ = slice(h * RN, (h + 1) * RN)
            pe.eng.matmul(o, lhsT=kappa[rows, t, at_], rhs=v_[rows, t, at_], start=True, stop=False)
            m = pe.eng.matmul(o, lhsT=beta[rows, t, at_], rhs=U[rows, t, at_], start=False, stop=True)
        m = pe.mark(m)
        by_pair = bank[b][:, 0:4 * RN].rearrange("p (a n) -> p a n", a=4)
        m = dve.mark(dve.after(m).tensor_tensor(states[:, c + 1], by_pair, states[:, c], ALU.add))
        bank_read[b] = [m]
        st_ready = dve.mark(dve.after(m).tensor_tensor(states[:, c + 1], states[:, c + 1],
                                                       Gend[:, :, c:c + 1].broadcast_to([P, 4, RN]), ALU.mult))
    yh = by_head(y)
    y_marks = []
    for t in range(TT):
        b = side_bank(us_ready, st_ready)
        for h in range(RH):
            for rows in HALF:
                at_ = slice(h * RN, (h + 1) * RN)
                pe.eng.matmul(bank[b][rows, at_], lhsT=D1[rows, t, h, :], rhs=U[rows, t, at_], start=True, stop=False)
                m = pe.eng.matmul(bank[b][rows, at_], lhsT=D2[rows, t, h, :], rhs=v_[rows, t, at_], start=False, stop=True)
        m = pe.mark(m)
        y_ready = act.mark(act.after(m, bonus_ready).copy(y[:, t, :], bank[b]))
        bank_read[b] = [y_ready]
        for q in range(2):
            b = side_bank()
            for h in odds[q]:
                for cp in range(2):
                    m = pe.eng.matmul(bank[b][HALF[cp], h // 2 * RN:(h // 2 + 1) * RN],
                                      lhsT=arT[HALF[q], h // 2, 1, chunk(t, cp)],
                                      rhs=states[HALF[q], 2 * t + cp, h // 2, :], start=True, stop=True)
            m = pe.mark(m)
            yq = yh[:, t, q:RH:2, :]
            m = dve.mark(dve.after(m, y_ready).tensor_tensor(yq, yq, bank[b][:, 0:4 * RN].rearrange("p (h n) -> p h n", h=4),
                                                             ALU.add))
            bank_read[b] = [m]
            y_marks.append(m)
    ys = stat[:, 96:112]
    ysv = ys.rearrange("p (t h) -> p t h", t=TT)
    cursor[0] = temps
    fence()
    ysq = carve("ysq", TT, RD)

    def each(v):
        return v.unsqueeze(3).broadcast_to([P, TT, RH, RN])

    m = dve.mark(dve.after(*y_marks).tensor_reduce(ysv, yh, AX, ALU.add))
    m = dve.mark(dve.after(m).tensor_scalar(ys, ys, -1.0 / RN, None, ALU.mult))
    yc = tt(dve, yh, yh, each(ysv), ALU.add, m)
    m = act.mark(act.after(yc).activation(ysq, y, ACT.Square))
    m = dve.mark(dve.after(m).tensor_reduce(ysv, by_head(ysq), AX, ALU.add))
    m = rstd(ys, ys, RN, 2, m)
    m = tt(dve, yh, yh, each(ysv), ALU.mult, m)
    m = tt(dve, y, y, both(vec["ln_x_w_2"]), ALU.mult, m)
    m = tt(dve, y, y, both(vec["ln_x_b_2"]), ALU.add, m)
    m2 = tt(pool, by_head(v_), by_head(v_), each(bonus.rearrange("p (t h) -> p t h", t=TT)), ALU.mult, bonus_ready)
    m = tt(dve, y, y, v_, ALU.add, m, m2)
    m = tt(dve, y, y, g_, ALU.mult, m)
    fence()
    cursor[0] = block2_top
    yT, merged, aside = carve("yT", 4, S), carve("merged", TT, D), carve("aside2", TT, D)
    y_ready = to_features(yT, y)
    gates2 = [lambda t, at, g=g: P2[:, t, GATES + g * D + at.start:GATES + g * D + at.stop] for g in range(2)]
    pe.after(*om_ready)
    project(omT, 4, CW, take_gated(gates2[0], merged, aside, False, gates2_ready), parts=2)
    act.after(last["merged"])
    pe.after(*y_ready)
    project(yT, 4, CW, take_gated(gates2[1], merged, aside, True, gates2_ready), parts=2)
    pe.after(*to_features(hT, merged, last["merged"]))
    dve.after(second_loaded)
    for c in range(2):
        take = take_residual(aside, gt)
        project(hT, KT, CW, lambda part, t, sums, done: take(c, t, sums, done))
    fence()
    for q in everyone:
        q.after(*[c.now() for c in taken])
    cursor[0] = persistent_top
    down_tile = [slot[0][:, j * D:(j + 1) * D] for j in range(4)]
    up_tile = [slot[1][:, j * D:(j + 1) * D] for j in range(4)]
    x_saved = load(I["x_dram"].rearrange("(t p) d -> p t d", p=P), X, x_out, act)
    cursor[0] = lasting_top
    hot1, hot2 = ([carve(f"{n}{j}", 4, P) for j in range(2)] for n in ("hot1_", "hot2_"))
    cursor[0] = lasting_top
    dT_low = [carve(f"dT_low{j}", KT, P) for j in range(2)]
    dT_high = [carve(f"dT_high{j}", KT, P) for j in range(2)]
    up_hi = [carve(f"up_high{j}", D) for j in range(2)]
    hT_high = carve("hT_high", KT, S)
    gl = [carve(f"gl{j}", S) for j in range(2)]
    sel_at = cursor[0]
    A_high, A_low = ([carve(f"{n}{j}", S) for j in range(2)] for n in ("A_high", "A_low"))
    cursor[0] = sel_at
    selT = carve("selT", 3, S)
    iota = carve("iota_keys", P)
    coeff_at = max(cursor[0], sel_at + 4 * 4 * S)
    cursor[0] = hT_at
    hT_low = carve("hT_low", KT, S)
    cursor[0] = slot_at + 4 * KT * CW
    up_low = [carve(f"up_low{j}", D) for j in range(4)]
    cursor[0] = coeff_at
    C = carve("C", N_KEYS, S)
    assert coeff_at >= persistent_top
    cursor[0] = coeff_at
    keys, keysT = carve("keys", 2, P), carve("keysT", 2, P)
    load(keys[:, 0, :], I["sub_keys1_2"][0], peer_in, act)
    load(keys[:, 1, :], I["sub_keys2_2"][0], peer_in, act)
    peer_loaded = load(iota, table("iota"), peer_in, act)
    qT, sc = carve("qT", 2 * PEER_H, S), carve("sc", TT * PEER_H, 2, N_KEYS)
    tmp = carve("peer_tmp", TT, D)
    keys_ready = transposes(lambda g, n: keysT, [keys[:, 0, :], keys[:, 1, :]], [peer_loaded], size=2)
    h_ready = features(tmp, modT[:, 7, :], modT[:, 3, :])

    pe.after(*h_ready, *keys_ready)
    scv = sc.rearrange("p (t h) a n -> p t h a n", t=TT)
    for c in range(4):
        j, arrived = next_chunk()
        w = slot_view(j, KT, CW)
        q_ready = []
        for t in range(2):
            sums = open_block(t, arrived).rearrange("p (a n) -> p a n", a=2)
            for a in range(2):
                for k in range(KT):
                    mm = pe.eng.matmul(sums[:, a, :], lhsT=w[:, k, (2 * t + a) * P:(2 * t + a + 1) * P], rhs=hT[:, k, :],
                                       start=(k == 0), stop=(k == KT - 1))
            q_ready.append(take_copy(qT[:, 4 * c + 2 * t:4 * c + 2 * t + 2, :], t, sums, block_done.mark(mm)))
        for t in range(TT):
            b = side_bank(*q_ready)
            o = bank[b].rearrange("p (h a n) -> p h a n", h=2, a=2)
            for h in range(2):
                for a in range(2):
                    m = pe.eng.matmul(o[:, h, a, :], lhsT=qT[:, 4 * c + 2 * h + a, t * P:(t + 1) * P],
                                      rhs=keysT[:, a, :], start=True, stop=True)
            m = pe.mark(m)
            sc_ready = act.mark(act.after(m).copy(scv[:, t, 2 * c:2 * c + 2], o))
            bank_read[b] = [sc_ready]


    def load_tile(j, row):
        exp_in[j].mark(sp.eng.dma_start(down_tile[j], I["expert_down_2"][0][bass.ds(row, P), :]))
        exp_in[j].mark(sp.eng.dma_start(up_tile[j], I["expert_up_2"][0][bass.ds(row, P), :]))

    sp.after(block_done.now())
    for j in range(4):
        load_tile(j, j * P)
    with engine_loop(nc, N_KEYS // 4 - 1, (sp,), {c: 32 for c in exp_in}) as (i, _):
        for j in range(4):
            sp.after(Mark(tile_done.sem, j + 1, i, 4))
            load_tile(j, i * (4 * P) + (4 + j) * P)

    TH = TT * PEER_H
    HALVES, PAIRS = 4, 2
    s_now, s_rest = carve("s_now", HALVES, N_KEYS), carve("s_rest", HALVES, N_KEYS)
    best, which = carve("best", HALVES, TOPK), carve("which", HALVES, TOPK, dt=U32)
    cand, cand_rest = carve("cand", PAIRS, TOPK, TOPK), carve("cand_rest", PAIRS, TOPK * TOPK)
    best_sum, which_sum = carve("best_sum", PAIRS, TOPK), carve("which_sum", PAIRS, TOPK, dt=U32)
    top_v, top_at = carve("top_v", TH, TOPK), carve("top_at", TH, TOPK, dt=U32)
    top_key = carve("top_key", TH, 2, TOPK, dt=U32)
    dve.after(sc_ready)
    with engine_loop(nc, TH // PAIRS, (dve,), {dve: 12}) as (i, start):
        def then(m):
            dve.after(dve.mark(m)).memset(stat[:, 190:191], 0.0)

        def sixteen(rows, values, v, at, rest):
            for r in rows:
                m = dve.eng.max(v[:, r, 0:8], values[:, r])
            then(m)
            for r in rows:
                dve.eng.max_index(at[:, r, 0:8], v[:, r, 0:8], values[:, r])
                m = dve.eng.match_replace(rest[:, r], v[:, r, 0:8], values[:, r], -3e38)
            then(m)
            for r in rows:
                m = dve.eng.max(v[:, r, 8:16], rest[:, r])
            then(m)
            for r in rows:
                m = dve.eng.max_index(at[:, r, 8:16], v[:, r, 8:16], rest[:, r])
            then(m)

        pairs = bass.ds(i * PAIRS, PAIRS)
        dve.after(start[dve])
        then(dve.eng.tensor_copy(s_now, sc[:, pairs, :, :].rearrange("p o a n -> p (o a) n")))
        sixteen(range(HALVES), s_now, best, which, s_rest)
        b4 = best.rearrange("p (o a) k -> p o a k", a=2)
        then(dve.eng.tensor_tensor(cand, b4[:, :, 0, :].unsqueeze(3).broadcast_to([P, PAIRS, TOPK, TOPK]),
                                   b4[:, :, 1, :].unsqueeze(2).broadcast_to([P, PAIRS, TOPK, TOPK]), ALU.add))
        sixteen(range(PAIRS), cand.rearrange("p o a b -> p o (a b)"), best_sum, which_sum, cand_rest)
        dve.eng.tensor_copy(top_v[:, pairs, :], best_sum)
        dve.eng.tensor_copy(top_key[:, pairs, :, :].rearrange("p o a k -> p (o a) k"), which)
        dve.mark(dve.eng.tensor_copy(top_at[:, pairs, :], which_sum))
        dve.mark(dve.after(dve.now()).memset(stat[:, 190:191], 0.0))
    dve.after(dve.now())
    gates = carve("gates", TH, TOPK)
    norm = carve("norm", TH)
    rank_u, rank = carve("rank_u", 2, TH, TOPK, dt=U32), carve("rank", 2, TH, TOPK)
    key_of = carve("key_of", 2, TH, TOPK)
    sel_key = carve("sel_key", 2, TH, TOPK)
    eq = [carve(f"eq{j}", TH, TOPK, TOPK) for j in range(2)]
    m = dve.mark(dve.eng.tensor_tensor(gates, top_v, top_v[:, :, 0:1].broadcast_to([P, TH, TOPK]), ALU.subtract))
    exp_ready = act.mark(act.after(m).activation(gates, gates, ACT.Exp))
    dve.mark(dve.eng.tensor_scalar(rank_u[:, 0], top_at, 4, None, ALU.logical_shift_right))
    m = dve.mark(dve.eng.tensor_scalar(rank_u[:, 1], top_at, 15, None, ALU.bitwise_and))
    dve.after(m)
    rank_ready = dve.mark(dve.eng.tensor_copy(rank, rank_u))
    for a in range(2):
        key_ready = dve.mark(dve.eng.tensor_copy(key_of[:, a], top_key[:, :, a, :]))
    m = dve.mark(dve.after(exp_ready).tensor_reduce(norm, gates, AX, ALU.add))
    m = dve.mark(dve.after(m).reciprocal(norm, norm))
    gates_ready = dve.mark(dve.after(m).tensor_tensor(gates, gates, norm.unsqueeze(2).broadcast_to([P, TH, TOPK]), ALU.mult))
    ranks = iota[:, 0:TOPK].unsqueeze(1).unsqueeze(1).broadcast_to([P, TH, TOPK, TOPK])
    sel_ready = []
    for a in range(2):
        q = (dve, pool)[a]
        dve.after(rank_ready, key_ready)
        m = dve.mark(dve.eng.tensor_tensor(eq[a], ranks, rank[:, a].unsqueeze(3).broadcast_to([P, TH, TOPK, TOPK]), ALU.is_equal))
        m = q.mark(q.after(m).tensor_tensor(eq[a], eq[a], key_of[:, a].unsqueeze(2).broadcast_to([P, TH, TOPK, TOPK]), ALU.mult))
        sel_ready.append(dve.mark(dve.after(m).tensor_reduce(sel_key[:, a], eq[a], AX, ALU.add)))
    sources = [x.rearrange("p (t h) k -> p t (h k)", t=TT) for x in (sel_key[:, 0], sel_key[:, 1], gates)]
    sel_marks = []
    for v in range(3):
        sel_marks += transposes(lambda g, n: selT[:, v, :].rearrange("p (t n) -> p t n", t=TT),
                                [sources[v][:, t, :] for t in range(TT)], [gates_ready] + sel_ready, size=2)
    fence()

    iota4 = iota.unsqueeze(1).broadcast_to([P, 4, P])
    with engine_loop(nc, S // 8, (pe, dve, act), {pe: 2, dve: 2, act: 2}) as (i, start):
        def earlier(q, u):
            return Mark(q.sem, start[q].base - 1 + u, i, 2)

        for u in range(2):
            tok = [i * 8 + 4 * u + n for n in range(4)]
            dve.after(earlier(pe, u))
            for n in range(4):
                dve.eng.tensor_scalar(hot1[u][:, n, :], iota, selT[:, 0, bass.ds(tok[n], 1)],
                                           selT[:, 2, bass.ds(tok[n], 1)], ALU.is_equal, ALU.mult)
            hot = dve.mark(dve.eng.tensor_tensor(
                hot2[u], iota4, selT[:, 1, bass.ds(tok[0], 4)].unsqueeze(2).broadcast_to([P, 4, P]), ALU.is_equal))
            pe.after(hot, earlier(act, u))
            for n in range(4):
                m = pe.eng.matmul(bank[4 + u][:, n * P:(n + 1) * P], lhsT=hot2[u][:, n, :], rhs=hot1[u][:, n, :],
                                  start=True, stop=True)
            m = pe.mark(m)
            act.mark(act.after(m).copy(C[:, :, bass.ds(tok[0], 4)].rearrange("p a n -> p n a"),
                                       bank[4 + u].rearrange("p (n a) -> p n a", n=4)))
    fence()

    def of(count, a, i, n=1):
        return Mark(count.sem, n * (a + 1), i, 4 * n) if i is not None else Mark(count.sem, n * (a + 1))

    def high(q, dst, src):
        dst = dst.bitcast(F32R)
        return q.eng.copy(dst, src) if q is act else q.eng.tensor_copy(dst, src)

    def low(q, dst, src, high_part):
        return q.eng.tensor_tensor(dst.bitcast(F32R), src, high_part, ALU.subtract)

    def three(o, lhs, lhs_high, rhs, rhs_high, start, stop):
        pe.eng.matmul(o, lhsT=lhs_high.bitcast(F32R), rhs=rhs_high.bitcast(F32R), start=start, stop=False,
                      skip_group_check=True)
        pe.eng.matmul(o, lhsT=lhs_high.bitcast(F32R), rhs=rhs.bitcast(F32R), start=False, stop=False,
                      skip_group_check=True)
        return pe.eng.matmul(o, lhsT=lhs.bitcast(F32R), rhs=rhs_high.bitcast(F32R), start=False, stop=stop,
                             skip_group_check=True)

    def arrived(a, i):
        return Mark(exp_in[a % 4].sem, 32 * (a // 4 + 1), i, 32)

    def turn(a, i):
        pe.after(arrived(a, i))
        if a > 1:
            act.after(of(down_done, a - 2, i))
        for g in range(2):
            if a > 0:
                pe.after(Mark(down_low.sem, 2 * a - 1 + g, i, 8))
            for k in range(4):
                m = pe.eng.transpose(bank[4 + g][:, k * P:(k + 1) * P],
                                     down_tile[a % 4][:, (4 * g + k) * P:(4 * g + k + 1) * P], ident)
            turned_done.mark(m)
            ks, src = slice(4 * g, 4 * g + 4), bank[4 + g].rearrange("p (k n) -> p k n", k=4)
            act.after(Mark(turned_done.sem, 2 * a + g + 1, i, 8))
            down_high.mark(high(act, dT_high[a % 2][:, ks, :], src))
            dve.after(Mark(down_high.sem, 2 * a + g + 1, i, 8))
            down_low.mark(low(dve, dT_low[a % 2][:, ks, :], src, dT_high[a % 2][:, ks, :]))

    def split_up(a, i):
        dve.after(arrived(a, i))
        if a > 1:
            dve.after(of(tile_done, a - 2, i))
        up_high.mark(high(dve, up_hi[a % 2], up_tile[a % 4]))
        pool.after(of(up_high, a, i))
        up_split.mark(low(pool, up_low[a % 4], up_tile[a % 4], up_hi[a % 2]))

    def down(a, i):
        b = bank[6 + a % 2][:, 0:S]
        pe.after(of(down_low, a, i, 2))
        if a > 1:
            pe.after(of(gelu_done, a - 2, i))
        for k in range(KT):
            m = three(b, dT_low[a % 2][:, k, :], dT_high[a % 2][:, k, :], hT_low[:, k, :], hT_high[:, k, :],
                      k == 0, k == KT - 1)
        down_done.mark(m)
        act.after(of(down_done, a, i))
        if a > 1:
            act.after(of(weighed_done, a - 2, i))
        gelu_done.mark(act.eng.activation(gl[a % 2], b, ACT.Gelu_apprx_tanh))
        at = a if i is None else i * 4 + a
        dve.after(of(gelu_done, a, i))
        if a > 1:
            dve.after(of(tile_done, a - 2, i))
        m = dve.mark(dve.eng.tensor_tensor(gl[a % 2].unsqueeze(1), gl[a % 2].unsqueeze(1), C[:, bass.ds(at, 1), :], ALU.mult))
        dve.after(m)
        m = dve.mark(high(dve, A_high[a % 2], gl[a % 2]))
        dve.after(m)
        weighed_done.mark(low(dve, A_low[a % 2], gl[a % 2], A_high[a % 2]))

    def up(a, i, stop=False):
        pe.after(of(weighed_done, a, i), of(up_split, a, i))
        for t in range(TT):
            for half in range(2):
                at = slice(half * CW, (half + 1) * CW)
                m = three(bank[2 * t + half], A_low[a % 2][:, t * P:(t + 1) * P], A_high[a % 2][:, t * P:(t + 1) * P],
                          up_low[a % 4][:, at], up_hi[a % 2][:, at], a == 0, stop)
        tile_done.mark(m)

    m = dve.mark(high(dve, hT_high, hT))
    dve.after(m)
    pe.after(dve.mark(low(dve, hT_low, hT, hT_high)))
    turn(0, None)
    turn(1, None)
    split_up(0, None)
    down(0, None)

    def tile_steps(a, i=None):
        if a + 2 < N_KEYS:
            turn(a + 2, i)
        if a + 1 < N_KEYS:
            split_up(a + 1, i)
            down(a + 1, i)
        up(a, i, a == N_KEYS - 1)

    for a in range(4):
        tile_steps(a)
    TURNS = N_KEYS // 4 - 2
    per_tile = {c: 4 for c in (up_high, up_split, down_done, gelu_done, weighed_done, tile_done)}
    with engine_loop(nc, TURNS, (pe, dve, act, pool), {turned_done: 8, down_high: 8, down_low: 8, dve: 8, **per_tile}) as (i, _):
        for a in range(4, 8):
            tile_steps(a, i)
    for a in range(4 * TURNS + 4, N_KEYS):
        tile_steps(a)

    cursor[0] = coeff_at
    X_back, gt_back, scaled = carve("X_back", TT, D), carve("gt_back", D), carve("scaled", TT, D)
    sp.after(x_saved, Mark(weighed_done.sem, N_KEYS // 2))
    load(X_back, I["x_dram"].rearrange("(t p) d -> p t d", p=P), x_in)
    x_back = load(gt_back, mod_dram[0, 5 * D:6 * D].partition_broadcast(P), x_in)
    dve.after(Mark(tile_done.sem, N_KEYS), x_back)
    for t in range(TT):
        for half in range(2):
            at = slice(half * CW, (half + 1) * CW)
            m = dve.mark(dve.eng.tensor_tensor(scaled[:, t, at], bank[2 * t + half], gt_back[:, at], ALU.mult))
            m = dve.mark(dve.after(m).tensor_tensor(scaled[:, t, at], scaled[:, t, at], X_back[:, t, at], ALU.add))
            sp.after(m)
            stored = out_done.mark(sp.eng.dma_start(out[0, t * P:(t + 1) * P, at], scaled[:, t, at]))
    sp.after(stored)


def kernel(**inputs):
    import concourse.bacc as bacc
    from concourse.bass_utils import run_bass_kernel_spmd

    nc = bacc.Bacc("TRN2", target_bir_lowering=False, num_devices=1)
    arrays, I = {}, {}

    def give(name, a):
        arrays[f"in_{name}_dram"] = a
        I[name] = nc.dram_tensor(f"in_{name}_dram", a.shape, mybir.dt.from_np(a.dtype), kind="ExternalInput").ap()

    for name in inputs:
        give(name, np.ascontiguousarray(inputs[name]))
    for name, tables in zip(("first", "second"), constants()):
        table, I[name + "_at"] = pack(tables)
        give(name, table)
    I["x_dram"] = nc.dram_tensor("x_dram", [S, D], F32, kind="Internal").ap()
    I["mod_dram"] = nc.dram_tensor("mod_dram", [1, 6 * D], F32, kind="Internal").ap()
    out = nc.dram_tensor("out_dram", [1, S, D], F32, kind="ExternalOutput").ap()
    build(nc, I, out)
    return run_bass_kernel_spmd(nc, [arrays], core_ids=[0]).results[0]["out_dram"]
```

```python
from contextlib import ExitStack, contextmanager

import numpy as np

import concourse.bass as bass
from concourse import mybir
from concourse.alu_op_type import AluOpType as ALU

F32 = mybir.dt.float32
I32 = mybir.dt.int32
U32 = mybir.dt.uint32
F32R = mybir.dt.float32r
ACT = mybir.ActivationFunctionType
AX = mybir.AxisListType.X

P = 128
S = 256
TT = S // P
D = 1024
KT = D // P
CW = 512
EPS = 1e-6
SB_H, SB_D = 8, 128
RET_H, RET_D, CHUNK = 4, 256, 64
MLA_H, NOPE, ROPE, VH, QH = 8, 64, 32, 64, 96
Q_LORA, KV_LORA = 256, 128
RH, RN = 8, 64
RD = RH * RN
GN_EPS = 64e-5
N_KEYS, PEER_H, TOPK = 128, 8, 16
NEG = -1e30


class Mark:

    def __init__(self, sem, base, i=None, per=0):
        self.sem, self.base, self.i, self.per = sem, base, i, per

    def value(self):
        return self.base if self.i is None else self.i * self.per + self.base


class Queue:

    name = "queue"

    def __init__(self, eng, sem):
        self.eng, self.sem, self.count = eng, sem, 0
        self.i, self.per, self.seen = None, 0, {}

    def after(self, *marks):
        for m in marks:
            if m.i is None:
                if self.seen.get(id(m.sem), 0) >= m.base:
                    continue
                if self.i is None:
                    self.seen[id(m.sem)] = m.base
            assert m.base > 0
            self.eng.wait_ge(m.sem, m.value())
        return self.eng

    def mark(self, instruction):
        instruction.then_inc(self.sem, 1)
        self.count += 1
        return self.now()

    def now(self):
        return Mark(self.sem, self.count, self.i, self.per)


class Count:

    name = "count"

    def __init__(self, sem, step=16):
        self.sem, self.step, self.count, self.i, self.per = sem, step, 0, None, 0

    def mark(self, instruction):
        instruction.then_inc(self.sem, self.step)
        self.count += self.step
        return self.now()

    def now(self, back=0):
        assert self.count >= back * self.step
        return Mark(self.sem, self.count - back * self.step, self.i, self.per)


@contextmanager
def engine_loop(nc, n, queues, per):
    with nc.Fori(0, n, 1, engines=tuple(q.eng.engine for q in queues)) as i:
        start = {}
        for c, k in per.items():
            start[c] = c.count
            c.i, c.per = i, k
        for q in queues:
            q.i = i
        yield i, {c: Mark(c.sem, start[c], i, per[c]) for c in per}
    for c, k in per.items():
        assert c.count - start[c] == k, (c.name, c.count - start[c], k)
        c.count = start[c] + n * k
    for c in list(per) + list(queues):
        c.i, c.per = None, 0


def constants():
    r = np.arange(P)
    s, t = r[:, None], r[None, :]
    lt = (s < t).astype(np.float32)
    c = {"ident": np.eye(P), "negtri": -(s >= t).astype(np.float32), "negones": -np.ones((P, P)),
         "lt": lt, "ltbias": np.concatenate([(1 - lt) * NEG, np.zeros((P, P)), (1 - lt) * NEG], 1)}
    tok = np.arange(S, dtype=np.float32)[:, None]
    inv = np.float32(10000.0) ** (-np.arange(0, RET_D, 2, dtype=np.float32) / np.float32(RET_D))
    ang = (tok * inv[None, :]).astype(np.float32).astype(np.float64).reshape(TT, P, RET_D // 2)
    c["cos"] = np.cos(ang).transpose(1, 0, 2).reshape(P, -1)
    c["sin"] = np.sin(ang).transpose(1, 0, 2).reshape(P, -1)
    full = np.arange(S)
    dec = []
    for h in range(RET_H):
        lg = np.log1p(-2.0 ** (-5.0 - h))
        m = np.exp(lg * np.abs(full[:, None] - full[None, :])) * RET_D ** -0.5
        m = m * ((full[:, None] // CHUNK) <= (full[None, :] // CHUNK))
        dec += [m[:P, :], m[P:, P:]]
    c["decay"] = np.concatenate(dec, 1)
    first = {k: np.asarray(v, np.float32) for k, v in c.items()}
    w = np.arange(RN)[None, :]
    sl = s % RN
    rate = -np.exp(-0.5)
    same = s // RN == t // RN
    c = {"upto": rate * ((s <= t) & same), "below": rate * ((s < t) & same),
         "ends": rate * np.stack([r // RN == 0, r // RN == 1], 1),
         "shift": (s == t - 1) * 1.0 - (s == t), "carry": (s == P - 1) & (t == 0),
         "strict": sl < w, "incl": sl <= w, "id64": sl == w, "a0": -1.0 * ((sl % 2 == 1) & (w == sl - 1)),
         "levels": np.concatenate([-1.0 * (((w // n) % 2 == 1) & (sl // n == w // n - 1))
                                   for n in (1, 2, 4, 8, 16, 32)], 1)}
    causal = np.where(t <= s, 0.0, NEG)
    c["causal"] = np.concatenate([causal, np.zeros((P, P)), causal], 1)
    c["iota"] = np.broadcast_to(t * 1.0, (P, P))
    inv = np.float32(10000.0) ** (-np.arange(ROPE // 2, dtype=np.float32) / np.float32(ROPE // 2))
    c["invf"] = np.broadcast_to(inv[None, :], (P, ROPE // 2))
    second = {k: np.asarray(v, np.float32) for k, v in c.items()}
    return first, second


def pack(tables):
    at, where = 0, {}
    for k, v in tables.items():
        where[k] = (at, v.shape[1])
        at += v.shape[1]
    return np.ascontiguousarray(np.concatenate(list(tables.values()), 1)), where


def build(nc, I, out):
    with ExitStack() as ctx:
        program(nc, ctx, I, out)


def program(nc, ctx, I, out):
    def sem(name):
        return ctx.enter_context(nc.semaphore(name))

    pe, dve = Queue(nc.tensor, sem("pe_done")), Queue(nc.vector, sem("dve_done"))
    act, pool = Queue(nc.scalar, sem("act_done")), Queue(nc.gpsimd, sem("pool_done"))
    sp = Queue(nc.sync, sem("sp_unused"))
    pe.name, dve.name, act.name, pool.name = "pe", "dve", "act", "pool"
    everyone = (pe, dve, act, pool)

    def arrivals(name, step=16):
        c = Count(sem(name), step)
        c.name = name
        return c

    slot_in = [arrivals("slot0_in"), arrivals("slot1_in")]
    block_done = arrivals("block_done", 1)
    taken = [arrivals("taken_dve", 1), arrivals("taken_act", 1)]
    start_in, first_in, merge_in = arrivals("start_in"), arrivals("first_in"), arrivals("merge_in")
    second_in, third_in = arrivals("second_in"), arrivals("third_in")
    NP = 6
    ada_in = [arrivals(f"ada{a}_in") for a in range(NP)]
    mod_out = [arrivals(f"mod_out{a}") for a in range(NP)]
    mod_in = arrivals("mod_in")
    out_done = arrivals("out_done")
    peer_in, x_out, x_in = arrivals("peer_in"), arrivals("x_out"), arrivals("x_in")
    down_in, up_in = ([arrivals(f"{n}{j}_in") for j in range(4)] for n in ("down", "up"))
    turned_done, down_high, down_low, up_high, up_split_dve, up_split, down_done, gelu_done, weighed_done, tile_done = (
        arrivals(n, 1) for n in ("turned_done", "down_high", "down_low", "up_high", "up_split_dve", "up_split", "down_done",
                                 "gelu_done", "weighed_done", "tile_done"))

    cursor = [(nc.sbuf_base + 63) // 64 * 64]

    def carve(name, *shape, dt=F32):
        n = int(np.prod(shape)) * 4
        t = nc.alloc_sbuf_tensor_at(name, [P, *shape], dt, offset=cursor[0])
        cursor[0] += (n + 31) // 32 * 32
        assert cursor[0] <= nc.sbuf_usable_end, (name, cursor[0])
        return t.ap()

    bank = [ctx.enter_context(nc.psum_tensor(f"bank{b}", [P, CW], F32)).ap() for b in range(8)]

    def fence():
        marks = [q.now() for q in everyone]
        for q in everyone:
            q.after(*marks)
        return marks

    ident = carve("ident", P)
    hT_at = cursor[0]
    hT = carve("hT", KT, S)
    slot_at = cursor[0]
    slot = [carve(f"slot{j}", KT * CW) for j in range(2)]
    stat = carve("stat", 192)
    col = carve("col", 3)
    cT, cs = carve("cT", KT), carve("cs", KT)
    gain1 = carve("gain1", KT)
    modT = carve("modT", 8, KT)
    lasting_top = cursor[0]
    X = carve("X", TT, D)
    gt = carve("gt", D)
    persistent_top = cursor[0]

    def load(dst, src, count, q=sp):
        return count.mark(q.eng.dma_start(dst, src, allow_slow_non_contiguous=True))

    def table(name):
        src, where = (I["first"], I["first_at"]) if name in I["first_at"] else (I["second"], I["second_at"])
        a, n = where[name]
        return src[:, a:a + n]

    load(X, I["x"][0].rearrange("(t p) d -> p t d", p=P), start_in)
    load(ident, table("ident"), start_in)
    load(gain1, I["norm_gain"][0].rearrange("(k p) -> p k", p=P), start_in)
    start_loaded = load(cT, I["c_2"][0].rearrange("(k p) -> p k", p=P), start_in)

    sp.after(start_loaded)
    blocks_behind = [0, 0]

    def slot_view(j, k, n):
        return slot[j][:, 0:k * n].rearrange("p (k n) -> p k n", k=k)

    def load_chunk(src, c, i=None):
        j = c % 2
        if c >= 2:
            sp.after(Mark(block_done.sem, blocks_behind[c], i, 4))
        slot_in[j].mark(sp.eng.dma_start(slot_view(j, src.shape[1], src.shape[2]), src))

    def used(blocks):
        blocks_behind.append(blocks + (blocks_behind[-1] if len(blocks_behind) > 2 else 0))

    def stream(W, starts_widths, blocks=2):
        for a, n in starts_widths:
            c = len(blocks_behind) - 2
            load_chunk(W[:, a:a + n].rearrange("(k p) n -> p k n", p=P), c)
            used(blocks)

    def stream_loop(W, c0, pairs):
        c = len(blocks_behind) - 2
        with engine_loop(nc, pairs, (sp,), {slot_in[0]: 16, slot_in[1]: 16}) as (i, _):
            for j in range(2):
                load_chunk(W[:, bass.ds(i * 2 * CW + c0 + j * CW, CW)].rearrange("(k p) n -> p k n", p=P), c + j, i)
        for _ in range(2 * pairs):
            used(2)

    w_in, w_in2 = I["w_in"][0], I["w_in_2"][0]
    MLA_IN = Q_LORA + KV_LORA + ROPE
    GATES = MLA_IN + 3 * RD + 64 + 64 + 128
    stream(w_in, [(0, CW), (CW, CW)])
    stream_loop(w_in, 2 * CW, 9)
    for name in ("w_branch_sb", "w_branch_ret", "w_out"):
        stream(I[name][0], [(0, CW), (CW, CW)])
    stream(w_in2, [(0, MLA_IN), (MLA_IN, CW), (MLA_IN + CW, CW)])
    stream(w_in2, [(MLA_IN + 2 * CW, CW)], 10)
    stream(w_in2, [(MLA_IN + 3 * CW, 256)] + [(GATES + CW * j, CW) for j in range(4)])
    stream(I["w_o_mla_2"][0], [(0, D)], 4)
    stream(I["w_o_rwkv_2"][0], [(0, D)], 4)
    stream(I["w_out_2"][0], [(0, CW), (CW, CW)])
    stream(I["w_query_2"][0], [(CW * j, CW) for j in range(4)])
    for c in slot_in:
        c.count = 0

    for k, v in enumerate((1.0, EPS, GN_EPS)):
        col_ready = dve.mark(dve.eng.memset(col[:, k:k + 1], v))
    for _ in range(2):
        taken[0].mark(dve.after(dve.now()).memset(stat[:, 190:191], 0.0))
        dve.after(taken[0].now())
        taken[1].mark(act.after(col_ready).copy(stat[:, 191:192], col[:, 0:1]))
        act.after(taken[1].now())

    next_slot, next_bank = [0], [0]
    untaken = [0, 0]

    def next_chunk():
        j = next_slot[0]
        next_slot[0] = 1 - j
        slot_in[j].count += 16
        return j, slot_in[j].now()

    def open_block(t, arrived):
        b = next_bank[0]
        next_bank[0] = (b + 1) % 4
        pe.after(arrived, taken[t].now(1 - untaken[t]))
        return bank[b]

    def token_block(lhs, w, t, arrived):
        sums = open_block(t, arrived)[:, 0:w.shape[2]]
        for k in range(w.shape[1]):
            mm = pe.eng.matmul(sums, lhsT=lhs[:, k, t * P:(t + 1) * P], rhs=w[:, k, :],
                               start=(k == 0), stop=(k == w.shape[1] - 1))
        return sums, block_done.mark(mm)

    def project(lhs, kn, n, take, parts=1, before=None):
        j, arrived = next_chunk()
        w = slot_view(j, kn, n * parts)
        for part in range(parts):
            for t in range(TT):
                if before:
                    before(part * TT + t)
                take(part, t, *token_block(lhs, w[:, :, part * n:(part + 1) * n], t, arrived))

    def ahead(lhs, kn, n, parts=1):
        j, arrived = next_chunk()
        w = slot_view(j, kn, n * parts)
        blocks = []
        for part in range(parts):
            for t in range(TT):
                blocks.append((part, t, *token_block(lhs, w[:, :, part * n:(part + 1) * n], t, arrived)))
                untaken[t] += 1
        return blocks

    def take_later(take, blocks):
        for block in blocks:
            take(*block)
            untaken[block[1]] -= 1

    def take_copy(dst, t, sums, done):
        if t == 0:
            return taken[0].mark(dve.after(done).tensor_copy(dst, sums))
        return taken[1].mark(act.after(done).copy(dst, sums))

    def rstd(dst, sums, n, eps_col, *after):
        m = act.mark(act.after(*after).activation(dst, sums, ACT.Sqrt, bias=col[:, eps_col:eps_col + 1],
                                                  scale=1.0 / n))
        return dve.mark(dve.after(m).reciprocal(dst, dst))

    bank_read = {b: [] for b in range(4, 8)}

    side = [0]

    def side_bank(*ready):
        b = 4 + side[0] % 4
        side[0] += 1
        pe.after(*bank_read[b], *ready)
        return b

    def transposes(dst, tiles, ready, scale=None, bias=None, size=4):
        marks = []
        for g in range(0, len(tiles), size):
            b = 4 + (g // size) % 4
            pe.after(*ready, *bank_read[b])
            n = size
            for k in range(n):
                tr = pe.eng.transpose(bank[b][:, k * P:(k + 1) * P], tiles[g + k], ident)
            tr = pe.mark(tr)
            to, frm = dst(g, n), bank[b][:, 0:n * P].rearrange("p (k n) -> p k n", k=n)
            if scale is None:
                q = (dve, act)[(g // size) % 2]
                m = q.mark(q.after(tr).tensor_copy(to, frm) if q is dve else q.after(tr).copy(to, frm))
            else:
                m = dve.mark(dve.after(tr).tensor_tensor(to, frm, scale(g, n), ALU.mult))
            bank_read[b] = [m]
            if bias is not None:
                m = dve.mark(dve.after(m).tensor_tensor(to, to, bias(g, n), ALU.add))
            marks.append(m)
        return marks

    def features(tmp, gain, bias, *ready):
        def of(v):
            return lambda g, n: v[:, g:g + n].unsqueeze(2).broadcast_to([P, n, P])

        squared = [act.mark(act.after(*ready).activation(tmp[:, t, :], X[:, t, :], ACT.Square,
                                                         accum_out=stat[:, t:t + 1])) for t in range(TT)]
        marks = []
        for t in range(TT):
            r = rstd(stat[:, 2 + t:3 + t], stat[:, t:t + 1], D, 1, squared[t])
            m = dve.mark(dve.after(r).tensor_scalar(tmp[:, t, :], X[:, t, :], stat[:, 2 + t:3 + t], None, ALU.mult))
            marks += transposes(lambda g, n: hT[:, g:g + n, t * P:(t + 1) * P],
                                [tmp[:, t, k * P:(k + 1) * P] for k in range(KT)], [m],
                                of(gain), of(bias) if bias is not None else None)
        return marks

    P1 = carve("P1", TT, 10, D)
    Q_, K_, V_, G_, RQ, RK, RV, RG, M1, M2 = range(10)
    negtri, negones, lt = carve("negtri", P), carve("negones", P), carve("lt", P)
    ltbias = carve("ltbias", 3 * P)
    cos1, sin1 = carve("cos1", TT, P), carve("sin1", TT, P)
    decay = carve("decay", RET_H, 3 * P)
    sbgain = carve("sbgain", 2)
    work_top = cursor[0]

    h_ready = features(P1[:, :, Q_, :], gain1, None, start_loaded)
    c_ready = act.mark(act.after(start_loaded).activation(cs, cT, ACT.Silu))

    AW, PIECES = 256, ((0, 1), (2,), (3, 4), (5,))
    ada_w = [P1[:, a // 3, RQ + 2 * (a % 3):RQ + 2 * (a % 3) + 2, :].rearrange("p g d -> p (g d)")
             .rearrange("p (k n) -> p k n", k=KT) for a in range(NP)]
    ada_acc = [carve(f"ada_acc{a}", AW) for a in range(NP)]
    ada_b = [carve(f"ada_b{a}", AW) for a in range(NP)]
    mod_row = [carve(f"mod_row{a}", AW) for a in range(NP)]
    w_ada, mod_dram = I["w_ada_2"][0], I["mod_dram"]

    def load_piece(a, i):
        at = i * (NP * AW) + a * AW
        ada_in[a].mark(act.eng.dma_start(ada_w[a], w_ada[:, bass.ds(at, AW)].rearrange("(k p) n -> p k n", p=P)))
        ada_in[a].mark(act.eng.dma_start(ada_b[a][0:1, :], I["b_ada_2"][:, bass.ds(at, AW)]))

    for a in range(NP):
        load(mod_row[a][0:1, :], I["b_ada_2"][:, 0:AW], mod_out[a], act)
        load_piece(a, 0)
    for name, ap in (("negtri", negtri), ("negones", negones), ("lt", lt), ("ltbias", ltbias)):
        load(ap, table(name), first_in, act)
    for name, ap in (("cos", cos1), ("sin", sin1)):
        load(ap, table(name).rearrange("p (t n) -> p t n", t=TT), first_in, act)
    load(decay, table("decay").rearrange("p (h n) -> p h n", h=RET_H), first_in, act)
    load(sbgain[:, 0:1], I["sb_q_gain"].rearrange("a p -> p a"), first_in, act)
    first_loaded = load(sbgain[:, 1:2], I["sb_k_gain"].rearrange("a p -> p a"), first_in, act)
    P1c = P1.rearrange("p t g d -> p t (g d)")
    pe.after(*h_ready)
    dve.after(c_ready, *h_ready)
    act.after(*h_ready)

    def turn_a(i, start, load_next):
        piece_done, row_done = {}, {}

        def sum_pieces(b):
            for a in PIECES[b]:
                acc, w = ada_acc[a], ada_w[a]
                m = dve.mark(dve.after(start[ada_in[a]], start[pe]).tensor_scalar(acc, w[:, 0, :], cs[:, 0:1], None, ALU.mult))
                for k in range(1, KT):
                    m = dve.mark(dve.after(m).scalar_tensor_tensor(acc, w[:, k, :], cs[:, k:k + 1], acc,
                                                                   ALU.mult, ALU.add))
                piece_done[a] = m

        def sum_rows(b):
            for a in PIECES[b]:
                row = bank[4 + a % 2][0:1, 0:AW]
                m = pe.mark(pe.after(piece_done[a]).matmul(row, lhsT=col[:, 0:1], rhs=ada_acc[a],
                                                           start=True, stop=True))
                row_done[a] = dve.mark(dve.after(m, start[mod_out[a]]).tensor_tensor(
                    mod_row[a][0:1, :], row, ada_b[a][0:1, :], ALU.add))

        def store_rows(b):
            for a in PIECES[b]:
                act.after(row_done[a])
                mod_out[a].mark(act.eng.dma_start(mod_dram[:, bass.ds(i * (NP * AW) + a * AW, AW)],
                                                  mod_row[a][0:1, :]))
                if load_next:
                    load_piece(a, i + 1)

        for j in range(2):
            def take(part, t, sums, done):
                take_copy(P1c[:, t, bass.ds(i * (2 * CW) + j * CW, CW)], t, sums, done)
                sum_rows(2 * j + t)
                store_rows(2 * j + t)
            project(hT, KT, CW, take, before=lambda b: sum_pieces(2 * j + b))

    with engine_loop(nc, 3, (pe, dve, act),
                     {pe: 6, dve: 54, block_done: 4, taken[0]: 2, taken[1]: 2, slot_in[0]: 16, slot_in[1]: 16,
                      **{c: 32 for c in ada_in}, **{c: 16 for c in mod_out}}) as (i, start):
        turn_a(i, start, True)
    turn_a(3, {c: c.now() for c in (pe, *ada_in, *mod_out)}, False)
    mod_stored = [c.now() for c in mod_out]

    fence()
    act.after(taken[0].now(), taken[1].now())
    dve.after(taken[0].now(), taken[1].now())
    sq = P1[:, :, M1:M2 + 1, :]
    sums = stat[:, 0:32].rearrange("p (t g h) -> p t g h", t=TT, g=2)
    for t in range(TT):
        m = act.mark(act.eng.activation(sq[:, t], P1[:, t, Q_:K_ + 1, :], ACT.Square))
        m = dve.mark(dve.after(m).tensor_reduce(sums[:, t], sq[:, t].rearrange("p g (h d) -> p g h d", h=SB_H), AX, ALU.add))
    qk_rstd = rstd(stat[:, 0:32], stat[:, 0:32], SB_D, 1, m)
    gate_ready = act.mark(act.eng.activation(P1[:, :, G_, :], P1[:, :, G_, :], ACT.Silu))
    gains_ready = dve.mark(dve.after(first_loaded).tensor_scalar(sbgain[:, 0:1], sbgain[:, 0:1], SB_D ** -0.5, None, ALU.mult))

    cursor[0] = work_top
    sb_n = [carve(f"sb_n{j}", TT, 2, P) for j in range(2)]
    sb_T = [carve(f"sb_T{j}", 2, TT * P) for j in range(2)]
    sb_e = [carve(f"sb_e{j}", 3 * P) for j in range(2)]
    sb_p = [carve(f"sb_p{j}", 3 * P) for j in range(2)]
    sb_w = [carve(f"sb_w{j}", 3 * P) for j in range(2)]
    rq = stat[:, 0:32].rearrange("p (t g h) -> p t g h", t=TT, g=2)
    T01, T1 = slice(0, 2 * P), slice(2 * P, 3 * P)
    ret_gain, bmerge = carve("ret_gain", D), carve("bmerge", 2 * D)
    load(ret_gain, I["ret_out_gain"][0].rearrange("h d -> (h d)").partition_broadcast(P), merge_in, act)
    merge_loaded = load(bmerge, I["b_merge"][0].rearrange("a d -> (a d)").partition_broadcast(P), merge_in, act)
    dve.after(qk_rstd, gate_ready, gains_ready, *mod_stored)
    act.after(*mod_stored)
    mod_rows = carve("mod_rows", P)
    load(mod_rows[0:48, :], mod_dram.rearrange("a (r p) -> (a r) p", p=P), mod_in, act)
    load(mod_rows[48:56, :], I["norm_mix_2"][0].rearrange("(r p) -> r p", p=P), mod_in, act)
    mod_loaded = load(mod_rows[56:64, :], I["norm_ffn_2"][0].rearrange("(r p) -> r p", p=P), mod_in, act)
    pe.after(first_loaded)
    with engine_loop(nc, 4, (pe, dve, act),
                     {pe: 8, dve: 14, act: 8, block_done: 4, taken[0]: 2, taken[1]: 2,
                      slot_in[0]: 16, slot_in[1]: 16}) as (i, start):
        n, pm, wm, tr = {}, {}, {}, {}
        dve.after(start[pe], start[act])
        act.after(start[pe], start[dve])

        def head(j):
            return bass.ds(i * 2 + j, 1)

        def cols(j):
            return bass.ds(i * (2 * SB_D) + j * SB_D, SB_D)

        def normed(j):
            n[j] = dve.mark(dve.eng.tensor_tensor(sb_n[j], P1[:, :, Q_:K_ + 1, cols(j)],
                                                  rq[:, :, :, head(j)].broadcast_to([P, TT, 2, SB_D]), ALU.mult))

        def turned(j):
            b = bank[4 + j]
            pe.after(n[j])
            for g in range(2):
                for t in range(TT):
                    m = pe.eng.transpose(b[:, (2 * g + t) * P:(2 * g + t + 1) * P], sb_n[j][:, t, g, :], ident)
            m = pe.mark(m)
            for g in range(2):
                tr[j] = dve.mark(dve.after(m).tensor_scalar(sb_T[j][:, g, :], b[:, g * 2 * P:(g + 1) * 2 * P],
                                                            sbgain[:, g:g + 1], None, ALU.mult))

        def scores(j):
            z, (q, k) = bank[6 + j], (sb_T[j][:, 0, :], sb_T[j][:, 1, :])
            pe.after(tr[j])
            pe.eng.matmul(z[:, T01], lhsT=k[:, 0:P], rhs=q, start=True, stop=False, skip_group_check=True)
            m = pe.mark(pe.eng.matmul(z[:, T1], lhsT=k[:, P:], rhs=q[:, P:], start=False, stop=False,
                                      skip_group_check=True))
            m = act.mark(act.after(m).activation(sb_e[j], z[:, 0:3 * P], ACT.Abs))
            m = act.mark(act.after(m).activation(sb_e[j], sb_e[j], ACT.Exp, scale=-1.0))
            m = act.mark(act.after(m).activation(sb_e[j], sb_e[j], ACT.Ln, bias=col[:, 0:1]))
            m = dve.mark(dve.after(m).scalar_tensor_tensor(sb_p[j], z[:, 0:3 * P], 0.0, sb_e[j], ALU.max, ALU.add))
            diag = sb_p[j].rearrange("p (b n) -> p b n", b=3)[:, 0:3:2, :]
            pm[j] = dve.mark(dve.after(m).tensor_tensor(diag, diag, lt.unsqueeze(1).broadcast_to([P, 2, P]), ALU.mult))

        def kept(j):
            z = bank[6 + j]
            pe.after(pm[j])
            pe.eng.matmul(z[:, T01], lhsT=negtri, rhs=sb_p[j][:, T01], start=False, stop=False, skip_group_check=True)
            pe.eng.matmul(z[:, P:2 * P], lhsT=negones, rhs=sb_p[j][:, T1], start=False, stop=False, skip_group_check=True)
            m = pe.mark(pe.eng.matmul(z[:, T1], lhsT=negtri, rhs=sb_p[j][:, T1], start=False, stop=True,
                                      skip_group_check=True))
            m = dve.mark(dve.after(m).scalar_tensor_tensor(sb_w[j], z[:, 0:3 * P], 0.0, ltbias, ALU.min, ALU.add))
            wm[j] = act.mark(act.after(m).activation(sb_w[j], sb_w[j], ACT.Exp))

        def weighed(j):
            o, w = bank[4 + j], sb_w[j]
            v = [P1[:, t, V_, cols(j)] for t in range(TT)]
            pe.after(wm[j])
            pe.eng.matmul(o[:, 0:P], lhsT=w[:, 0:P], rhs=v[0], start=True, stop=True)
            pe.eng.matmul(o[:, P:2 * P], lhsT=w[:, P:2 * P], rhs=v[0], start=True, stop=False)
            m = pe.mark(pe.eng.matmul(o[:, P:2 * P], lhsT=w[:, T1], rhs=v[1], start=False, stop=True))
            g = P1[:, :, G_, cols(j)]
            dve.mark(dve.after(m).tensor_tensor(g, o[:, 0:2 * P].rearrange("p (t d) -> p t d", t=TT), g, ALU.mult))

        def before(b):
            for j in range(2):
                [normed, turned, scores, kept][b](j)

        for c in range(2):
            project(hT, KT, CW, lambda part, t, sums, done: take_copy(
                P1c[:, t, bass.ds(i * (2 * CW) + RQ * D + c * CW, CW)], t, sums, done),
                before=lambda b: before(2 * c + b))
        for j in range(2):
            weighed(j)

    fence()
    act.after(*[c.now() for c in taken])
    dve.after(*[c.now() for c in taken])
    m = act.mark(act.eng.activation(P1[:, :, RG, :], P1[:, :, RG, :], ACT.Silu))
    gate_ready = dve.mark(dve.after(m, merge_loaded).tensor_tensor(
        P1[:, :, RG, :], P1[:, :, RG, :], ret_gain.unsqueeze(1).broadcast_to([P, TT, D]), ALU.mult))

    ret_t = [carve(f"ret_t{j}", TT, 2, P) for j in range(2)]
    ret_n = [carve(f"ret_n{j}", TT, 2, 2, P) for j in range(2)]
    ret_T = [carve(f"ret_T{j}", 2, 2, TT * P) for j in range(2)]
    ret_w = [carve(f"ret_w{j}", 3 * P) for j in range(2)]
    with engine_loop(nc, 2, (pe, dve, act),
                     {pe: 8, dve: 16, act: 4, block_done: 4, taken[0]: 2, taken[1]: 2,
                      slot_in[0]: 16, slot_in[1]: 16}) as (i, start):
        n, tr, wm = {}, {}, {}
        dve.after(start[pe], start[act])
        act.after(start[pe], start[dve])

        def rotated(j):
            def half(h):
                return P1[:, :, RQ:RK + 1, bass.ds(i * (2 * RET_D) + (j * RET_D + h * P), P)]
            c, s = (v.unsqueeze(2).broadcast_to([P, TT, 2, P]) for v in (cos1, sin1))
            for h, (x, y, op) in enumerate(((c, s, ALU.subtract), (s, c, ALU.add))):
                dve.mark(dve.eng.tensor_tensor(ret_t[0], half(0), x, ALU.mult))
                m = dve.mark(dve.eng.tensor_tensor(ret_t[1], half(1), y, ALU.mult))
                n[j] = dve.mark(dve.after(m).tensor_tensor(ret_n[j][:, :, :, h, :], ret_t[0], ret_t[1], op))
                dve.after(n[j])

        def turned(j):
            for g in range(2):
                b = bank[4 + 2 * j + g]
                pe.after(n[j])
                for h in range(2):
                    for t in range(TT):
                        m = pe.eng.transpose(b[:, (2 * h + t) * P:(2 * h + t + 1) * P], ret_n[j][:, t, g, h, :], ident)
                m = pe.mark(m)
                dst, src = ret_T[j][:, g, :, :], b.rearrange("p (h n) -> p h n", h=2)
                tr[j, g] = dve.mark(dve.after(m).tensor_copy(dst, src)) if g == 0 else act.mark(act.after(m).copy(dst, src))

        def scores(j):
            z, q, k = bank[4 + 2 * j], ret_T[j][:, 0], ret_T[j][:, 1]
            pe.after(tr[j, 0], tr[j, 1])
            for h in range(2):
                pe.eng.matmul(z[:, T01], lhsT=k[:, h, 0:P], rhs=q[:, h, :], start=(h == 0), stop=False,
                              skip_group_check=True)
                m = pe.eng.matmul(z[:, T1], lhsT=k[:, h, P:], rhs=q[:, h, P:], start=False, stop=(h == 1),
                                  skip_group_check=True)
            m = pe.mark(m)
            wm[j] = dve.mark(dve.after(m, first_loaded).tensor_tensor(
                ret_w[j], z[:, 0:3 * P], decay[:, bass.ds(i * 2 + j, 1), :].rearrange("p a n -> p (a n)"), ALU.mult))

        def weighed(j):
            o, w = bank[5 + 2 * j], ret_w[j]
            v = [P1[:, t, RV, bass.ds(i * (2 * RET_D) + j * RET_D, RET_D)] for t in range(TT)]
            pe.after(wm[j])
            pe.eng.matmul(o[:, 0:RET_D], lhsT=w[:, 0:P], rhs=v[0], start=True, stop=True)
            pe.eng.matmul(o[:, RET_D:], lhsT=w[:, P:2 * P], rhs=v[0], start=True, stop=False)
            m = pe.mark(pe.eng.matmul(o[:, RET_D:], lhsT=w[:, T1], rhs=v[1], start=False, stop=True))
            act.mark(act.after(m).copy(P1[:, :, RQ, bass.ds(i * (2 * RET_D) + j * RET_D, RET_D)],
                                       o.rearrange("p (t d) -> p t d", t=TT)))

        def before(b):
            for j in range(2):
                [rotated, turned, scores, weighed][b](j)

        for c in range(2):
            project(hT, KT, CW, lambda part, t, sums, done: take_copy(
                P1c[:, t, bass.ds(i * (2 * CW) + M1 * D + c * CW, CW)], t, sums, done),
                before=lambda b: before(2 * c + b))

    fence()
    act.after(*[c.now() for c in taken])
    dve.after(*[c.now() for c in taken])
    cursor[0] = work_top
    oaT, obT = carve("oaT", KT, S), carve("obT", KT, S)

    def tiles_of(x):
        return [x[:, t, k * P:(k + 1) * P] for t in range(TT) for k in range(x.shape[2] // P)]

    def to_features(dst, x, *ready):
        n = x.shape[2] // P
        return transposes(lambda g, c: dst[:, g % n:g % n + c, (g // n) * P:(g // n + 1) * P], tiles_of(x), ready,
                          size=min(n, 4))

    oa_ready = to_features(oaT, P1[:, :, G_, :])
    b = side_bank(mod_loaded)
    m = pe.mark(pe.eng.transpose(bank[b][:, 0:64], mod_rows[0:64, :], ident[0:64, 0:64]))
    m = dve.mark(dve.after(m).tensor_copy(modT.rearrange("p a k -> p (a k)"), bank[b][:, 0:64]))
    bank_read[b] = [m]
    for k, g in ((1, 6), (4, 7)):
        gains = dve.mark(dve.after(m).scalar_tensor_tensor(modT[:, g, :], modT[:, k, :], 1.0, modT[:, g, :], ALU.add, ALU.mult))
    merge = P1[:, :, M1:M2 + 1, :]
    bm = bmerge.rearrange("p (g d) -> p g d", g=2)
    for t in range(TT):
        m = dve.mark(dve.after(merge_loaded).tensor_tensor(merge[:, t], merge[:, t], bm, ALU.add))
        merge_ready = act.mark(act.after(m).activation(merge[:, t], merge[:, t], ACT.Sigmoid))
    ret_o, ret_sq = P1[:, :, RQ, :], P1[:, :, RK, :]
    m = act.mark(act.eng.activation(ret_sq, ret_o, ACT.Square))
    rs = stat[:, 32:40].rearrange("p (t h) -> p t h", t=TT)
    for t in range(TT):
        m = dve.mark(dve.after(m).tensor_reduce(rs[:, t], ret_sq[:, t].rearrange("p (h d) -> p h d", h=RET_H), AX, ALU.add))
    m = rstd(stat[:, 32:40], stat[:, 32:40], RET_D, 1, m)
    for t in range(TT):
        o = ret_o[:, t].rearrange("p (h d) -> p h d", h=RET_H)
        m = dve.mark(dve.after(m).tensor_tensor(o, o, rs[:, t].unsqueeze(2).broadcast_to([P, RET_H, RET_D]), ALU.mult))
    m = dve.mark(dve.after(m, gate_ready).tensor_tensor(ret_o, ret_o, P1[:, :, RG, :], ALU.mult))
    ret_ready = m

    last = {}

    def take_gated(gate, merged, aside, add, ready):
        def take(c, t, sums, done):
            at = slice(c * CW, (c + 1) * CW)
            to = aside if add else merged
            if t == 0:
                m = taken[0].mark(dve.after(done, ready).tensor_tensor(to[:, t, at], sums, gate(t, at), ALU.mult))
            else:
                m = taken[1].mark(act.after(done).copy(aside[:, t, at], sums))
                m = dve.mark(dve.after(m, ready).tensor_tensor(to[:, t, at], aside[:, t, at], gate(t, at), ALU.mult))
            if add:
                m = dve.mark(dve.after(m).tensor_tensor(merged[:, t, at], merged[:, t, at], aside[:, t, at], ALU.add))
            last["merged"] = m
        return take

    def take_residual(aside, gate=None):
        def take(c, t, sums, done):
            at = slice(c * CW, (c + 1) * CW)
            x, s = X[:, t, at], aside[:, t, at]
            if t == 1:
                done = taken[1].mark(act.after(done).copy(s, sums))
                sums = s
            if gate is None:
                m = dve.after(done).tensor_tensor(x, x, sums, ALU.add)
            else:
                m = dve.after(done).tensor_tensor(s, sums, gate[:, at], ALU.mult)
            m = taken[0].mark(m) if t == 0 else dve.mark(m)
            if gate is not None:
                m = dve.mark(dve.after(m).tensor_tensor(x, x, s, ALU.add))
        return take

    merged, aside = P1[:, :, Q_, :], P1[:, :, K_, :]
    pe.after(*oa_ready)
    for c in range(2):
        take = take_gated(lambda t, at: P1[:, t, M1, at], merged, aside, False, merge_ready)
        project(oaT, KT, CW, lambda part, t, sums, done: take(c, t, sums, done))
    act.after(last["merged"])
    ob_ready = to_features(obT, ret_o, ret_ready)
    pe.after(*ob_ready)
    for c in range(2):
        take = take_gated(lambda t, at: P1[:, t, M2, at], merged, aside, True, merge_ready)
        project(obT, KT, CW, lambda part, t, sums, done: take(c, t, sums, done))
    m_ready = to_features(hT, merged, last["merged"])
    pe.after(*m_ready)
    for c in range(2):
        take = take_residual(aside)
        project(hT, KT, CW, lambda part, t, sums, done: take(c, t, sums, done))

    fence()
    for q in everyone + (sp,):
        q.after(*[c.now() for c in taken])
    cursor[0] = persistent_top
    P2 = carve("P2", TT, w_in2.shape[1])
    upto, below, shift, carry = (carve(n, P) for n in ("upto", "below", "shift", "carry"))
    ends = carve("ends", 2)
    strict, incl, id64, a0 = (carve(n, RN) for n in ("strict", "incl", "id64", "a0"))
    levels = carve("levels", 6 * RN)
    causal, invf = carve("causal", 3 * P), carve("invf", ROPE // 2)
    pos = carve("pos", TT, dt=I32)
    qa_gain, kva_gain, q_gain, k_gain = carve("qa_gain", Q_LORA), carve("kva_gain", KV_LORA), carve("q_gain", QH), carve("k_gain", QH)
    mla_weights = cursor[0]
    w_uq, w_ukv = carve("w_uq", 2, MLA_H * QH), carve("w_ukv", 1, MLA_H * (NOPE + VH))
    lora = carve("lora", RD)
    w_gate = carve("w_gate", RD)
    base_rows = carve("base_rows", 2, RD)
    ones_row = carve("ones_row", P)
    vec = {n: carve(n, RD) for n in ("k_k_2", "k_a_2", "r_k_2", "ln_x_w_2", "ln_x_b_2")}
    mu_at = cursor[0]
    mu = carve("mu", 3 * RD + 256)
    block2_top = cursor[0]

    ones_row_ready = pool.mark(pool.eng.memset(ones_row[0:1, :], 1.0))

    h_ready = features(P2[:, :, 0:D], modT[:, 6, :], modT[:, 0, :], gains)

    for name, ap in (("upto", upto), ("below", below), ("shift", shift), ("carry", carry), ("ends", ends),
                     ("strict", strict), ("incl", incl), ("id64", id64), ("a0", a0), ("levels", levels),
                     ("causal", causal), ("invf", invf)):
        load(ap, table(name), second_in, act)

    def spread(name):
        v = I[name][0]
        return (v if len(v.shape) == 1 else v.rearrange("h d -> (h d)")).partition_broadcast(P)

    load(pos, I["positions_2"].rearrange("a (t p) -> p (a t)", p=P), second_in, act)
    for name, ap in (("q_a_norm_2", qa_gain), ("kv_a_norm_2", kva_gain), ("q_norm_2", q_gain), ("k_norm_2", k_gain)):
        load(ap, spread(name), second_in, act)
    load(w_uq, I["w_uq_2"][0].rearrange("(k p) n -> p k n", p=P), second_in, act)
    load(w_ukv, I["w_ukv_2"][0].rearrange("(k p) n -> p k n", p=P), second_in, act)
    load(lora[0:64, :], I["w_decay_up_2"][0], second_in, act)
    load(lora[64:128, :], I["w_aaa_up_2"][0], second_in, act)
    load(w_gate, I["w_gate_up_2"][0], second_in, act)
    load(base_rows[0:1, 0, :], I["decay_base_2"], second_in, act)
    load(base_rows[0:1, 1, :], I["aaa_base_2"], second_in, act)
    second_loaded = load(gt, mod_dram[0, 2 * D:3 * D].partition_broadcast(P), second_in, act)
    for name, ap in list(vec.items()) + [("mu_shift_2", mu)]:
        third_loaded = load(ap, spread(name), third_in, act)
    pe.after(*h_ready)
    for q in (dve, act):
        q.after(*h_ready)
    def take_into(at, n):
        return lambda part, t, sums, done: take_copy(P2[:, t, at:at + n], t, sums, done)

    project(hT, KT, MLA_IN, take_into(0, MLA_IN))

    all_in = [c.now() for c in taken]
    dve.after(*all_in, second_loaded)
    act.after(*all_in)
    lat = carve("lat", TT, Q_LORA + KV_LORA)
    latT = carve("latT", 3, S)
    kpe = carve("kpe", TT, 1, ROPE)
    tmp = carve("tmp", TT, MLA_H * P)
    Qm, KVm = carve("Qm", TT, MLA_H * QH), carve("KVm", TT, MLA_H * P)
    qh, kh = carve("qh", TT, MLA_H, QH), carve("kh", TT, MLA_H, QH)
    cs2 = carve("cs2", 4, TT * ROPE // 2)
    ropet = [carve(f"ropet{j}", TT, MLA_H, ROPE // 2) for j in range(2)]
    for t in range(TT):
        for j, (c0, n) in enumerate(((0, Q_LORA), (Q_LORA, KV_LORA), (Q_LORA + KV_LORA, ROPE))):
            m = act.mark(act.eng.activation(tmp[:, t, 0:n], P2[:, t, c0:c0 + n], ACT.Square,
                                            accum_out=stat[:, 48 + 2 * j + t:49 + 2 * j + t]))
            act.after(m)
    for j, n in enumerate((Q_LORA, KV_LORA, ROPE)):
        r = rstd(stat[:, 48 + 2 * j:50 + 2 * j], stat[:, 48 + 2 * j:50 + 2 * j], n, 1, m)
    for t in range(TT):
        for j, (c0, n, g) in enumerate(((0, Q_LORA, qa_gain), (Q_LORA, KV_LORA, kva_gain))):
            m = dve.mark(dve.after(r).scalar_tensor_tensor(lat[:, t, c0:c0 + n], P2[:, t, c0:c0 + n],
                                                           stat[:, 48 + 2 * j + t:49 + 2 * j + t], g, ALU.mult, ALU.mult))
        dve.mark(dve.eng.scalar_tensor_tensor(
            kpe[:, t, 0, :], P2[:, t, Q_LORA + KV_LORA:MLA_IN], stat[:, 52 + t:53 + t], k_gain[:, NOPE:], ALU.mult, ALU.mult))
    lat_done = m

    two_pi, pi = 2 * np.pi, float(np.nextafter(np.float32(np.pi), np.float32(0)))
    c1 = 6.28125
    c2 = float(np.round((two_pi - c1) * 2.0 ** 21) / 2.0 ** 21)
    c3 = two_pi - c1 - c2
    magic = 1.5 * 2.0 ** 23
    angle, turns, cosv, sinv = (cs2[:, k, :] for k in range(4))
    posf = stat[:, 60:62]
    m = dve.mark(dve.eng.tensor_copy(posf, pos))
    m = dve.mark(dve.after(m).tensor_tensor(angle.rearrange("p (t n) -> p t n", t=TT), posf.unsqueeze(2).broadcast_to([P, TT, ROPE // 2]),
                                            invf.unsqueeze(1).broadcast_to([P, TT, ROPE // 2]), ALU.mult))
    m = dve.mark(dve.after(m).tensor_scalar(turns, angle, 1 / two_pi, magic, ALU.mult, ALU.add))
    m = dve.mark(dve.after(m).tensor_scalar(turns, turns, -magic, None, ALU.add))
    for c in (c1, c2, c3):
        m = dve.mark(dve.after(m).scalar_tensor_tensor(angle, turns, -c, angle, ALU.mult, ALU.add))
    m = dve.mark(dve.after(m).tensor_scalar(angle, angle, pi, -pi, ALU.min, ALU.max))
    m = dve.mark(dve.after(m).tensor_scalar(cosv, angle, np.pi / 2, None, ALU.add))
    m = dve.mark(dve.after(m).tensor_scalar(turns, cosv, np.pi, -two_pi, ALU.is_gt, ALU.mult))
    m = dve.mark(dve.after(m).tensor_tensor(cosv, cosv, turns, ALU.add))
    m = dve.mark(dve.after(m).tensor_scalar(cosv, cosv, pi, -pi, ALU.min, ALU.max))
    m = act.mark(act.after(m).activation(cs2[:, 2, :], cosv, ACT.Sin))
    angles_ready = act.mark(act.eng.activation(sinv, angle, ACT.Sin))
    m = dve.mark(dve.eng.tensor_scalar(q_gain, q_gain, QH ** -0.5, None, ALU.mult))
    cos2, sin2 = (cs2[:, k, :].rearrange("p (t a n) -> p t a n", t=TT, a=1) for k in (2, 3))

    project(hT, KT, CW, take_into(MLA_IN, CW))
    lat_ready = to_features(latT, lat, lat_done)
    project(hT, KT, CW, take_into(MLA_IN + CW, CW))
    pe.after(*lat_ready)
    for half in range(2):
        n = MLA_H * QH // 2
        for t in range(TT):
            sums, done = token_block(latT, w_uq[:, :, half * n:(half + 1) * n], t, second_loaded)
            take_copy(Qm[:, t, half * n:(half + 1) * n], t, sums, done)
    for half in range(2):
        for t in range(TT):
            sums, done = token_block(latT[:, 2:3, :], w_ukv[:, :, half * CW:(half + 1) * CW], t, second_loaded)
            take_copy(KVm[:, t, half * CW:(half + 1) * CW], t, sums, done)
    for q in (dve, act):
        q.after(*[c.now() for c in taken])
    behind = [(take_into(at, n), ahead(hT, KT, n)) for at, n in ((MLA_IN + 2 * CW, CW), (MLA_IN + 3 * CW, 256))]
    Qv = Qm.rearrange("p t (h d) -> p t h d", h=MLA_H)
    KVv = KVm.rearrange("p t (h d) -> p t h d", h=MLA_H)
    sqQ = tmp[:, :, 0:MLA_H * QH].rearrange("p t (h d) -> p t h d", h=MLA_H)
    m = act.mark(act.after(m).activation(sqQ, Qv, ACT.Square))
    st = [stat[:, 64 + 16 * k:80 + 16 * k] for k in range(3)]
    sv = [x.rearrange("p (t h) -> p t h", t=TT) for x in st]
    dve.after(m)
    dve.mark(dve.eng.tensor_reduce(sv[0], sqQ[:, :, :, 0:NOPE], AX, ALU.add))
    m = dve.mark(dve.eng.tensor_reduce(sv[1], sqQ[:, :, :, NOPE:], AX, ALU.add))
    sqK = tmp.rearrange("p t (h d) -> p t h d", h=MLA_H)
    m = act.mark(act.after(m).activation(sqK, KVv, ACT.Square))
    m = dve.mark(dve.after(m).tensor_reduce(sv[2], sqK[:, :, :, 0:NOPE], AX, ALU.add))
    for k, n in enumerate((NOPE, ROPE, NOPE)):
        r = rstd(st[k], st[k], n, 1, m)

    def over(v, n):
        return v.unsqueeze(3).broadcast_to([P, TT, MLA_H, n])

    def gain(v, n):
        return v.unsqueeze(1).broadcast_to([P, MLA_H, n])

    dve.after(r)
    for dst, src, f, g, n, at_ in ((qh, Qv, 0, q_gain[:, 0:NOPE], NOPE, 0), (qh, Qv, 1, q_gain[:, NOPE:], ROPE, NOPE),
                              (kh, KVv, 2, k_gain[:, 0:NOPE], NOPE, 0)):
        d = dst[:, :, :, at_:at_ + n]
        m = dve.mark(dve.eng.tensor_tensor(d, src[:, :, :, at_:at_ + n], over(sv[f], n), ALU.mult))
        for t in range(TT):
            m = dve.mark(dve.after(m).tensor_tensor(d[:, t], d[:, t], gain(g, n), ALU.mult))
    dve.after(m, angles_ready)

    def rope(dst, x, heads):
        R = ROPE // 2
        c, s = (v.broadcast_to([P, TT, heads, R]) if heads == 1 else v for v in (cos2, sin2))
        a, b = (v[:, :, 0:heads, :] for v in ropet)
        lo, hi = x[:, :, :, 0:R], x[:, :, :, R:]
        def mul(d, u, v):
            for t in range(TT):
                m = dve.mark(dve.eng.tensor_tensor(d[:, t], u[:, t], v[:, t].broadcast_to([P, heads, R]), ALU.mult))
            return m
        mul(a, lo, cos2)
        m = mul(b, hi, sin2)
        m1 = dve.mark(dve.after(m).tensor_tensor(a, a, b, ALU.subtract))
        dve.after(m1)
        m = mul(b, hi, cos2)
        x2 = rope_c[:, :, 0:heads, :]
        m = mul(x2, lo, sin2)
        m = dve.mark(dve.after(m).tensor_tensor(b, b, x2, ALU.add))
        dve.after(m)
        dve.mark(dve.eng.tensor_copy(dst[:, :, :, 0:R], a))
        m = dve.mark(dve.eng.tensor_copy(dst[:, :, :, R:], b))
        dve.after(m)
        return m

    rope_c = carve("rope_c", TT, MLA_H, ROPE // 2)
    rope(qh[:, :, :, NOPE:], qh[:, :, :, NOPE:], MLA_H)
    rope(kpe, kpe, 1)
    for t in range(TT):
        heads_ready = dve.mark(dve.eng.tensor_copy(kh[:, t, :, NOPE:], kpe[:, t].broadcast_to([P, MLA_H, ROPE])))

    for take, blocks in behind:
        take_later(take, blocks)

    mla_i = [carve(f"mla_i{j}", TT, 2, QH) for j in range(4)]
    mla_T = [carve(f"mla_T{j}", 4, P) for j in range(4)]
    mla_s = [carve(f"mla_s{j}", 3 * P) for j in range(4)]
    mla_w = [carve(f"mla_w{j}", 3 * P) for j in range(4)]
    om = tmp[:, :, 0:MLA_H * VH]
    st4 = stat[:, 112:144].rearrange("p (j n) -> p j n", j=4)
    pe.after(heads_ready)
    dve.after(heads_ready)
    with engine_loop(nc, 2, (pe, dve, act),
                     {pe: 16, dve: 40, act: 12, block_done: 4, taken[0]: 2, taken[1]: 2,
                      slot_in[0]: 16, slot_in[1]: 16}) as (i, start):
        ready, tr, sm, wm = {}, {}, {}, {}
        dve.after(start[pe], start[act])
        act.after(start[pe], start[dve])

        def staged(j):
            for t in range(TT):
                for g, x in enumerate((qh, kh)):
                    ready[j] = dve.mark(dve.eng.tensor_copy(mla_i[j][:, t, g, :],
                                                            x[:, t, bass.ds(i * 4 + j, 1), :].rearrange("p a d -> p (a d)")))

        def turned(j):
            b = bank[4 + j]
            pe.after(ready[j])
            for g in range(2):
                for t in range(TT):
                    m = pe.eng.transpose(b[0:QH, (2 * g + t) * P:(2 * g + t + 1) * P], mla_i[j][:, t, g, :], ident)
            m = pe.mark(m)
            dst, src = mla_T[j][0:QH].rearrange("p a n -> p (a n)"), b[0:QH, :]
            tr[j] = dve.mark(dve.after(m).tensor_copy(dst, src)) if j % 2 else act.mark(act.after(m).copy(dst, src))

        def scores(j):
            z, T = bank[4 + j], mla_T[j][0:QH].rearrange("p a n -> p (a n)")
            pe.after(tr[j])
            pe.eng.matmul(z[:, 0:P], lhsT=T[:, 0:P], rhs=T[:, 2 * P:3 * P], start=True, stop=True)
            m = pe.mark(pe.eng.matmul(z[:, P:3 * P], lhsT=T[:, P:2 * P], rhs=T[:, 2 * P:], start=True, stop=True))
            m = dve.mark(dve.after(m).tensor_tensor(mla_s[j], z[:, 0:3 * P], causal, ALU.add))
            for t, at_ in enumerate((slice(0, P), slice(P, 3 * P))):
                m = dve.mark(dve.after(m).tensor_reduce(st4[:, j, t:t + 1], mla_s[j][:, at_], AX, ALU.max, negate=True))
            for t, at_ in enumerate((slice(0, P), slice(P, 3 * P))):
                m = act.mark(act.after(m).activation(mla_w[j][:, at_], mla_s[j][:, at_], ACT.Exp, bias=st4[:, j, t:t + 1],
                                                     accum_out=st4[:, j, 2 + t:3 + t]))
            sm[j] = m
            dve.mark(dve.after(m).reciprocal(st4[:, j, 4:6], st4[:, j, 2:4]))

        def by_keys(j):
            b = bank[4 + j]
            pe.after(sm[j])
            for k in range(3):
                m = pe.eng.transpose(b[:, k * P:(k + 1) * P], mla_w[j][:, k * P:(k + 1) * P], ident)
            m = pe.mark(m)
            dst, src = mla_s[j], b[:, 0:3 * P]
            wm[j] = act.mark(act.after(m).copy(dst, src)) if j % 2 else dve.mark(dve.after(m).tensor_copy(dst, src))

        def weighed(j):
            o, w = bank[4 + j], mla_s[j]
            v = [KVm[:, t, bass.ds(i * (4 * P) + (j * P + NOPE), VH)] for t in range(TT)]
            pe.after(wm[j])
            pe.eng.matmul(o[:, 0:VH], lhsT=w[:, 0:P], rhs=v[0], start=True, stop=True)
            pe.eng.matmul(o[:, VH:2 * VH], lhsT=w[:, P:2 * P], rhs=v[0], start=True, stop=False)
            m = pe.mark(pe.eng.matmul(o[:, VH:2 * VH], lhsT=w[:, 2 * P:], rhs=v[1], start=False, stop=True))
            dve.after(m)
            dve.mark(dve.eng.tensor_tensor(
                om[:, :, bass.ds(i * (4 * VH) + j * VH, VH)], o[:, 0:2 * VH].rearrange("p (t d) -> p t d", t=TT),
                st4[:, j, 4:6].unsqueeze(2).broadcast_to([P, TT, VH]), ALU.mult))

        def before(b):
            for j in range(4):
                [staged, turned, scores, by_keys][b](j)

        for c in range(2):
            project(hT, KT, CW, lambda part, t, sums, done: take_copy(
                P2[:, t, bass.ds(i * (2 * CW) + (GATES + c * CW), CW)], t, sums, done),
                before=lambda b: before(2 * c + b))
        for j in range(4):
            weighed(j)
    fence()
    for q in everyone:
        q.after(*[c.now() for c in taken])

    omT = hT.rearrange("p k n -> p (k n)")[:, 0:4 * S].rearrange("p (k n) -> p k n", k=4)
    om_ready = to_features(omT, om)
    fence()
    cursor[0] = block2_top
    RW = carve("RW", TT, 3 * RD + 256)
    beta, kappa = carve("beta", TT, RD), carve("kappa", TT, RD)
    arT = carve("arT", 4, 2, S)
    betaT, kappaT = carve("betaT", 4, S), carve("kappaT", 4, S)
    ldT = carve("ldT", 2, S)
    WT = carve("WT", 4, S)
    Gend = carve("Gend", 4, 4)
    temps = cursor[0]
    sg, a_, kk, kx = (carve(n, TT, RD) for n in ("sg", "a", "kk", "kx"))
    cursor[0] = mla_weights
    alpha, u0 = carve("alpha", TT, RD), carve("u0", TT, RD)
    cursor[0] = mu_at
    states = carve("states", 4, 4, RN)
    U = hT.rearrange("p k n -> p (k n)")[:, TT * RD:].rearrange("p (t n) -> p t n", t=TT)
    r_, k_, v_ = (RW[:, :, j * RD:(j + 1) * RD] for j in range(3))
    y = P2[:, :, MLA_IN:MLA_IN + RD]
    g_ = P2[:, :, MLA_IN + RD:MLA_IN + 2 * RD]
    NM = P2[:, :, MLA_IN + 2 * RD:MLA_IN + 3 * RD]
    rho = NM
    pe.after(second_loaded, ones_row_ready)
    dve.after(third_loaded)
    pool.after(third_loaded)
    for j, n in ((3, 256), (0, CW), (1, CW), (2, CW)):
        for t in range(TT):
            b = side_bank()
            at_ = slice(MLA_IN + j * CW, MLA_IN + j * CW + n)
            m = pe.eng.matmul(bank[b][:, 0:n], lhsT=shift, rhs=P2[:, t, at_], start=True, stop=(t == 0))
            if t == 1:
                m = pe.eng.matmul(bank[b][:, 0:n], lhsT=carry, rhs=P2[:, 0, at_], start=False, stop=True)
            m = pe.mark(m)
            d = RW[:, t, j * CW:j * CW + n]
            m = dve.mark(dve.after(m).tensor_tensor(d, bank[b][:, 0:n], mu[:, j * CW:j * CW + n], ALU.mult))
            bank_read[b] = [m]
            shifted = pool.mark(pool.after(m).tensor_tensor(d, d, P2[:, t, at_], ALU.add))
        if j == 3:
            m = act.mark(act.after(shifted).activation(RW[:, :, 3 * RD:3 * RD + 64], RW[:, :, 3 * RD:3 * RD + 64], ACT.Tanh))
            low_in = act.mark(act.eng.activation(RW[:, :, 3 * RD + 128:], RW[:, :, 3 * RD + 128:], ACT.Sigmoid))
    m = to_features(ldT, RW[:, :, 3 * RD:], low_in)
    pe.after(*m)
    act.after(shifted)
    for t in range(TT):
        tok = slice(t * P, (t + 1) * P)
        for which, dst in ((0, sg), (1, a_)):
            rows = slice(64 * which, 64 * which + 64)
            b = side_bank()
            pe.eng.matmul(bank[b], lhsT=ldT[rows, 0, tok], rhs=lora[rows, :], start=True, stop=False)
            m = pe.mark(pe.eng.matmul(bank[b], lhsT=ones_row[0:1, :], rhs=base_rows[0:1, which, :], start=False, stop=True))
            low_ready = act.mark(act.after(m).activation(dst[:, t, :], bank[b], ACT.Sigmoid))
            bank_read[b] = [low_ready]
        b = side_bank()
        m = pe.mark(pe.eng.matmul(bank[b], lhsT=ldT[:, 1, tok], rhs=w_gate, start=True, stop=True))
        bank_read[b] = [act.mark(act.after(m).copy(g_[:, t, :], bank[b]))]

    def both(v):
        return v.unsqueeze(1).broadcast_to([P, TT, RD])

    def by_head(x):
        return x.rearrange("p t (h d) -> p t h d", h=RH)

    def tt(q, out_, x, z, op, *after):
        return q.mark(q.after(*after).tensor_tensor(out_, x, z, op))

    m = tt(dve, kk, k_, both(vec["k_k_2"]), ALU.mult, shifted)
    m = act.mark(act.after(m).activation(alpha, kk, ACT.Square))
    ks = stat[:, 64:80]
    m = dve.mark(dve.after(m).tensor_reduce(ks.rearrange("p (t h) -> p t h", t=TT), by_head(alpha), AX, ALU.add))
    m = act.mark(act.after(m).activation(ks, ks, ACT.Sqrt))
    m = dve.mark(dve.after(m).tensor_scalar(ks, ks, 1e-12, None, ALU.max))
    m = dve.mark(dve.after(m).reciprocal(ks, ks))
    ksv = ks.rearrange("p (t h) -> p t h", t=TT)
    kk_ready = tt(dve, by_head(kk), by_head(kk), ksv.unsqueeze(3).broadcast_to([P, TT, RH, RN]), ALU.mult, m)
    m = dve.mark(dve.after(low_ready).scalar_tensor_tensor(kx, a_, -1.0, both(vec["k_a_2"]), ALU.add, ALU.mult))
    kx_ready = dve.mark(dve.after(m).scalar_tensor_tensor(kx, kx, 1.0, k_, ALU.add, ALU.mult))
    m = tt(pool, y, r_, kx, ALU.mult, kx_ready)
    m = tt(pool, y, y, both(vec["r_k_2"]), ALU.mult, m)
    bonus = stat[:, 80:96]
    bonus_ready = dve.mark(dve.after(m).tensor_reduce(bonus.rearrange("p (t h) -> p t h", t=TT), by_head(y), AX, ALU.add))

    for t in range(TT):
        b = side_bank(low_ready)
        m = pe.mark(pe.eng.matmul(bank[b], lhsT=upto, rhs=sg[:, t, :], start=True, stop=True))
        act.mark(act.after(m).activation(rho[:, t, :], bank[b], ACT.Exp))
        e1 = act.mark(act.eng.activation(beta[:, t, :], bank[b], ACT.Exp, scale=-1.0))
        bank_read[b] = [e1]
        b = side_bank()
        m = pe.mark(pe.eng.matmul(bank[b], lhsT=below, rhs=sg[:, t, :], start=True, stop=True))
        e2 = act.mark(act.after(m, kk_ready).activation(alpha[:, t, :], bank[b], ACT.Exp))
        bank_read[b] = [e2]
    b = side_bank()
    for p in range(4):
        for t in range(TT):
            m = pe.eng.matmul(bank[b][:, 4 * p + 2 * t:4 * p + 2 * t + 2], lhsT=sg[:, t, p * P:(p + 1) * P], rhs=ends,
                              start=True, stop=True)
    m = pe.mark(m)
    gend_ready = act.mark(act.after(m).activation(Gend.rearrange("p a c -> p (a c)"), bank[b][:, 0:16], ACT.Exp))
    bank_read[b] = [gend_ready]
    a_ready = tt(dve, alpha, alpha, kk, ALU.mult, e2, kk_ready)
    r_ready = tt(dve, rho, rho, r_, ALU.mult)
    k_ready = tt(pool, kappa, kx, beta, ALU.mult, e1, kx_ready)
    m = tt(dve, a_, a_, kk, ALU.mult)
    b_ready = tt(dve, beta, beta, a_, ALU.mult, m, k_ready)
    to_features(arT[:, :, 0, :], alpha, a_ready)
    to_features(arT[:, :, 1, :], rho, r_ready)
    to_features(kappaT, kappa, k_ready)
    to_features(betaT, beta, b_ready)
    fence()

    cursor[0] = temps
    AT, BT, D1, D2, XI, YI, T1_ = (carve(n, TT, RH, RN) for n in ("AT", "BT", "D1", "D2", "XI", "YI", "T1_"))
    HALF = [slice(0, 64), slice(64, 128)]
    odds = [range(q, RH, 2) for q in range(2)]

    def mask(v, n=RH):
        return v.unsqueeze(1).broadcast_to([P, n, RN])

    def chunk(t, cp):
        return slice((2 * t + cp) * RN, (2 * t + cp + 1) * RN)

    for t in range(TT):
        g = P2[:, t, GATES:]
        gates2_ready = act.mark(act.eng.activation(g, g, ACT.Sigmoid))
    for t in range(TT):
        for src, lt_, le_ in ((betaT, AT, D1), (kappaT, BT, D2)):
            for q in range(2):
                b = side_bank()
                for h in odds[q]:
                    for cp in range(2):
                        o = bank[b][HALF[cp], h // 2 * P:h // 2 * P + P].rearrange("p (a n) -> p a n", a=2)
                        m = pe.eng.matmul(o, lhsT=src[HALF[q], h // 2, chunk(t, cp)],
                                          rhs=arT[HALF[q], h // 2, :, chunk(t, cp)], start=True, stop=True)
                m = pe.mark(m)
                o = bank[b].rearrange("p (h a n) -> p h a n", h=4, a=2)
                dve.mark(dve.after(m).tensor_tensor(lt_[:, t, q:RH:2, :], o[:, :, 0, :], mask(strict, 4), ALU.mult))
                m = dve.mark(dve.eng.tensor_tensor(le_[:, t, q:RH:2, :], o[:, :, 1, :], mask(incl, 4), ALU.mult))
                bank_read[b] = [m]
        for q in range(2):
            b = side_bank()
            for h in odds[q]:
                for cp in range(2):
                    m = pe.eng.matmul(bank[b][HALF[cp], h // 2 * RN:(h // 2 + 1) * RN],
                                      lhsT=arT[HALF[q], h // 2, 0, chunk(t, cp)],
                                      rhs=betaT[HALF[q], h // 2, chunk(t, cp)], start=True, stop=True)
            m = pe.mark(m)
            m = dve.mark(dve.after(m).tensor_tensor(XI[:, t, q:RH:2, :], bank[b][:, 0:4 * RN].rearrange("p (h n) -> p h n", h=4),
                                                    mask(a0, 4), ALU.mult))
            bank_read[b] = [m]
        dve.mark(dve.after(m).tensor_tensor(XI[:, t], XI[:, t], mask(id64), ALU.add))
        m = dve.mark(dve.eng.tensor_tensor(YI[:, t], AT[:, t], mask(levels[:, 0:RN]), ALU.mult))
        m = dve.mark(dve.after(m).tensor_tensor(YI[:, t], YI[:, t], mask(id64), ALU.add))

    NMv = NM.rearrange("p t (h n) -> p t h n", h=RH)
    with engine_loop(nc, 5, (pe, dve, act), {pe: 4, dve: 6, act: 2}) as (i, start):
        dve.after(start[pe], start[dve])
        lev = levels[:, bass.ds(i * RN + RN, RN)]
        nm = [dve.mark(dve.eng.tensor_tensor(NMv[:, t], AT[:, t], mask(lev), ALU.mult)) for t in range(TT)]
        pe.after(start[dve], start[act])
        act.after(start[pe])

        def carry_wait(t):
            pe.eng.matmul(bank[6 + t][:, 0:P], lhsT=ident, rhs=ident, start=True, stop=True)

        t1 = []
        for t in range(TT):
            pe.after(nm[t])
            carry_wait(t)
            for h in range(RH):
                for rows in HALF:
                    m = pe.eng.matmul(bank[4 + t][rows, h * RN:(h + 1) * RN], lhsT=NMv[rows, t, h, :],
                                      rhs=XI[rows, t, h, :], start=True, stop=True)
            m = pe.mark(m)
            t1.append(act.mark(act.after(m).copy(T1_[:, t].rearrange("p h n -> p (h n)"), bank[4 + t])))
        for t in range(TT):
            pe.after(t1[t])
            carry_wait(t)
            for h in range(RH):
                for rows in HALF:
                    at_ = slice(h * RN, (h + 1) * RN)
                    pe.eng.matmul(bank[t][rows, at_], lhsT=YI[rows, t, h, :], rhs=T1_[rows, t, h, :], start=True, stop=True)
                    m = pe.eng.matmul(bank[2 + t][rows, at_], lhsT=T1_[rows, t, h, :], rhs=YI[rows, t, h, :], start=True, stop=True)
            m = pe.mark(m)
            for dst, b in ((XI, t), (YI, 2 + t)):
                d = dst[:, t].rearrange("p h n -> p (h n)")
                dve.mark(dve.after(m).tensor_tensor(d, d, bank[b], ALU.add))
    fence()

    side[0] = 0
    vh = v_.rearrange("p t (h n) -> p t h n", h=RH)
    for t in range(TT):
        b = side_bank()
        for h in range(RH):
            for rows in HALF:
                m = pe.eng.matmul(bank[b][rows, h * RN:(h + 1) * RN], lhsT=BT[rows, t, h, :], rhs=vh[rows, t, h, :],
                                  start=True, stop=True)
        m = pe.mark(m)
        bv_ready = act.mark(act.after(m).copy(T1_[:, t].rearrange("p h n -> p (h n)"), bank[b]))
        bank_read[b] = [bv_ready]
        for cp in range(2):
            b = side_bank()
            for h in range(RH):
                m = pe.eng.matmul(bank[b][HALF[h % 2], h // 2 * RN:(h // 2 + 1) * RN],
                                  lhsT=alpha[HALF[cp], t, h * RN:(h + 1) * RN], rhs=YI[HALF[cp], t, h, :],
                                  start=True, stop=True)
            m = pe.mark(m)
            w_ready = dve.mark(dve.after(m).tensor_copy(WT[:, :, chunk(t, cp)],
                                                        bank[b][:, 0:4 * RN].rearrange("p (a n) -> p a n", a=4)))
            bank_read[b] = [w_ready]
        b = side_bank(bv_ready)
        for h in range(RH):
            for rows in HALF:
                m = pe.eng.matmul(bank[b][rows, h * RN:(h + 1) * RN], lhsT=YI[rows, t, h, :], rhs=T1_[rows, t, h, :],
                                  start=True, stop=True)
        m = pe.mark(m)
        u_ready = act.mark(act.after(m).mul(u0[:, t, :], bank[b], -1.0))
        bank_read[b] = [u_ready]

    dve.after(u_ready)
    pe.after(w_ready)
    st_ready = dve.mark(dve.eng.memset(states[:, 0], 0.0))
    for c in range(4):
        t, rows = c // 2, HALF[c % 2]
        for q in range(2):
            b = side_bank(st_ready)
            for h in odds[q]:
                m = pe.eng.matmul(bank[b][rows, h // 2 * RN:(h // 2 + 1) * RN], lhsT=WT[HALF[q], h // 2, chunk(t, c % 2)],
                                  rhs=states[HALF[q], c, h // 2, :], start=True, stop=True)
            m = pe.mark(m)
            uq, u0q = (x[rows, t, :].rearrange("p (h n) -> p h n", h=RH)[:, q:RH:2, :] for x in (U, u0))
            m = dve.mark(dve.after(m).tensor_tensor(uq, u0q, bank[b][rows, 0:4 * RN].rearrange("p (h n) -> p h n", h=4),
                                                    ALU.subtract))
            bank_read[b] = [m]
        us_ready = m
        if c == 3:
            break
        b = side_bank(us_ready)
        for h in range(RH):
            o = bank[b][HALF[h % 2], h // 2 * RN:(h // 2 + 1) * RN]
            at_ = slice(h * RN, (h + 1) * RN)
            pe.eng.matmul(o, lhsT=kappa[rows, t, at_], rhs=v_[rows, t, at_], start=True, stop=False)
            m = pe.eng.matmul(o, lhsT=beta[rows, t, at_], rhs=U[rows, t, at_], start=False, stop=True)
        m = pe.mark(m)
        by_pair = bank[b][:, 0:4 * RN].rearrange("p (a n) -> p a n", a=4)
        m = dve.mark(dve.after(m).tensor_tensor(states[:, c + 1], by_pair, states[:, c], ALU.add))
        bank_read[b] = [m]
        st_ready = dve.mark(dve.after(m).tensor_tensor(states[:, c + 1], states[:, c + 1],
                                                       Gend[:, :, c:c + 1].broadcast_to([P, 4, RN]), ALU.mult))

    yh = by_head(y)
    y_marks = []
    for t in range(TT):
        b = side_bank(us_ready, st_ready)
        for h in range(RH):
            for rows in HALF:
                at_ = slice(h * RN, (h + 1) * RN)
                pe.eng.matmul(bank[b][rows, at_], lhsT=D1[rows, t, h, :], rhs=U[rows, t, at_], start=True, stop=False)
                m = pe.eng.matmul(bank[b][rows, at_], lhsT=D2[rows, t, h, :], rhs=v_[rows, t, at_], start=False, stop=True)
        m = pe.mark(m)
        y_ready = act.mark(act.after(m, bonus_ready).copy(y[:, t, :], bank[b]))
        bank_read[b] = [y_ready]
        for q in range(2):
            b = side_bank()
            for h in odds[q]:
                for cp in range(2):
                    m = pe.eng.matmul(bank[b][HALF[cp], h // 2 * RN:(h // 2 + 1) * RN],
                                      lhsT=arT[HALF[q], h // 2, 1, chunk(t, cp)],
                                      rhs=states[HALF[q], 2 * t + cp, h // 2, :], start=True, stop=True)
            m = pe.mark(m)
            yq = yh[:, t, q:RH:2, :]
            m = dve.mark(dve.after(m, y_ready).tensor_tensor(yq, yq, bank[b][:, 0:4 * RN].rearrange("p (h n) -> p h n", h=4),
                                                             ALU.add))
            bank_read[b] = [m]
            y_marks.append(m)

    ys = stat[:, 96:112]
    ysv = ys.rearrange("p (t h) -> p t h", t=TT)
    cursor[0] = temps
    fence()
    ysq, yT, aside = carve("ysq", TT, RD), carve("yT", 4, S), carve("aside2", TT, D)
    pe.after(*om_ready)
    mla_blocks = ahead(omT, 4, CW, parts=2)

    def each(v):
        return v.unsqueeze(3).broadcast_to([P, TT, RH, RN])

    m = dve.mark(dve.after(*y_marks).tensor_reduce(ysv, yh, AX, ALU.add))
    m = dve.mark(dve.after(m).tensor_scalar(ys, ys, -1.0 / RN, None, ALU.mult))
    yc = tt(dve, yh, yh, each(ysv), ALU.add, m)
    m = act.mark(act.after(yc).activation(ysq, y, ACT.Square))
    m = dve.mark(dve.after(m).tensor_reduce(ysv, by_head(ysq), AX, ALU.add))
    m = rstd(ys, ys, RN, 2, m)
    m = tt(dve, yh, yh, each(ysv), ALU.mult, m)
    m = tt(dve, y, y, both(vec["ln_x_w_2"]), ALU.mult, m)
    m = tt(dve, y, y, both(vec["ln_x_b_2"]), ALU.add, m)
    m2 = tt(pool, by_head(v_), by_head(v_), each(bonus.rearrange("p (t h) -> p t h", t=TT)), ALU.mult, bonus_ready)
    m = tt(dve, y, y, v_, ALU.add, m, m2)
    m = tt(dve, y, y, g_, ALU.mult, m)

    y_ready = to_features(yT, y, m)
    merged = P2[:, :, GATES:GATES + D]
    gates2 = [lambda t, at, g=g: P2[:, t, GATES + g * D + at.start:GATES + g * D + at.stop] for g in range(2)]
    take_later(take_gated(gates2[0], merged, aside, False, gates2_ready), mla_blocks)
    act.after(last["merged"])
    pe.after(*y_ready)
    project(yT, 4, CW, take_gated(gates2[1], merged, aside, True, gates2_ready), parts=2)
    pe.after(*to_features(hT, merged, last["merged"]))
    dve.after(second_loaded)
    for c in range(2):
        take = take_residual(aside, gt)
        project(hT, KT, CW, lambda part, t, sums, done: take(c, t, sums, done))

    fence()
    for q in everyone:
        q.after(*[c.now() for c in taken])
    cursor[0] = persistent_top
    down_tile = [slot[0][:, j * D:(j + 1) * D] for j in range(4)]
    up_tile = [slot[1][:, j * D:(j + 1) * D] for j in range(4)]
    x_saved = load(I["x_dram"].rearrange("(t p) d -> p t d", p=P), X, x_out, act)
    cursor[0] = lasting_top
    hot = [carve(f"hot{j}", 2, 4, P) for j in range(4)]
    cursor[0] = lasting_top
    dT_low = [carve(f"dT_low{j}", KT, P) for j in range(2)]
    dT_high = [carve(f"dT_high{j}", KT, P) for j in range(2)]
    raw = [carve(f"raw{j}", KT, P) for j in range(2)]
    cursor[0] -= 2 * 4 * D
    up_hi = [carve(f"up_high{j}", D) for j in range(2)]
    hT_high = carve("hT_high", KT, S)
    gl = [carve(f"gl{j}", S) for j in range(2)]
    sel_at = cursor[0]
    A_high, A_low = ([carve(f"{n}{j}", S) for j in range(2)] for n in ("A_high", "A_low"))
    cursor[0] = sel_at
    selT = carve("selT", 3, S)
    iota = carve("iota_keys", P)
    coeff_at = max(cursor[0], sel_at + 4 * 4 * S)
    cursor[0] = hT_at
    hT_low = carve("hT_low", KT, S)
    cursor[0] = slot_at + 4 * KT * CW
    up_low = [carve(f"up_low{j}", D) for j in range(4)]
    cursor[0] = coeff_at
    C = carve("C", N_KEYS, S)
    assert coeff_at >= persistent_top
    EARLY = 32
    cursor[0] = coeff_at + 4 * EARLY * S
    keys, keysT = carve("keys", 2, P), carve("keysT", 2, P)
    load(keys[:, 0, :], I["sub_keys1_2"][0], peer_in, act)
    load(keys[:, 1, :], I["sub_keys2_2"][0], peer_in, act)
    peer_loaded = load(iota, table("iota"), peer_in, act)
    qT, sc = carve("qT", 2 * PEER_H, S), carve("sc", TT * PEER_H, 2, N_KEYS)
    tmp = carve("peer_tmp", TT, D)
    keys_ready = transposes(lambda g, n: keysT, [keys[:, 0, :], keys[:, 1, :]], [peer_loaded], size=2)
    h_ready = features(tmp, modT[:, 7, :], modT[:, 3, :])

    pe.after(*h_ready, *keys_ready)
    scv = sc.rearrange("p (t h) a n -> p t h a n", t=TT)
    for c in range(4):
        j, arrived = next_chunk()
        w = slot_view(j, KT, CW)
        q_ready = []
        for t in range(2):
            sums = open_block(t, arrived).rearrange("p (a n) -> p a n", a=2)
            for a in range(2):
                for k in range(KT):
                    mm = pe.eng.matmul(sums[:, a, :], lhsT=w[:, k, (2 * t + a) * P:(2 * t + a + 1) * P], rhs=hT[:, k, :],
                                       start=(k == 0), stop=(k == KT - 1))
            q_ready.append(take_copy(qT[:, 4 * c + 2 * t:4 * c + 2 * t + 2, :], t, sums, block_done.mark(mm)))
        for t in range(TT):
            b = side_bank(*q_ready)
            o = bank[b].rearrange("p (h a n) -> p h a n", h=2, a=2)
            for h in range(2):
                for a in range(2):
                    m = pe.eng.matmul(o[:, h, a, :], lhsT=qT[:, 4 * c + 2 * h + a, t * P:(t + 1) * P],
                                      rhs=keysT[:, a, :], start=True, stop=True)
            m = pe.mark(m)
            sc_ready = act.mark(act.after(m).copy(scv[:, t, 2 * c:2 * c + 2], o))
            bank_read[b] = [sc_ready]

    def load_down(a, i=0):
        down_in[a % 4].mark(sp.eng.dma_start(down_tile[a % 4], I["expert_down_2"][0][bass.ds(i * (4 * P) + a * P, P), :]))

    def load_up(a, i=0):
        up_in[a % 4].mark(sp.eng.dma_start(up_tile[a % 4], I["expert_up_2"][0][bass.ds(i * (4 * P) + a * P, P), :]))

    def down_room(a, i=None):
        sp.after(Mark(turned_done.sem, 2 * (a - 3), i, 8))

    def up_room(a, i=None):
        sp.after(Mark(tile_done.sem, a - 3, i, 4))

    def next_loads(a, i=None):
        up_room(a, i)
        load_up(a, 0 if i is None else i)
        if a + 2 < N_KEYS:
            down_room(a + 2, i)
            load_down(a + 2, 0 if i is None else i)

    sp.after(block_done.now())
    for a in range(4):
        load_down(a)
        load_up(a)
    with engine_loop(nc, EARLY // 4, (sp,), {c: 16 for c in down_in}) as (i, _):
        for a in range(4, 8):
            down_room(a, i)
            load_down(a, i)
    with engine_loop(nc, EARLY // 4 - 1, (sp,), {c: 16 for c in up_in}) as (i, _):
        for a in range(4, 8):
            up_room(a, i)
            load_up(a, i)
    for a in range(EARLY, EARLY + 2):
        up_room(a)
        load_up(a)
    TURNS = (N_KEYS - EARLY - 4) // 4
    with engine_loop(nc, TURNS, (sp,), {c: 16 for c in down_in + up_in}) as (i, _):
        for a in range(EARLY + 2, EARLY + 6):
            next_loads(a, i)
    for a in range(4 * TURNS + EARLY + 2, N_KEYS):
        next_loads(a)

    def of(count, a, i, n=1):
        return Mark(count.sem, n * (a + 1), i, 4 * n) if i is not None else Mark(count.sem, n * (a + 1))

    def high(q, dst, src):
        dst = dst.bitcast(F32R)
        return q.eng.copy(dst, src) if q is act else q.eng.tensor_copy(dst, src)

    def low(q, dst, src, high_part):
        return q.eng.tensor_tensor(dst.bitcast(F32R), src, high_part, ALU.subtract)

    def three(o, lhs, lhs_high, rhs, rhs_high, start, stop):
        pe.eng.matmul(o, lhsT=lhs_high.bitcast(F32R), rhs=rhs_high.bitcast(F32R), start=start, stop=False,
                      skip_group_check=True)
        pe.eng.matmul(o, lhsT=lhs_high.bitcast(F32R), rhs=rhs.bitcast(F32R), start=False, stop=False,
                      skip_group_check=True)
        return pe.eng.matmul(o, lhsT=lhs.bitcast(F32R), rhs=rhs_high.bitcast(F32R), start=False, stop=stop,
                             skip_group_check=True)

    def turn(a, i, early=False):
        pe.after(Mark(down_in[a % 4].sem, 16 * (a // 4 + 1), i, 16))
        if a > 1:
            act.after(of(down_done, a - 2, i))
            if early:
                act.after(of(down_low, a - 2, i, 2))
        for g in range(2):
            if a > 0:
                pe.after(Mark((down_high if early else down_low).sem, 2 * a - 1 + g, i, 8))
            for k in range(4):
                m = pe.eng.transpose(bank[4 + g][:, k * P:(k + 1) * P],
                                     down_tile[a % 4][:, (4 * g + k) * P:(4 * g + k + 1) * P], ident)
            turned_done.mark(m)
            ks, src = slice(4 * g, 4 * g + 4), bank[4 + g].rearrange("p (k n) -> p k n", k=4)
            act.after(Mark(turned_done.sem, 2 * a + g + 1, i, 8))
            high_part, low_part = dT_high[a % 2][:, ks, :], dT_low[a % 2][:, ks, :]
            m = high(act, high_part, src)
            q = dve
            if early:
                q, copy = pool, raw[a % 2][:, ks, :]
                m = act.eng.copy(copy, src)
                src = copy
            down_high.mark(m)
            q.after(Mark(down_high.sem, 2 * a + g + 1, i, 8))
            down_low.mark(low(q, low_part, src, high_part))

    def down(a, i, early=False):
        b = bank[6 + a % 2][:, 0:S]
        pe.after(of(down_low, a, i, 2))
        if a > 1:
            pe.after(of(gelu_done, a - 2, i))
        for k in range(KT):
            m = three(b, dT_low[a % 2][:, k, :], dT_high[a % 2][:, k, :], hT_low[:, k, :], hT_high[:, k, :],
                      k == 0, k == KT - 1)
        down_done.mark(m)
        act.after(of(down_done, a, i))
        if early:
            dst, src = C[:, bass.ds(a if i is None else i * 4 + a, 1), :], b.unsqueeze(1)
        else:
            act.after(of(weighed_done, a - 2, i))
            dst, src = gl[a % 2], b
        gelu_done.mark(act.eng.activation(dst, src, ACT.Gelu_apprx_tanh))

    fence()
    act.after(x_saved)
    pool.after(x_saved)
    m = dve.mark(high(dve, hT_high, hT))
    dve.after(m)
    pe.after(dve.mark(low(dve, hT_low, hT, hT_high)))
    def early_steps(a, i=None):
        if a + 1 < EARLY:
            turn(a + 1, i, True)
        down(a, i, True)

    turn(0, None, True)
    for a in range(3):
        early_steps(a)
    chain = {turned_done: 8, down_high: 8, down_low: 8, down_done: 4, gelu_done: 4}
    EARLY_TURNS = (EARLY - 4) // 4
    with engine_loop(nc, EARLY_TURNS, (pe, act, pool), chain) as (i, _):
        for a in range(3, 7):
            early_steps(a, i)
    early_steps(EARLY - 1)
    for b in (4, 5):
        bank_read[b] = [down_high.now()]
    for b in (6, 7):
        bank_read[b] = [gelu_done.now()]

    TH = TT * PEER_H
    HALVES, PAIRS = 4, 2
    s_now, s_rest = carve("s_now", HALVES, N_KEYS), carve("s_rest", HALVES, N_KEYS)
    best, which = carve("best", HALVES, TOPK), carve("which", HALVES, TOPK, dt=U32)
    cand, cand_rest = carve("cand", PAIRS, TOPK, TOPK), carve("cand_rest", PAIRS, TOPK * TOPK)
    best_sum, which_sum = carve("best_sum", PAIRS, TOPK), carve("which_sum", PAIRS, TOPK, dt=U32)
    top_v, top_at = carve("top_v", TH, TOPK), carve("top_at", TH, TOPK, dt=U32)
    top_key = carve("top_key", TH, 2, TOPK, dt=U32)
    dve.after(sc_ready)
    with engine_loop(nc, TH // PAIRS, (dve,), {dve: 12}) as (i, start):
        def then(m):
            dve.after(dve.mark(m)).memset(stat[:, 190:191], 0.0)

        def sixteen(rows, values, v, at, rest):
            for r in rows:
                m = dve.eng.max(v[:, r, 0:8], values[:, r])
            then(m)
            for r in rows:
                dve.eng.max_index(at[:, r, 0:8], v[:, r, 0:8], values[:, r])
                m = dve.eng.match_replace(rest[:, r], v[:, r, 0:8], values[:, r], -3e38)
            then(m)
            for r in rows:
                m = dve.eng.max(v[:, r, 8:16], rest[:, r])
            then(m)
            for r in rows:
                m = dve.eng.max_index(at[:, r, 8:16], v[:, r, 8:16], rest[:, r])
            then(m)

        pairs = bass.ds(i * PAIRS, PAIRS)
        dve.after(start[dve])
        then(dve.eng.tensor_copy(s_now, sc[:, pairs, :, :].rearrange("p o a n -> p (o a) n")))
        sixteen(range(HALVES), s_now, best, which, s_rest)
        b4 = best.rearrange("p (o a) k -> p o a k", a=2)
        then(dve.eng.tensor_tensor(cand, b4[:, :, 0, :].unsqueeze(3).broadcast_to([P, PAIRS, TOPK, TOPK]),
                                   b4[:, :, 1, :].unsqueeze(2).broadcast_to([P, PAIRS, TOPK, TOPK]), ALU.add))
        sixteen(range(PAIRS), cand.rearrange("p o a b -> p o (a b)"), best_sum, which_sum, cand_rest)
        dve.eng.tensor_copy(top_v[:, pairs, :], best_sum)
        dve.eng.tensor_copy(top_key[:, pairs, :, :].rearrange("p o a k -> p (o a) k"), which)
        dve.mark(dve.eng.tensor_copy(top_at[:, pairs, :], which_sum))
        dve.mark(dve.after(dve.now()).memset(stat[:, 190:191], 0.0))

    dve.after(dve.now())
    gates = carve("gates", TH, TOPK)
    norm = carve("norm", TH)
    rank_u, rank = carve("rank_u", 2, TH, TOPK, dt=U32), carve("rank", 2, TH, TOPK)
    key_of = carve("key_of", 2, TH, TOPK)
    sel_key = carve("sel_key", 2, TH, TOPK)
    eq = [carve(f"eq{j}", TH, TOPK, TOPK) for j in range(2)]
    m = dve.mark(dve.eng.tensor_tensor(gates, top_v, top_v[:, :, 0:1].broadcast_to([P, TH, TOPK]), ALU.subtract))
    exp_ready = act.mark(act.after(m).activation(gates, gates, ACT.Exp))
    dve.mark(dve.eng.tensor_scalar(rank_u[:, 0], top_at, 4, None, ALU.logical_shift_right))
    m = dve.mark(dve.eng.tensor_scalar(rank_u[:, 1], top_at, 15, None, ALU.bitwise_and))
    dve.after(m)
    rank_ready = dve.mark(dve.eng.tensor_copy(rank, rank_u))
    for a in range(2):
        key_ready = dve.mark(dve.eng.tensor_copy(key_of[:, a], top_key[:, :, a, :]))
    ranks = iota[:, 0:TOPK].unsqueeze(1).unsqueeze(1).broadcast_to([P, TH, TOPK, TOPK])
    sel_ready = []
    for a in range(2):
        dve.after(rank_ready, key_ready)
        m = dve.mark(dve.eng.tensor_tensor(eq[a], ranks, rank[:, a].unsqueeze(3).broadcast_to([P, TH, TOPK, TOPK]), ALU.is_equal))
        m = dve.mark(dve.after(m).tensor_tensor(eq[a], eq[a], key_of[:, a].unsqueeze(2).broadcast_to([P, TH, TOPK, TOPK]), ALU.mult))
        sel_ready.append(dve.mark(dve.after(m).tensor_reduce(sel_key[:, a], eq[a], AX, ALU.add)))
    m = dve.mark(dve.after(exp_ready).tensor_reduce(norm, gates, AX, ALU.add))
    m = dve.mark(dve.after(m).reciprocal(norm, norm))
    gates_ready = dve.mark(dve.after(m).tensor_tensor(gates, gates, norm.unsqueeze(2).broadcast_to([P, TH, TOPK]), ALU.mult))
    sources = [x.rearrange("p (t h) k -> p t (h k)", t=TT) for x in (sel_key[:, 0], sel_key[:, 1], gates)]
    for v in range(3):
        transposes(lambda g, n: selT[:, v, :].rearrange("p (t n) -> p t n", t=TT),
                                [sources[v][:, t, :] for t in range(TT)], [gates_ready] + sel_ready, size=2)
    fence()

    iota8 = iota.unsqueeze(1).unsqueeze(1).broadcast_to([P, 2, 4, P])
    made = [bank[4 + u].rearrange("p (n a) -> p n a", n=4) for u in range(4)]

    def apply(u, turn, copied):
        to = C[:, 0:EARLY, bass.ds(turn * 16 + 4 * u, 4)].rearrange("p a n -> p n a")
        return dve.mark(dve.after(copied).tensor_tensor(to, to, made[u][:, :, 0:EARLY], ALU.mult))

    def sixteen_tokens(turn, last):
        for u in range(4):
            toks = bass.ds(turn * 16 + 4 * u, 4)
            if last:
                dve.after(last[u][0])
            m = dve.mark(dve.eng.tensor_tensor(
                hot[u], iota8, selT[:, 0:2, toks].unsqueeze(3).broadcast_to([P, 2, 4, P]), ALU.is_equal))
            m = pool.mark(pool.after(m).tensor_tensor(
                hot[u][:, 0], hot[u][:, 0], selT[:, 2, toks].unsqueeze(2).broadcast_to([P, 4, P]), ALU.mult))
            if last:
                pe.after(apply(u, turn - 1, last[u][1]))
            pe.after(m)
            for n in range(4):
                m = pe.eng.matmul(made[u][:, n, :], lhsT=hot[u][:, 1, n, :], rhs=hot[u][:, 0, n, :],
                                  start=True, stop=True)
            m = pe.mark(m)
            act.mark(act.after(m).copy(C[:, EARLY:, toks].rearrange("p a n -> p n a"), made[u][:, :, EARLY:]))

    sixteen_tokens(0, None)
    with engine_loop(nc, S // 16 - 1, (pe, dve, pool, act), {pe: 4, dve: 8, pool: 4, act: 4}) as (i, start):
        sixteen_tokens(i + 1, [(Mark(pe.sem, start[pe].base - 3 + u, i, 4), Mark(act.sem, start[act].base - 3 + u, i, 4))
                               for u in range(4)])
    for u in range(4):
        apply(u, S // 16 - 1, Mark(act.sem, act.count - 3 + u))
    fence()

    def split_up(a, i):
        dve.after(Mark(up_in[a % 4].sem, 16 * (a // 4 + 1), i, 16))
        if a > 1:
            dve.after(of(tile_done, a - 2, i))
        up_high.mark(high(dve, up_hi[a % 2], up_tile[a % 4]))
        dve.after(of(up_high, a, i))
        pool.after(of(up_high, a, i))
        for q, c, at in ((dve, up_split_dve, slice(0, CW)), (pool, up_split, slice(CW, D))):
            c.mark(low(q, up_low[a % 4][:, at], up_tile[a % 4][:, at], up_hi[a % 2][:, at]))

    def weigh(a, i, early=False):
        A, c = gl[a % 2].unsqueeze(1), C[:, bass.ds(a if i is None else i * 4 + a, 1), :]
        if a > 1:
            dve.after(of(tile_done, a - 2, i))
        if early:
            A = c
        else:
            dve.after(of(gelu_done, a, i))
            dve.after(dve.mark(dve.eng.tensor_tensor(A, A, c, ALU.mult)))
        dve.after(dve.mark(high(dve, A_high[a % 2].unsqueeze(1), A)))
        weighed_done.mark(low(dve, A_low[a % 2].unsqueeze(1), A, A_high[a % 2].unsqueeze(1)))

    def up(a, i, stop=False):
        pe.after(of(weighed_done, a, i), of(up_split, a, i), of(up_split_dve, a, i))
        for t in range(TT):
            for half in range(2):
                at = slice(half * CW, (half + 1) * CW)
                m = three(bank[2 * t + half], A_low[a % 2][:, t * P:(t + 1) * P], A_high[a % 2][:, t * P:(t + 1) * P],
                          up_low[a % 4][:, at], up_hi[a % 2][:, at], a == 0, stop)
        tile_done.mark(m)

    def tile_steps(a, i=None):
        if EARLY <= a + 2 < N_KEYS:
            turn(a + 2, i)
        if a + 1 < N_KEYS:
            split_up(a + 1, i)
            if a + 1 >= EARLY:
                down(a + 1, i)
            weigh(a + 1, i, a + 1 < EARLY)
        up(a, i, a == N_KEYS - 1)

    ups = {c: 4 for c in (up_high, up_split_dve, up_split, weighed_done, tile_done)}
    split_up(0, None)
    weigh(0, None, True)
    for a in range(4):
        tile_steps(a)
    with engine_loop(nc, EARLY // 4 - 2, (pe, dve, pool), {dve: 4, **ups}) as (i, _):
        for a in range(4, 8):
            tile_steps(a, i)
    for a in range(EARLY - 4, EARLY):
        tile_steps(a)
    with engine_loop(nc, TURNS, (pe, dve, act, pool), {dve: 8, **chain, **ups}) as (i, _):
        for a in range(EARLY, EARLY + 4):
            tile_steps(a, i)
    for a in range(4 * TURNS + EARLY, N_KEYS):
        tile_steps(a)

    cursor[0] = coeff_at
    X_back, gt_back, scaled = carve("X_back", TT, D), carve("gt_back", D), carve("scaled", TT, D)
    sp.after(x_saved, Mark(weighed_done.sem, N_KEYS // 2))
    load(X_back, I["x_dram"].rearrange("(t p) d -> p t d", p=P), x_in)
    x_back = load(gt_back, mod_dram[0, 5 * D:6 * D].partition_broadcast(P), x_in)
    dve.after(Mark(tile_done.sem, N_KEYS), x_back)
    for t in range(TT):
        for half in range(2):
            at = slice(half * CW, (half + 1) * CW)
            m = dve.mark(dve.eng.tensor_tensor(scaled[:, t, at], bank[2 * t + half], gt_back[:, at], ALU.mult))
            m = dve.mark(dve.after(m).tensor_tensor(scaled[:, t, at], scaled[:, t, at], X_back[:, t, at], ALU.add))
            sp.after(m)
            stored = out_done.mark(sp.eng.dma_start(out[0, t * P:(t + 1) * P, at], scaled[:, t, at]))
    sp.after(stored)


def kernel(**inputs):
    import concourse.bacc as bacc
    from concourse.bass_utils import run_bass_kernel_spmd

    nc = bacc.Bacc("TRN2", target_bir_lowering=False, num_devices=1)
    arrays, I = {}, {}

    def give(name, a):
        arrays[f"in_{name}_dram"] = a
        I[name] = nc.dram_tensor(f"in_{name}_dram", a.shape, mybir.dt.from_np(a.dtype), kind="ExternalInput").ap()

    for name in inputs:
        give(name, np.ascontiguousarray(inputs[name]))
    for name, tables in zip(("first", "second"), constants()):
        table, I[name + "_at"] = pack(tables)
        give(name, table)
    I["x_dram"] = nc.dram_tensor("x_dram", [S, D], F32, kind="Internal").ap()
    I["mod_dram"] = nc.dram_tensor("mod_dram", [1, 6 * D], F32, kind="Internal").ap()
    out = nc.dram_tensor("out_dram", [1, S, D], F32, kind="ExternalOutput").ap()
    build(nc, I, out)
    return run_bass_kernel_spmd(nc, [arrays], core_ids=[0]).results[0]["out_dram"]
```
